# Optimizing a Trainium2 kernel written in Bass

```python
import math
import jax, jax.numpy as jnp
from jax import lax
import numpy as np

D_MODEL = 1024
BATCH = 1
SEQ = 256
DEPTH = 2

HEAD_DIM = 64
QBLOCK = 128
A_HEADS = 8
A_KV = 2
A_WINDOW = 128
B_HEADS = 8
B_KV = 2
CMP_BLOCK = 32
CMP_STRIDE = 16
CMP_HIDDEN = 128
SEL_BLOCK = 64
SEL_TOPN = 16
B_WINDOW = 512
SEL_QCHUNK = 16
C_HEADS = 8
BRANCH_WIDTH = 512
N_BRANCH = 3
REL_BUCKETS = 32
REL_MAX_DIST = 128
D_FF = 2816
FFN_RES = 0.5
N_SUB = 3
EPS = 1e-6
IN_WIDTH = (A_HEADS + 2 * A_KV) * HEAD_DIM + (B_HEADS + 6 * B_KV) * HEAD_DIM + 3 * B_HEADS + 3 * C_HEADS * HEAD_DIM + N_BRANCH * D_MODEL

kernel_name = "hybrid_gated_swa_nsa_stickbreak_macaron"

def in_layout():
    widths = [
        ("a_q", A_HEADS * HEAD_DIM), ("a_k", A_KV * HEAD_DIM), ("a_v", A_KV * HEAD_DIM),
        ("b_q", B_HEADS * HEAD_DIM),
        ("b_k_cmp", B_KV * HEAD_DIM), ("b_v_cmp", B_KV * HEAD_DIM),
        ("b_k_slc", B_KV * HEAD_DIM), ("b_v_slc", B_KV * HEAD_DIM),
        ("b_k_win", B_KV * HEAD_DIM), ("b_v_win", B_KV * HEAD_DIM),
        ("b_gate", 3 * B_HEADS),
        ("c_q", C_HEADS * HEAD_DIM), ("c_k", C_HEADS * HEAD_DIM), ("c_v", C_HEADS * HEAD_DIM),
        ("merge_gate", N_BRANCH * D_MODEL),
    ]
    out, off = {}, 0
    for name, w in widths:
        out[name] = (off, off + w)
        off += w
    return out

def rms_norm(x, gain):
    x32 = x.astype(jnp.float32)
    y = x32 * lax.rsqrt(jnp.mean(x32 * x32, axis=-1, keepdims=True) + EPS)
    return (y * gain.astype(jnp.float32)).astype(x.dtype)

def swiglu(h, w_gate, w_up, w_down):
    return (jax.nn.silu(h @ w_gate) * (h @ w_up)) @ w_down

def t5_bucket(dist):
    max_exact = REL_BUCKETS // 2
    d = jnp.maximum(dist, 0)
    ratio = jnp.log(jnp.maximum(d, 1).astype(jnp.float32) / max_exact) / math.log(REL_MAX_DIST / max_exact)
    large = jnp.minimum(max_exact + (ratio * (REL_BUCKETS - max_exact)).astype(jnp.int32), REL_BUCKETS - 1)
    return jnp.where(d < max_exact, d, large)

def masked_softmax(logits, mask):
    logits = jnp.where(mask, logits.astype(jnp.float32), -1e30)
    m = jnp.max(logits, axis=-1, keepdims=True)
    e = jnp.where(mask, jnp.exp(logits - m), 0.0)
    s = jnp.sum(e, axis=-1, keepdims=True)
    return e / jnp.where(s > 0, s, 1.0)

def band_bias(table, window):
    dist = window + jnp.arange(QBLOCK)[:, None] - jnp.arange(window + QBLOCK)[None, :]
    return jnp.moveaxis(table[t5_bucket(dist)], -1, 0).astype(jnp.float32)

def banded_attention(q, k, v, bias, window, sink):
    bsz, g, hpg, s, dh = q.shape
    nblk = s // QBLOCK
    span = window + QBLOCK
    kp = jnp.pad(k, ((0, 0), (0, 0), (window, 0), (0, 0)))
    vp = jnp.pad(v, ((0, 0), (0, 0), (window, 0), (0, 0)))
    qb = jnp.moveaxis(q.reshape(bsz, g, hpg, nblk, QBLOCK, dh), 3, 0)
    iq = jnp.arange(QBLOCK)[:, None]
    jk = jnp.arange(span)[None, :]
    dist = window + iq - jk
    in_band = (dist >= 0) & (dist < window)
    scale = 1.0 / math.sqrt(dh)

    def block(args):
        qi, blk = args
        start = blk * QBLOCK
        kb = lax.dynamic_slice_in_dim(kp, start, span, axis=2)
        vb = lax.dynamic_slice_in_dim(vp, start, span, axis=2)
        mask = in_band & (start - window + jk >= 0)
        logits = jnp.einsum('bghqd,bgkd->bghqk', qi, kb).astype(jnp.float32) * scale + bias
        logits = jnp.where(mask, logits, -1e30)
        if sink is None:
            p = jax.nn.softmax(logits, axis=-1)
        else:
            sk = sink.astype(jnp.float32)[None, :, :, None, None]
            m = jnp.maximum(jnp.max(logits, axis=-1, keepdims=True), sk)
            e = jnp.exp(logits - m)
            p = e / (jnp.sum(e, axis=-1, keepdims=True) + jnp.exp(sk - m))
        return jnp.einsum('bghqk,bgkd->bghqd', p.astype(vb.dtype), vb)

    out = lax.map(block, (qb, jnp.arange(nblk)))
    return jnp.moveaxis(out, 0, 3).reshape(bsz, g, hpg, s, dh)

def swa_sink_attention(q, k, v, sinks, rel_table_a):
    bsz, s, _ = q.shape
    hpg = A_HEADS // A_KV
    qh = q.reshape(bsz, s, A_KV, hpg, HEAD_DIM).transpose(0, 2, 3, 1, 4)
    kh = k.reshape(bsz, s, A_KV, HEAD_DIM).transpose(0, 2, 1, 3)
    vh = v.reshape(bsz, s, A_KV, HEAD_DIM).transpose(0, 2, 1, 3)
    bias = band_bias(rel_table_a, A_WINDOW).reshape(A_KV, hpg, QBLOCK, A_WINDOW + QBLOCK)
    o = banded_attention(qh, kh, vh, bias, A_WINDOW, sinks.reshape(A_KV, hpg))
    return o.transpose(0, 3, 1, 2, 4).reshape(bsz, s, A_HEADS * HEAD_DIM)

def nsa_compress(kv, pos, w1, w2):
    bsz, s, _ = kv.shape
    ncmp = (s - CMP_BLOCK) // CMP_STRIDE + 1
    kv_r = kv.reshape(bsz, s, B_KV, HEAD_DIM)
    idx = jnp.arange(ncmp)[:, None] * CMP_STRIDE + jnp.arange(CMP_BLOCK)[None, :]
    blocks = kv_r[:, idx] + pos[None, None, :, None, :]
    flat = blocks.transpose(0, 3, 1, 2, 4).reshape(bsz, B_KV, ncmp, CMP_BLOCK * HEAD_DIM)
    return jax.nn.gelu(flat @ w1) @ w2

def nsa_selected_attention(qh, k_slc, v_slc, sel_idx, rel_table_b):
    bsz, g, hpg, s, dh = qh.shape
    nsel = s // SEL_BLOCK
    n_top = sel_idx.shape[-1]
    nk = n_top * SEL_BLOCK
    nchunk = s // SEL_QCHUNK
    kb = k_slc.reshape(bsz, nsel, SEL_BLOCK, g, dh).transpose(0, 3, 1, 2, 4)
    vb = v_slc.reshape(bsz, nsel, SEL_BLOCK, g, dh).transpose(0, 3, 1, 2, 4)
    qc = jnp.moveaxis(qh.reshape(bsz, g, hpg, nchunk, SEL_QCHUNK, dh), 3, 0)
    ic = jnp.moveaxis(sel_idx.reshape(bsz, g, nchunk, SEL_QCHUNK, n_top), 2, 0)
    tc = jnp.arange(s).reshape(nchunk, SEL_QCHUNK)
    table = rel_table_b.reshape(REL_BUCKETS, g, hpg).transpose(1, 0, 2)
    gidx = jnp.arange(g)[None, :, None, None]
    gather = jax.vmap(jax.vmap(lambda blocks, ix: blocks[ix]))
    scale = 1.0 / math.sqrt(dh)

    def chunk(args):
        qi, ii, ti = args
        kg = gather(kb, ii).reshape(bsz, g, SEL_QCHUNK, nk, dh)
        vg = gather(vb, ii).reshape(bsz, g, SEL_QCHUNK, nk, dh)
        kpos = (ii[..., None] * SEL_BLOCK + jnp.arange(SEL_BLOCK)).reshape(bsz, g, SEL_QCHUNK, nk)
        dist = ti[None, None, :, None] - kpos
        bias = jnp.moveaxis(table[gidx, t5_bucket(dist)], -1, 2)
        logits = jnp.einsum('bghqd,bgqkd->bghqk', qi, kg).astype(jnp.float32) * scale + bias
        p = masked_softmax(logits, (dist >= 0)[:, :, None])
        return jnp.einsum('bghqk,bgqkd->bghqd', p.astype(vg.dtype), vg)

    out = lax.map(chunk, (qc, ic, tc))
    return jnp.moveaxis(out, 0, 3).reshape(bsz, g, hpg, s, dh)

def nsa_attention(q, k_cmp, v_cmp, k_slc, v_slc, k_win, v_win, gate_logits, cmp_pos, cmp_w1, cmp_w2, rel_table_b):
    bsz, s, _ = q.shape
    g, hpg = B_KV, B_HEADS // B_KV
    qh = q.reshape(bsz, s, g, hpg, HEAD_DIM).transpose(0, 2, 3, 1, 4)
    t = jnp.arange(s)
    scale = 1.0 / math.sqrt(HEAD_DIM)
    kc = nsa_compress(k_cmp, cmp_pos[0], cmp_w1[0], cmp_w2[0])
    vc = nsa_compress(v_cmp, cmp_pos[1], cmp_w1[1], cmp_w2[1])
    ncmp = kc.shape[2]
    cstart = jnp.arange(ncmp) * CMP_STRIDE
    cmp_mask = (cstart + CMP_BLOCK - 1)[None, :] <= t[:, None]
    logits_c = jnp.einsum('bghsd,bgnd->bghsn', qh, kc).astype(jnp.float32) * scale
    p_cmp = masked_softmax(logits_c, cmp_mask)
    o_cmp = jnp.einsum('bghsn,bgnd->bghsd', p_cmp.astype(vc.dtype), vc)
    nsel = s // SEL_BLOCK
    sstart = jnp.arange(nsel) * SEL_BLOCK
    overlap = ((cstart[:, None] < sstart[None, :] + SEL_BLOCK) & (cstart[:, None] + CMP_BLOCK > sstart[None, :])).astype(jnp.float32)
    imp = jnp.einsum('bgsn,nj->bgsj', jnp.sum(p_cmp, axis=2), overlap)
    cur = t // SEL_BLOCK
    jsel = jnp.arange(nsel)[None, :]
    forced = (jsel == 0) | (jsel == cur[:, None]) | (jsel == cur[:, None] - 1)
    future = sstart[None, :] > t[:, None]
    prio = jnp.where(forced, jnp.inf, jnp.where(future, -jnp.inf, imp))
    _, sel_idx = lax.top_k(prio, min(SEL_TOPN, nsel))
    o_slc = nsa_selected_attention(qh, k_slc, v_slc, sel_idx, rel_table_b)
    kw = k_win.reshape(bsz, s, g, HEAD_DIM).transpose(0, 2, 1, 3)
    vw = v_win.reshape(bsz, s, g, HEAD_DIM).transpose(0, 2, 1, 3)
    bias_w = band_bias(rel_table_b, B_WINDOW).reshape(g, hpg, QBLOCK, B_WINDOW + QBLOCK)
    o_win = banded_attention(qh, kw, vw, bias_w, B_WINDOW, None)
    gates = jax.nn.sigmoid(gate_logits.astype(jnp.float32)).reshape(bsz, s, 3, g, hpg).transpose(2, 0, 3, 4, 1)[..., None]
    gates = gates.astype(q.dtype)
    o = gates[0] * o_cmp + gates[1] * o_slc + gates[2] * o_win
    return o.transpose(0, 3, 1, 2, 4).reshape(bsz, s, B_HEADS * HEAD_DIM)

def stick_breaking_attention(q, k, v):
    bsz, s, _ = q.shape
    qh = q.reshape(bsz, s, C_HEADS, HEAD_DIM).transpose(0, 2, 1, 3)
    kh = k.reshape(bsz, s, C_HEADS, HEAD_DIM).transpose(0, 2, 1, 3)
    vh = v.reshape(bsz, s, C_HEADS, HEAD_DIM).transpose(0, 2, 1, 3)
    scale = 1.0 / math.sqrt(HEAD_DIM)
    outs = []
    for blk in range(s // QBLOCK):
        s0, s1 = blk * QBLOCK, (blk + 1) * QBLOCK
        z = jnp.einsum('bhqd,bhkd->bhqk', qh[:, :, s0:s1], kh[:, :, :s1]).astype(jnp.float32) * scale
        strict = jnp.arange(s1)[None, :] < jnp.arange(s0, s1)[:, None]
        log_keep = jnp.where(strict, jax.nn.log_sigmoid(-z), 0.0)
        later = lax.cumsum(log_keep, axis=3, reverse=True) - log_keep
        w = jnp.where(strict, jnp.exp(jax.nn.log_sigmoid(z) + later), 0.0)
        outs.append(jnp.einsum('bhqk,bhkd->bhqd', w.astype(vh.dtype), vh[:, :, :s1]))
    o = jnp.concatenate(outs, axis=2)
    return o.transpose(0, 2, 1, 3).reshape(bsz, s, C_HEADS * HEAD_DIM)

def token_mixing(u, w_in, sinks, cmp_pos, cmp_w1, cmp_w2, w_branch, w_out, rel_bias):
    lay = in_layout()

    def proj(name):
        a, b = lay[name]
        return u @ w_in[:, a:b]

    y_a = swa_sink_attention(proj("a_q"), proj("a_k"), proj("a_v"), sinks, rel_bias[:, :A_HEADS])
    y_b = nsa_attention(proj("b_q"), proj("b_k_cmp"), proj("b_v_cmp"), proj("b_k_slc"), proj("b_v_slc"),
                        proj("b_k_win"), proj("b_v_win"), proj("b_gate"), cmp_pos, cmp_w1, cmp_w2,
                        rel_bias[:, A_HEADS:A_HEADS + B_HEADS])
    y_c = stick_breaking_attention(proj("c_q"), proj("c_k"), proj("c_v"))
    bsz, s, _ = u.shape
    gates = jax.nn.sigmoid(proj("merge_gate")).reshape(bsz, s, N_BRANCH, D_MODEL)
    merged = (gates[:, :, 0] * (y_a @ w_branch[0]) + gates[:, :, 1] * (y_b @ w_branch[1])
              + gates[:, :, 2] * (y_c @ w_branch[2]))
    return merged @ w_out

def sandwich(x, mod, i, ln_pre, ln_post, fn, res_w):
    shift, scale, gate = mod[:, i, 0][:, None, :], mod[:, i, 1][:, None, :], mod[:, i, 2][:, None, :]
    h = rms_norm(x, ln_pre[i]) * (1 + scale) + shift
    return x + res_w * gate * rms_norm(fn(h), ln_post[i])

def setup_inputs(seed: int = 0) -> dict:
    key = jax.random.key(seed)
    ks = jax.random.split(key, 20)
    f32 = jnp.float32

    def nrm(k, shape, scale):
        return jax.random.normal(k, shape, f32) * scale

    D = D_MODEL
    return {
        "x": nrm(ks[0], (BATCH, SEQ, D), 1.0),
        "c": nrm(ks[1], (BATCH, D), 1.0),
        "rel_bias": nrm(ks[2], (REL_BUCKETS, A_HEADS + B_HEADS), 0.5),
        "ada_w": nrm(ks[3], (DEPTH, D, N_SUB * 3 * D), 0.5 * D ** -0.5),
        "ada_b": nrm(ks[4], (DEPTH, N_SUB * 3 * D), 0.02),
        "ln_pre": 1.0 + nrm(ks[5], (DEPTH, N_SUB, D), 0.02),
        "ln_post": 1.0 + nrm(ks[6], (DEPTH, N_SUB, D), 0.02),
        "ffn_w_gate": nrm(ks[7], (DEPTH, 2, D, D_FF), D ** -0.5),
        "ffn_w_up": nrm(ks[8], (DEPTH, 2, D, D_FF), D ** -0.5),
        "ffn_w_down": nrm(ks[9], (DEPTH, 2, D_FF, D), D_FF ** -0.5),
        "w_in": nrm(ks[10], (DEPTH, D, IN_WIDTH), D ** -0.5),
        "attn_sinks": nrm(ks[11], (DEPTH, A_HEADS), 1.0),
        "cmp_pos": nrm(ks[12], (DEPTH, 2, CMP_BLOCK, HEAD_DIM), 0.1),
        "cmp_w1": nrm(ks[13], (DEPTH, 2, CMP_BLOCK * HEAD_DIM, CMP_HIDDEN), (CMP_BLOCK * HEAD_DIM) ** -0.5),
        "cmp_w2": nrm(ks[14], (DEPTH, 2, CMP_HIDDEN, HEAD_DIM), CMP_HIDDEN ** -0.5),
        "w_branch": nrm(ks[15], (DEPTH, N_BRANCH, BRANCH_WIDTH, D), BRANCH_WIDTH ** -0.5),
        "w_out": nrm(ks[16], (DEPTH, D, D), D ** -0.5),
    }

def reference(x, c, rel_bias, ada_w, ada_b, ln_pre, ln_post, ffn_w_gate, ffn_w_up, ffn_w_down,
              w_in, attn_sinks, cmp_pos, cmp_w1, cmp_w2, w_branch, w_out):
    bsz = x.shape[0]
    c_act = jax.nn.silu(c)
    for l in range(DEPTH):
        mod = (c_act @ ada_w[l] + ada_b[l]).reshape(bsz, N_SUB, 3, D_MODEL)
        x = sandwich(x, mod, 0, ln_pre[l], ln_post[l],
                     lambda h: swiglu(h, ffn_w_gate[l, 0], ffn_w_up[l, 0], ffn_w_down[l, 0]), FFN_RES)
        x = sandwich(x, mod, 1, ln_pre[l], ln_post[l],
                     lambda h: token_mixing(h, w_in[l], attn_sinks[l], cmp_pos[l], cmp_w1[l], cmp_w2[l],
                                            w_branch[l], w_out[l], rel_bias), 1.0)
        x = sandwich(x, mod, 2, ln_pre[l], ln_post[l],
                     lambda h: swiglu(h, ffn_w_gate[l, 1], ffn_w_up[l, 1], ffn_w_down[l, 1]), FFN_RES)
    return x


_drawn_inputs = setup_inputs


def setup_inputs(seed=0):
    import zlib

    import numpy as np

    out = dict(_drawn_inputs(seed))
    spreads = {}
    factors = {'ln_pre': 4.462, 'ln_post': 5.434, 'attn_sinks': 5.002, 'cmp_pos': 4.661}
    for name, (base, spread) in spreads.items():
        noise = np.random.default_rng([zlib.crc32(name.encode()), seed]).standard_normal(out[name].shape)
        drawn = base * np.exp(spread * noise) if base else spread * noise
        out[name] = __import__('jax').numpy.asarray(drawn.astype(out[name].dtype))
    for name, factor in factors.items():
        out[name] = (out[name] * factor).astype(out[name].dtype)
    return out
```

```python
from contextlib import ExitStack

import concourse.bass as bass
from concourse import mybir

F32 = mybir.dt.float32
F32R = mybir.dt.float32r
ACT = mybir.ActivationFunctionType
ALU = mybir.AluOpType
AX = mybir.AxisListType

P = 128
D = 1024
S = 256
DEPTH = 2
DH = 64
HEADS = 8
HPG = 4
FF = 2816
NSUB = 3
CMP_BLOCK = 32
CMP_STRIDE = 16
NCMP = (S - CMP_BLOCK) // CMP_STRIDE + 1
IN_WIDTH = 6680
EPS = 1e-6
NEG = -1e30
KC = D // P
TOK = S // P

RING = 3
UNIT = 2048
LOADS = 2
FB = 256
FSTEPS = FF // FB
FFN_UNITS = 3 * FSTEPS
SUMS_AHEAD = 8
ADA_STEPS = 8
QKV_UNITS = 14
MIX_UNITS = QKV_UNITS + 3 * 6 + 4
LAYER_UNITS = 2 * FFN_UNITS + MIX_UNITS
GATE_COL = 2048
MERGE_COL = 3608
MOD = 3 * D
HALF = MOD // 2

JOBS = ([("a", h) for h in range(HEADS)]
        + [(k, h) for h in range(HEADS) for k in ("slc", "win")]
        + [("c", h) for h in range(HEADS)])
NJ = len(JOBS)


def job_slots(step):
    if 3 <= step <= 6:
        return range(2 * (step - 3), 2 * (step - 3) + 2)
    if 9 <= step <= 16:
        return range(HEADS + 2 * (step - 9), HEADS + 2 * (step - 9) + 2)
    if 17 <= step <= 26:
        return range(3 * HEADS + step - 17, 3 * HEADS + step - 16)
    return range(0)


def pair_done(n):
    kind, h = JOBS[n]
    if h % 2 == 0 or kind == "slc":
        return None
    return {"a": 0, "win": 4, "c": 8}[kind] + h // 2


def trunk_program(nc, A, out):
    ctx = ExitStack()
    with ctx:
        def sb(name, shape, dt=F32):
            return ctx.enter_context(nc.sbuf_tensor(name, shape, dt))

        def sem(name):
            return ctx.enter_context(nc.semaphore(name))

        x = sb("x", [P, TOK, D])
        h_hi = sb("h_hi", [P, KC, S], F32R)
        h_lo = sb("h_lo", [P, KC, S], F32R)
        w_raw = sb("w_raw", [P, RING, UNIT])
        w_hi = sb("w_hi", [P, RING, UNIT], F32R)
        w_lo = sb("w_lo", [P, RING, UNIT], F32R)
        act_hi = sb("act_hi", [P, 2, 4, S], F32R)
        act_lo = sb("act_lo", [P, 2, 4, S], F32R)
        g_raw = sb("g_raw", [P, KC, 24])
        g_hi = sb("g_hi", [P, KC, 24], F32R)
        g_lo = sb("g_lo", [P, KC, 24], F32R)
        bias = sb("bias", [P, 2 * HEADS, 2 * P])
        ident = sb("ident", [P, P])
        neg_tri = sb("neg_tri", [P, P])
        neg_ones = sb("neg_ones", [P, P])
        ones = sb("ones", [P, 1])
        causal01 = sb("causal01", [P, 3 * P])
        causal_neg = sb("causal_neg", [P, 3 * P])
        cmp_neg = sb("cmp_neg", [P, TOK, NCMP])
        cmp_01 = sb("cmp_01", [P, TOK, NCMP])
        ln_t = sb("ln_t", [P, 2, DEPTH * NSUB * KC])
        adab_t = sb("adab_t", [P, DEPTH * NSUB * 24])
        pos_t = sb("pos_t", [DH, DEPTH, 2 * CMP_BLOCK])
        c_act = sb("c_act", [P, KC])
        sink = sb("sink", [P, DEPTH, HEADS])
        eps_t = sb("eps_t", [P, 1])
        modc = sb("modc", [P, NSUB, 24])
        mod_a = sb("mod_a", [P, NSUB, KC])
        mod_g = sb("mod_g", [P, NSUB, KC])
        gt = sb("gt", [KC, NSUB, P])
        stat = sb("stat", [P, 16])
        w2k = sb("w2k", [P, 2, DH])
        w2v = sb("w2v", [P, DH])
        hid = sb("hid", [P, 2, 2, NCMP])
        hid_v = sb("hid_v", [P, 2, 4, 32])
        kc_t = sb("kc_t", [P, 2, NCMP])
        vc = sb("vc", [P, 2, DH])
        egate = sb("egate", [P, TOK, 24])
        bgate = egate
        cmp_p = sb("cmp_p", [P, 2 * TOK * 4, 32])
        cmp_pt = sb("cmp_pt", [P, 2, TOK, P])
        cst = sb("cst", [P, 3, 16])
        jst = sb("jst", [P, 2, 12])

        AR = 15872
        arena = sb("arena", [P, AR])

        def region(at, *shape, parts=P):
            n = 1
            for d_ in shape:
                n *= d_
            v = arena[0:parts, at:at + n]
            if len(shape) == 2:
                return v.rearrange("p (a b) -> p a b", b=shape[1])
            if len(shape) == 3:
                return v.rearrange("p (a b c) -> p a b c", b=shape[1], c=shape[2])
            return v

        ada_acc = region(0, 2 * MOD)
        ada_raw = region(2 * MOD, 4, HALF)
        ffn_a = region(12288, TOK, FB)
        ffn_s = region(12800, TOK, FB)
        SCR = AR - 2048
        xs = region(SCR, TOK, D)
        gate_sb = region(12288, 2, 512)
        w1 = region(0, 2, 16, P)
        mg = region(0, TOK, 512)
        hbuf = region(0, KC, S)
        o_ = 4096
        aq = region(o_, 4, S); o_ += 1024
        ak = region(o_, 2, S); o_ += 512
        bq = region(o_, 4, S); o_ += 1024
        bks = region(o_, 2, S); o_ += 512
        bkw = region(o_, 2, S); o_ += 512
        cq = region(o_, 4, S); o_ += 1024
        ck = region(o_, 4, S); o_ += 1024
        av = region(o_, TOK, P); o_ += 256
        bvs = region(o_, TOK, P); o_ += 256
        bvw = region(o_, TOK, P); o_ += 256
        cv = region(o_, TOK, 512); o_ += 1024
        job_s = region(o_, 2, 3 * P); o_ += 768
        job_p = region(o_, 2, 3 * P); o_ += 768
        job_t = region(o_, 2, 3 * P); o_ += 768
        assert o_ <= SCR
        kvin = region(SCR, 2, 2, S, parts=DH)
        zc = region(SCR + 1024, 2, 16, 2 * NCMP)
        merged = region(SCR, TOK, D)

        ps = ctx.enter_context(nc.psum_tensor("ps", [P, 8, 512], F32))
        GU, TB, MODB = 4, 6, 7
        QB, MB, SB, MID, OB = 0, 2, 4, 6, 7

        const_in = sem("const_in")
        setup_in = [sem(f"setup_in{i}") for i in range(4)]
        x_in = sem("x_in")
        raw_full = [sem(f"raw_full{i}") for i in range(RING)]
        hi_ready = sem("hi_ready")
        lo_ready = sem("lo_ready")
        unit_used = sem("unit_used")
        ada_full = [sem(f"ada_full{i}") for i in range(4)]
        ada_half = [sem(f"ada_half{i}") for i in range(2)]
        ada_sums = sem("ada_sums")
        ada_done = sem("ada_done")
        modps_done = sem("modps_done")
        mod_read = sem("mod_read")
        mod_ready = sem("mod_ready")
        gt_ps = sem("gt_ps")
        gt_ready = sem("gt_ready")
        h_ps = sem("h_ps")
        h32_ready = sem("h32_ready")
        hhi_ready = sem("hhi_ready")
        hlo_ready = sem("hlo_ready")
        xsq_done = sem("xsq_done")
        xrms_done = sem("xrms_done")
        xs_ready = sem("xs_ready")
        x_done = sem("x_done")
        g_ps = sem("g_ps")
        ysq_done = sem("ysq_done")
        yrms_done = sem("yrms_done")
        gu_done = sem("gu_done")
        silu_done = sem("silu_done")
        act_done = sem("act_done")
        at_ps = sem("at_ps")
        ahi_ready = sem("ahi_ready")
        alo_ready = sem("alo_ready")
        q_out_act = sem("q_out_act")
        q_out_dve = sem("q_out_dve")
        bg_in = sem("bg_in")
        bg_hi = sem("bg_hi")
        bg_lo = sem("bg_lo")
        bg_ps = sem("bg_ps")
        bg_exp = sem("bg_exp")
        bg_ready = sem("bg_ready")
        w1_in = sem("w1_in")
        z_ready = sem("z_ready")
        hid_ps = sem("hid_ps")
        hid_ready = sem("hid_ready")
        kc_ps = sem("kc_ps")
        kc_ready = sem("kc_ready")
        cs_ps = sem("cs_ps")
        cs_ready = sem("cs_ready")
        cexp_done = sem("cexp_done")
        cp_ready = sem("cp_ready")
        cpt_ps = sem("cpt_ps")
        cpt_ready = sem("cpt_ready")
        sc_done = sem("sc_done")
        s_read = sem("s_read")
        s_ready = sem("s_ready")
        front_done = sem("front_done")
        p_ready = sem("p_ready")
        mid_done = sem("mid_done")
        mask_done = sem("mask_done")
        pt_ready = sem("pt_ready")
        pv_done = sem("pv_done")
        y_hi = sem("y_hi")
        y_lo = sem("y_lo")
        mg_ps = sem("mg_ps")
        mg_ready = sem("mg_ready")
        br_ps = sem("br_ps")
        br_read = sem("br_read")
        m_ready = sem("m_ready")
        m_ps = sem("m_ps")
        mhi_ready = sem("mhi_ready")
        mlo_ready = sem("mlo_ready")
        act_own = sem("act_own")
        dve_own = sem("dve_own")
        setup_pe = sem("setup_pe")
        setup_dve = sem("setup_dve")
        scratch_out = sem("scratch_out")
        out_sem = sem("out_sem")

        OWN = 512

        class Own:

            def __init__(self, eng, s):
                self.eng, self.s, self.n, self.base = eng, s, 0, 0

            def end(self):
                assert self.n < OWN
                self.eng.sem_inc(self.s, OWN - self.n)

            def done(self, ins):
                ins.then_inc(self.s, 1)
                self.n += 1
                self.eng.wait_ge(self.s, self.base + self.n)

        block = ctx.enter_context(nc.Block())

        def used(l, k):
            return l * LAYER_UNITS + k + RING + 1

        def unit_of(l, k):
            return l * LAYER_UNITS + k

        def ada_width(f):
            return (2 if f == 0 else 1) * MOD // ADA_STEPS

        def ada_view(f, half):
            w = ada_width(f)
            at = 2 * MOD + half * 4 * w
            return arena[:, at:at + 4 * w].rearrange("p (c n) -> p c n", n=w)

        def ada_before(l, f, j):
            return (l * 2 + f) * KC * ADA_STEPS + (j - 1) * KC

        def unit_parts(k, l, j):
            slot = k % RING
            r = w_raw[:, slot, :]
            f, q = (0, k) if k < FFN_UNITS else (1, k - FFN_UNITS - MIX_UNITS)
            if 0 <= q < FFN_UNITS:
                kind, j = j
                if kind == "D":
                    rows = A["ffn_w_down"][l, f, bass.ds(j * FB, FB), :].rearrange("(c p) n -> p c n", p=P)
                    v = r.rearrange("p (c n) -> p c n", n=D)
                    return [(v[:, c], rows[:, c]) for c in range(2)]
                v = r.rearrange("p (c n) -> p c n", n=2 * FB)
                k0 = 0 if kind == "GA" else 4 * P
                return [(v[:, :, i * FB:(i + 1) * FB],
                         A[w][l, f, k0:k0 + 4 * P, bass.ds(j * FB, FB)].rearrange("(c p) n -> p c n", p=P))
                        for i, w in enumerate(("ffn_w_gate", "ffn_w_up"))]
            v_ = k - FFN_UNITS
            if v_ < QKV_UNITS:
                col = 256 * v_ if v_ < 8 else GATE_COL + 24 + 256 * (v_ - 8)
                v = r.rearrange("p (c n) -> p c n", n=256)
                src = A["w_in"][l, :, col:col + 256].rearrange("(c p) n -> p c n", p=P)
                return [(v[:, 4 * i:4 * i + 4], src[:, 4 * i:4 * i + 4]) for i in range(2)]
            v_ -= QKV_UNITS
            if v_ < 18:
                i, half, part = v_ // 6, v_ // 3 % 2, v_ % 3
                v = r.rearrange("p (c n) -> p c n", n=512)
                if part < 2:
                    c0 = MERGE_COL + i * D + half * 512
                    src = A["w_in"][l, part * 512:part * 512 + 512, c0:c0 + 512]
                else:
                    src = A["w_branch"][l, i, :, half * 512:half * 512 + 512]
                src = src.rearrange("(c p) n -> p c n", p=P)
                return [(v[:, 2 * e:2 * e + 2], src[:, 2 * e:2 * e + 2]) for e in range(2)]
            v_ -= 18
            rows = A["w_out"][l, v_ * 256:v_ * 256 + 256, :].rearrange("(c p) n -> p c n", p=P)
            v = r.rearrange("p (c n) -> p c n", n=D)
            return [(v[:, c], rows[:, c]) for c in range(2)]

        @block.sync
        def _(sp):
            for dst, src in ((ident, "k_ident"), (neg_tri, "k_negtri"), (causal01, "k_causal01"),
                             (causal_neg, "k_causalneg")):
                sp.dma_start(dst[:, :], A[src]).then_inc(const_in, 16)
            sp.dma_start(cmp_neg[:, :, :], A["k_cmpneg"]).then_inc(const_in, 16)
            sp.dma_start(cmp_01[:, :, :], A["k_cmp01"]).then_inc(const_in, 16)
            sp.dma_start(arena[0:KC, 12288:12288 + P], A["c"].rearrange("b (c p) -> (b c) p", p=P)).then_inc(setup_in[0], 16)
            sp.dma_start(arena[0:48, 12416:12416 + P],
                         A["ln_pre"].rearrange("l s (c p) -> (l s c) p", p=P)).then_inc(setup_in[0], 16)
            sp.dma_start(arena[0:48, 12544:12544 + P],
                         A["ln_post"].rearrange("l s (c p) -> (l s c) p", p=P)).then_inc(setup_in[0], 16)
            sp.dma_start(arena[0:72, 12672:12672 + 2 * P].rearrange("r (l p) -> r l p", p=P),
                         A["ada_b"].rearrange("l (r p) -> r l p", p=P)).then_inc(setup_in[0], 16)
            sp.dma_start(arena[0:DH, 12928:12928 + 2 * DH].rearrange("r (l d) -> r l d", d=DH),
                         A["cmp_pos"].rearrange("l k j d -> (k j) l d")).then_inc(setup_in[0], 16)
            sp.dma_start(x[:, :, :], A["x"][0].rearrange("(t p) d -> p t d", p=P)).then_inc(x_in, 16)
            for n in range(16):
                if n >= 4:
                    sp.wait_ge(ada_done, n - 3)
                b, k = n // KC, n % KC
                sp.dma_start(ada_raw[:, n % 4, :],
                             A["ada_w"][0, k * P:k * P + P, b * HALF:b * HALF + HALF]).then_inc(ada_full[n % 4], 16)
            sp.dma_start(w_raw[0:33, 0, 0:1024], A["k_buckets"]).then_inc(setup_in[1], 16)
            sp.dma_start(w_raw[0:32, 0, 1024:1040], A["rel_bias"]).then_inc(setup_in[1], 16)
            sp.dma_start(w_raw[:, 0, 1536:1536 + P], A["k_flip"]).then_inc(setup_in[1], 16)
            sp.dma_start(sink[:, :, :].rearrange("p l h -> p (l h)"),
                         A["attn_sinks"].rearrange("l h -> (l h)").unsqueeze(0).to_broadcast([P, DEPTH * HEADS])).then_inc(setup_in[1], 16)
            sp.wait_ge(setup_dve, 8)
            sp.dma_start(A["scratch"][:, :, :].rearrange("a h n -> h a n"),
                         w_raw[0:8, 1, 0:1024].rearrange("h (a n) -> h a n", n=512)[:, :, 0:384]).then_inc(scratch_out, 16)
            sp.wait_ge(scratch_out, 16)
            sc = A["scratch"]
            for i in range(2):
                sp.dma_start(w_raw[:, 1 + i, :].rearrange("p (h n) -> p h n", n=256),
                             bass.AP(tensor=sc.tensor, offset=i * 8 * 384, ap=[[1, P], [384, 8], [1, 256]])).then_inc(setup_in[2], 16)
            sp.wait_ge(setup_pe, 12)

            def load(l, k, j=None):
                sp.wait_ge(lo_ready, unit_of(l, k) + 1)
                for dst, src in unit_parts(k, l, j):
                    sp.dma_start(dst, src).then_inc(raw_full[k % RING], 16)

            def ffn(l, f):
                k0 = f * (FFN_UNITS + MIX_UNITS)
                load(l, k0, ("GA", 0))
                load(l, k0 + 1, ("GB", 0))

                def step(j, ada):
                    for i, kind in enumerate(("GA", "GB", "D")):
                        sp.wait_ge(lo_ready, unit_of(l, k0 + i) + j * 3)
                        for dst, src in unit_parts(k0 + 2 + i, l, (kind, j - 1 if kind == "D" else j)):
                            sp.dma_start(dst, src).then_inc(raw_full[(k0 + 2 + i) % RING], 16)
                        if i < 2 and ada:
                            if f == 0:
                                ada_load(j - 1, i)
                            else:
                                with sp.If(l < DEPTH - 1):
                                    ada_load(j - 1, i)

                def ada_load(j, half):
                    w = ada_width(f)
                    lw, col = (l, MOD) if f == 0 else ((l + 1) % DEPTH, 0)
                    sp.wait_ge(ada_sums, ada_before(l, f, j) + 4 * half - 4 + SUMS_AHEAD)
                    sp.dma_start(ada_view(f, half),
                                 A["ada_w"][lw, 4 * P * half:4 * P * half + 4 * P, bass.ds(col + (j - 1) * w, w)]
                                 .rearrange("(c p) n -> p c n", p=P)).then_inc(ada_half[half], 16)

                step(1, False)
                with sp.Fori(2, ADA_STEPS + 2) as j:
                    step(j, True)
                with sp.Fori(ADA_STEPS + 2, FSTEPS) as j:
                    step(j, False)
                load(l, k0 + FFN_UNITS - 1, ("D", FSTEPS - 1))

            with sp.Fori(0, DEPTH) as l:
                ffn(l, 0)
                for v in range(MIX_UNITS):
                    if v == 3:
                        sp.wait_ge(modps_done, l * 3 + 3)
                        sp.wait_ge(hlo_ready, (l * 3 + 1) * 4 + 4)
                        for e in range(2):
                            rows = A["cmp_w1"][l, e].rearrange("(c p) h -> p c h", p=P)
                            for half in range(2):
                                cs = slice(8 * half, 8 * half + 8)
                                sp.dma_start(w1[:, e, cs], rows[:, cs]).then_inc(w1_in, 16)
                        for e in range(2):
                            sp.dma_start(w2k[:, e, :], A["cmp_w2"][l, 0]).then_inc(w1_in, 16)
                        sp.dma_start(w2v[:, :], A["cmp_w2"][l, 1]).then_inc(w1_in, 16)
                        sp.dma_start(g_raw[:, :, :], A["w_in"][l, :, GATE_COL:GATE_COL + 24].rearrange("(c p) n -> p c n", p=P)).then_inc(bg_in, 16)
                    load(l, FFN_UNITS + v)
                ffn(l, 1)
            sp.wait_ge(x_done, DEPTH * NSUB * TOK + TOK)
            sp.dma_start(out[0].rearrange("(t p) d -> p t d", p=P), x[:, :, :]).then_inc(out_sem, 16)
            sp.wait_ge(out_sem, 16)

        @block.gpsimd
        def _(pool):
            pool.memset(ones[:, :], 1.0).then_inc(setup_in[3], 1)
            pool.memset(neg_ones[:, :], -1.0).then_inc(setup_in[3], 1)
            pool.memset(eps_t[:, :], EPS).then_inc(setup_in[3], 1)
            pool.memset(hid_v[:, :, :, :], 0.0).then_inc(setup_in[3], 1)
            pool.memset(cmp_p[:, :, :], 0.0).then_inc(setup_in[3], 1)

        @block.scalar
        def _(act):
            own = Own(act, act_own)

            def hi_parts(l, k):
                u = unit_of(l, k)
                act.wait_ge(raw_full[k % RING], l * (16 * LOADS * LAYER_UNITS // RING) + 16 * LOADS * (k // RING + 1) )
                act.wait_ge(unit_used, u + 1)
                act.activation(w_hi[:, k % RING, :], w_raw[:, k % RING, :], ACT.Copy).then_inc(hi_ready, 1)

            def rms_of_x(l, s):
                for t in range(TOK):
                    if s == 0:
                        act.wait_ge(x_done, l * 6 + t + 1)
                    else:
                        act.wait_ge(x_done, l * 6 + 2 * s + t + 1)
                    own.done(act.activation(xs[:, t, :], x[:, t, :], ACT.Square, accum_out=stat[:, t:t + 1]))
                act.activation(stat[:, 2:4], stat[:, 0:2], ACT.Sqrt, scale=1.0 / D, bias=eps_t[:, 0:1]).then_inc(xrms_done, 1)

            def split_h(l, s):
                for q in range(4):
                    act.wait_ge(h32_ready, (l * NSUB + s) * 4 + q + 1)
                    act.activation(h_hi[:, 2 * q:2 * q + 2, :], hbuf[:, 2 * q:2 * q + 2, :], ACT.Copy).then_inc(hhi_ready, 1)

            def rms_of_y(l, s):
                act.wait_ge(unit_used, used(l, (FFN_UNITS, FFN_UNITS + MIX_UNITS, LAYER_UNITS)[s] - 1))
                for t in range(TOK):
                    own.done(act.activation(xs[:, t, :].rearrange("p (a b) -> p a b", b=512), ps[:, 2 * t:2 * t + 2, :],
                                            ACT.Square, accum_out=stat[:, 4 + t:5 + t]))
                act.activation(stat[:, 6:8], stat[:, 4:6], ACT.Sqrt, scale=1.0 / D, bias=eps_t[:, 0:1]).then_inc(yrms_done, 1)

            def ffn(l, f):
                k0 = f * (FFN_UNITS + MIX_UNITS)

                def step(j, end, units):
                    n = (l * 2 + f) * FSTEPS
                    for t in range(TOK):
                        if t == 0:
                            act.wait_ge(gu_done, n + j + 1)
                        else:
                            act.wait_ge(unit_used, used(l, k0) + end)
                        act.activation(ffn_s[:, t, :], ps[:, GU + t, 0:FB], ACT.Silu).then_inc(silu_done, 1)
                    units(0)
                    units(1)
                    act.wait_ge(at_ps, n + j + 1)
                    act.activation(act_hi[:, 0, 0:2, :], ps[:, TB, :].rearrange("p (a b) -> p a b", b=S),
                                   ACT.Copy).then_inc(ahi_ready, 1)
                    units(2)

                step(0, 1, lambda i: hi_parts(l, k0 + 3 + i))
                with act.Fori(1, FSTEPS - 1) as j:
                    def units(i):
                        k = k0 + 3 + i
                        act.wait_ge(raw_full[k % RING], l * (16 * LOADS * LAYER_UNITS // RING) + j * (16 * LOADS) + 16 * LOADS * (k // RING + 1))
                        act.wait_ge(unit_used, unit_of(l, k) + j * 3 + 1)
                        act.activation(w_hi[:, k % RING, :], w_raw[:, k % RING, :], ACT.Copy).then_inc(hi_ready, 1)
                    step(j, 3 * j, units)
                step(FSTEPS - 1, 3 * FSTEPS - 3, (lambda i: hi_parts(l, k0 + FFN_UNITS + i)) if f == 0 else (lambda i: None))

            def front(l, n):
                kind, h = JOBS[n]
                b = n % 2
                if kind == "c":
                    act.wait_ge(sc_done, l * NJ + n + 1)
                    if n >= 26:
                        act.wait_ge(p_ready, l * NJ + n - 1)
                    own.done(act.activation(job_s[:, b, :], ps[:, SB + b, 0:3 * P], ACT.Abs))
                    own.done(act.activation(job_s[:, b, :], job_s[:, b, :], ACT.Exp, scale=-1.0))
                    act.activation(job_s[:, b, :], job_s[:, b, :], ACT.Ln, bias=1.0).then_inc(front_done, 1)
                    return
                act.wait_ge(s_ready, l * 24 + n + 1)
                if n >= 2:
                    act.wait_ge(mid_done, l * NJ + n - 1)
                st = jst[:, b, :]
                act.activation(job_p[:, b, 0:P], job_s[:, b, 0:P], ACT.Exp, bias=st[:, 2:3], accum_out=st[:, 4:5])
                if kind == "a":
                    act.activation(st[:, 6:8], st[:, 2:4], ACT.Exp, bias=sink[:, bass.ds(l, 1), h])
                act.activation(job_p[:, b, P:3 * P], job_s[:, b, P:3 * P], ACT.Exp, bias=st[:, 3:4],
                               accum_out=st[:, 5:6]).then_inc(front_done, 1)

            def back(l, n):
                b = n % 2
                if JOBS[n][0] == "c":
                    act.wait_ge(mask_done, l * HEADS + n - 24 + 1)
                    act.activation(job_t[:, b, :], job_t[:, b, :], ACT.Exp).then_inc(pt_ready, 1)
                    return
                act.wait_ge(mid_done, l * NJ + n + 1)
                act.activation(job_t[:, b, :], ps[:, MID, 0:3 * P], ACT.Copy).then_inc(pt_ready, 1)

            def pair_out(l, n):
                q = pair_done(n)
                if q is None:
                    return
                act.wait_ge(pv_done, l * NJ + n + 1)
                act.activation(act_hi[:, (q // 4) % 2, q % 4, :], ps[:, OB, 0:S], ACT.Copy).then_inc(y_hi, 1)

            def jobs(l, step):
                for n in job_slots(step):
                    if n < NJ:
                        front(l, n)
                    if 1 <= n <= NJ and JOBS[n - 1][0] != "c":
                        back(l, n - 1)
                    if n >= 2 and JOBS[n - 2][0] == "c":
                        back(l, n - 2)
                    if n >= 2:
                        pair_out(l, n - 2)

            act.wait_ge(x_in, 16)
            act.wait_ge(setup_in[3], 5)
            act.wait_ge(setup_dve, 1)
            act.activation(c_act[:, :], stat[:, 8:16], ACT.Silu).then_inc(setup_in[3], 1)

            with act.Fori(0, DEPTH) as l:
                own.n, own.base = 0, l * OWN
                rms_of_x(l, 0)
                for k in range(RING):
                    hi_parts(l, k)
                split_h(l, 0)
                ffn(l, 0)
                rms_of_y(l, 0)
                rms_of_x(l, 1)
                split_h(l, 1)
                for v in range(MIX_UNITS):
                    if v < QKV_UNITS:
                        if v not in (2, 5, 6, 7):
                            act.wait_ge(unit_used, used(l, FFN_UNITS + v))
                            bank = ps[:, QB + v % 2, :]
                            if v in (0, 1, 3, 4, 8, 9):
                                dst = {0: aq, 1: aq, 3: bq, 4: bq, 8: cq, 9: cq}[v]
                                b0 = {0: 0, 1: 2, 3: 0, 4: 2, 8: 0, 9: 2}[v]
                                act.activation(dst[:, b0:b0 + 2, :], bank.rearrange("p (a b) -> p a b", b=S),
                                               ACT.Copy, scale=DH ** -0.5).then_inc(q_out_act, 1)
                            elif v in (10, 11):
                                act.activation(ck[:, 2 * (v - 10):2 * (v - 10) + 2, :],
                                               bank.rearrange("p (a b) -> p a b", b=S), ACT.Copy).then_inc(q_out_act, 1)
                            else:
                                act.activation(cv[:, :, 256 * (v - 12):256 * (v - 12) + 256].rearrange("p t (a b) -> p t a b", b=P),
                                               bank.rearrange("p (a t b) -> p t a b", a=2, b=P), ACT.Copy).then_inc(q_out_act, 1)
                    if v == 5:
                        act.wait_ge(bg_in, l * 16 + 16)
                        act.activation(g_hi[:, :, :], g_raw[:, :, :], ACT.Copy).then_inc(bg_hi, 1)
                    if v == 6:
                        act.wait_ge(hid_ps, l + 1)
                        hp = ps[:, MB, 0:4 * NCMP].rearrange("p (k g n) -> p k g n", k=2, g=2)
                        act.activation(hid[:, 0, :, :], hp[:, 0], ACT.Gelu_apprx_tanh).then_inc(hid_ready, 1)
                        act.activation(hid[:, 1, :, :], hp[:, 1], ACT.Gelu_apprx_tanh).then_inc(hid_ready, 1)
                    if v == 7:
                        act.wait_ge(bg_ps, l + 1)
                        act.activation(egate[:, :, :], ps[:, MB + 1, 0:48].rearrange("p (t n) -> p t n", n=24),
                                       ACT.Exp, scale=-1.0).then_inc(bg_exp, 1)
                    if v == 8:
                        act.wait_ge(cs_ready, l + 1)
                        act.activation(cmp_p[:, :, 0:NCMP], cmp_p[:, :, 0:NCMP], ACT.Exp).then_inc(cexp_done, 1)
                    if v == 9:
                        act.wait_ge(cpt_ps, l + 1)
                        act.activation(cmp_pt[:, :, :, :], ps[:, MB + 1, :].rearrange("p (g t q) -> p g t q", g=2, t=2),
                                       ACT.Copy).then_inc(cpt_ready, 1)
                    if 14 <= v < 32 and (v - 14) % 3 == 1:
                        it = (v - 14) // 3
                        for t in range(TOK):
                            if t == 0:
                                act.wait_ge(mg_ps, l * 6 + it + 1)
                            else:
                                act.wait_ge(unit_used, used(l, FFN_UNITS + v))
                            if it:
                                act.wait_ge(br_read, (l * 6 + it) * 2)
                            act.activation(mg[:, t, :], ps[:, MB + t, :], ACT.Sigmoid).then_inc(mg_ready, 1)
                    if v >= 3 and v <= 26:
                        jobs(l, v)
                    if v == 31:
                        for q in range(4):
                            act.wait_ge(m_ps, l * 4 + q + 1)
                            act.activation(h_hi[:, 2 * q:2 * q + 2, :], ps[:, SB + q, :].rearrange("p (a b) -> p a b", b=S),
                                           ACT.Copy).then_inc(mhi_ready, 1)
                    hi_parts(l, FFN_UNITS + v + 3)
                rms_of_y(l, 1)
                rms_of_x(l, 2)
                split_h(l, 2)
                ffn(l, 1)
                rms_of_y(l, 2)
                own.end()

        @block.vector
        def _(dve):
            own = Own(dve, dve_own)

            def lo_parts(l, k):
                u = unit_of(l, k)
                dve.wait_ge(hi_ready, u + 1)
                dve.tensor_tensor(w_lo[:, k % RING, :], w_raw[:, k % RING, :], w_hi[:, k % RING, :].bitcast(F32),
                                  ALU.subtract).then_inc(lo_ready, 1)

            def modulate(l, s, n, lw=None):
                lw = l if lw is None else lw
                dve.wait_ge(modps_done, n)
                c0 = (lw * NSUB + s) * 24
                own.done(dve.tensor_tensor(modc[:, s, :], ps[:, MODB, s * 32:s * 32 + 24], adab_t[:, bass.ds(c0, 24)], ALU.add))
                g0 = (lw * NSUB + s) * KC
                own.done(dve.scalar_tensor_tensor(out=mod_a[:, s, :], in0=modc[:, s, KC:2 * KC], scalar=1.0,
                                                  in1=ln_t[:, 0, bass.ds(g0, KC)], op0=ALU.add, op1=ALU.mult))
                dve.scalar_tensor_tensor(out=mod_g[:, s, :], in0=modc[:, s, 2 * KC:3 * KC],
                                         scalar=1.0 if s == 1 else 0.5,
                                         in1=ln_t[:, 1, bass.ds(g0, KC)], op0=ALU.mult, op1=ALU.mult).then_inc(mod_ready, 1)
                dve.wait_ge(gt_ps, n)
                dve.tensor_copy(gt[:, s, :], ps[0:KC, MODB, 128:256]).then_inc(gt_ready, 1)

            def norm_h(l, s):
                dve.wait_ge(xrms_done, l * NSUB + s + 1)
                own.done(dve.reciprocal(stat[:, 0:2], stat[:, 2:4]))
                for t in range(TOK):
                    dve.tensor_scalar(out=xs[:, t, :], in0=x[:, t, :], scalar1=stat[:, t:t + 1], scalar2=None,
                                      op0=ALU.mult).then_inc(xs_ready, 1)
                for q in range(4):
                    dve.wait_ge(h_ps, (l * NSUB + s) * 4 + q + 1)
                    for c in (2 * q, 2 * q + 1):
                        ins = dve.tensor_scalar(out=hbuf[:, c, :], in0=ps[:, 4 + q, (c % 2) * S:(c % 2) * S + S],
                                                scalar1=mod_a[:, s, c:c + 1], scalar2=modc[:, s, c:c + 1],
                                                op0=ALU.mult, op1=ALU.add)
                    ins.then_inc(h32_ready, 1)
                    if q >= 1:
                        low_h(l, s, q - 1)
                low_h(l, s, 3)

            def low_h(l, s, q):
                dve.wait_ge(hhi_ready, (l * NSUB + s) * 4 + q + 1)
                dve.tensor_tensor(h_lo[:, 2 * q:2 * q + 2, :], hbuf[:, 2 * q:2 * q + 2, :],
                                  h_hi[:, 2 * q:2 * q + 2, :].bitcast(F32), ALU.subtract).then_inc(hlo_ready, 1)

            def residual(l, s):
                dve.wait_ge(yrms_done, l * NSUB + s + 1)
                own.done(dve.reciprocal(stat[:, 4:6], stat[:, 6:8]))
                dve.wait_ge(g_ps, l * NSUB + s + 1)
                for t in range(TOK):
                    tmp = xs[:, t, :].rearrange("p (a b) -> p a b", b=512)
                    if t == 0:
                        own.done(dve.tensor_copy(gate_sb,
                                                 ps[:, GU:GU + 2, :]))
                    own.done(dve.scalar_tensor_tensor(out=tmp, in0=ps[:, 2 * t:2 * t + 2, :], scalar=stat[:, 4 + t:5 + t],
                                                      in1=gate_sb,
                                                      op0=ALU.mult, op1=ALU.mult))
                    dve.tensor_tensor(x[:, t, :], x[:, t, :], xs[:, t, :], ALU.add).then_inc(x_done, 1)

            def ffn(l, f):
                k0 = f * (FFN_UNITS + MIX_UNITS)

                def step(j, units):
                    n = (l * 2 + f) * FSTEPS
                    for t in range(TOK):
                        dve.wait_ge(silu_done, n * 2 + j * 2 + t + 1)
                        dve.tensor_tensor(ffn_a[:, t, :], ffn_s[:, t, :], ps[:, GU + t, FB:2 * FB], ALU.mult).then_inc(act_done, 1)
                    units(0)
                    units(1)
                    dve.wait_ge(ahi_ready, n + j + 1)
                    dve.tensor_tensor(act_lo[:, 0, 0:2, :], ps[:, TB, :].rearrange("p (a b) -> p a b", b=S),
                                      act_hi[:, 0, 0:2, :].bitcast(F32), ALU.subtract).then_inc(alo_ready, 1)
                    units(2)

                step(0, lambda i: lo_parts(l, k0 + 3 + i))

                def loop_step(j, ada):
                    def units(i):
                        k = k0 + 3 + i
                        dve.wait_ge(hi_ready, unit_of(l, k) + j * 3 + 1)
                        dve.tensor_tensor(w_lo[:, k % RING, :], w_raw[:, k % RING, :], w_hi[:, k % RING, :].bitcast(F32),
                                          ALU.subtract).then_inc(lo_ready, 1)
                        if i >= 1 and ada:
                            if f == 0:
                                ada_half_sum(j, i - 1)
                            else:
                                with dve.If(l < DEPTH - 1):
                                    ada_half_sum(j, i - 1)
                    step(j, units)

                def ada_half_sum(j, half):
                    w = ada_width(f)
                    acc = ada_acc[:, bass.ds((j - 1) * w, w)]
                    src = ada_view(f, half)
                    dve.wait_ge(ada_half[half], ((l * 2 + f) * ADA_STEPS + j) * 16)
                    for c in range(4):
                        k = 4 * half + c
                        if k == 0:
                            ins = dve.tensor_scalar(out=acc, in0=src[:, c], scalar1=c_act[:, k:k + 1], scalar2=None, op0=ALU.mult)
                        else:
                            dve.wait_ge(ada_sums, ada_before(l, f, j) + k + SUMS_AHEAD)
                            ins = dve.scalar_tensor_tensor(out=acc, in0=src[:, c], scalar=c_act[:, k:k + 1], in1=acc,
                                                           op0=ALU.mult, op1=ALU.add)
                        ins.then_inc(ada_sums, 1)

                with dve.Fori(1, ADA_STEPS + 1) as j:
                    loop_step(j, True)
                with dve.Fori(ADA_STEPS + 1, FSTEPS - 1) as j:
                    loop_step(j, False)
                step(FSTEPS - 1, (lambda i: lo_parts(l, k0 + FFN_UNITS + i)) if f == 0 else (lambda i: None))

            def front(l, n):
                kind, h = JOBS[n]
                if kind == "c":
                    return
                b = n % 2
                st = jst[:, b, :]
                row = bias[:, h if kind == "a" else HEADS + h, :]
                dve.wait_ge(sc_done, l * NJ + n + 1)
                dve.tensor_tensor(job_s[:, b, 0:P], ps[:, SB + b, 0:P], row[:, P:2 * P], ALU.add)
                dve_read = dve.tensor_tensor(job_s[:, b, P:3 * P], ps[:, SB + b, P:3 * P], row, ALU.add)
                dve_read.then_inc(s_read, 1)
                dve.wait_ge(s_read, l * NJ + n + 1)
                dve.tensor_reduce(st[:, 0:1], job_s[:, b, 0:P], axis=AX.X, op=ALU.max)
                own.done(dve.tensor_reduce(st[:, 1:2], job_s[:, b, P:3 * P], axis=AX.X, op=ALU.max))
                if kind == "a":
                    dve.tensor_scalar(out=st[:, 2:4], in0=st[:, 0:2], scalar1=sink[:, bass.ds(l, 1), h], scalar2=-1.0,
                                      op0=ALU.max, op1=ALU.mult).then_inc(s_ready, 1)
                else:
                    dve.tensor_scalar(out=st[:, 2:4], in0=st[:, 0:2], scalar1=-1.0, scalar2=None,
                                      op0=ALU.mult).then_inc(s_ready, 1)

            def middle(l, n):
                kind, h = JOBS[n]
                b = n % 2
                st = jst[:, b, :]
                dve.wait_ge(front_done, l * NJ + n + 1)
                if kind == "c":
                    if n >= 26:
                        dve.wait_ge(mid_done, l * NJ + n - 1)
                    ins = dve.scalar_tensor_tensor(out=job_p[:, b, :], in0=ps[:, SB + b, 0:3 * P], scalar=0.0,
                                                   in1=job_s[:, b, :], op0=ALU.max, op1=ALU.add)
                    ins.then_inc(s_read, 1)
                    dve.wait_ge(s_read, l * NJ + n + 1)
                    dve.tensor_tensor(job_p[:, b, :], job_p[:, b, :], causal01[:, :], ALU.mult).then_inc(p_ready, 1)
                    return
                if kind == "a":
                    own.done(dve.tensor_tensor(st[:, 4:6], st[:, 4:6], st[:, 6:8], ALU.add))
                own.done(dve.reciprocal(st[:, 8:10], st[:, 4:6]))
                if kind != "a":
                    c0 = HEADS * (1 if kind == "slc" else 2) + h
                    own.done(dve.tensor_tensor(st[:, 8:10], st[:, 8:10], bgate[:, :, c0], ALU.mult))
                dve.tensor_scalar(out=job_p[:, b, 0:P], in0=job_p[:, b, 0:P], scalar1=st[:, 8:9], scalar2=None, op0=ALU.mult)
                dve.tensor_scalar(out=job_p[:, b, P:3 * P], in0=job_p[:, b, P:3 * P], scalar1=st[:, 9:10], scalar2=None,
                                  op0=ALU.mult).then_inc(p_ready, 1)

            def mask(l, n):
                dve.wait_ge(mid_done, l * NJ + n + 1)
                dve.wait_ge(pv_done, l * NJ + n - 1)
                dve.tensor_tensor(job_t[:, n % 2, :], ps[:, MID, 0:3 * P], causal_neg[:, :], ALU.add).then_inc(mask_done, 1)

            def pair_out(l, n):
                q = pair_done(n)
                if q is None:
                    return
                dve.wait_ge(y_hi, l * 12 + q + 1)
                dve.tensor_tensor(act_lo[:, (q // 4) % 2, q % 4, :], ps[:, OB, 0:S],
                                  act_hi[:, (q // 4) % 2, q % 4, :].bitcast(F32), ALU.subtract).then_inc(y_lo, 1)

            def jobs(l, step):
                for n in job_slots(step):
                    if n < NJ:
                        front(l, n)
                    if 2 <= n and JOBS[n - 2][0] == "c":
                        mask(l, n - 2)
                    if 1 <= n <= NJ:
                        middle(l, n - 1)
                    if n >= 2:
                        pair_out(l, n - 2)

            dve.wait_ge(x_in, 16)
            dve.sem_inc(lo_ready, RING)
            dve.sem_inc(ada_sums, SUMS_AHEAD)
            dve.sem_inc(x_done, TOK)
            dve.wait_ge(setup_pe, 1)
            dve.tensor_copy(stat[:, 8:16], ps[:, 0, 0:KC]).then_inc(setup_dve, 1)
            dve.wait_ge(setup_pe, 7)
            dve.tensor_copy(ln_t[:, 0, :], ps[:, 1, 0:48]).then_inc(setup_dve, 1)
            dve.tensor_copy(ln_t[:, 1, :], ps[:, 1, 64:112]).then_inc(setup_dve, 1)
            dve.tensor_copy(adab_t[:, :].rearrange("p (l r) -> p l r", l=2),
                            ps[:, 1, 128:384].rearrange("p (l r) -> p l r", l=2)[:, :, 0:72]).then_inc(setup_dve, 1)
            dve.tensor_copy(pos_t[:, :, :], ps[0:DH, 1, 384:512].rearrange("p (l r) -> p l r", l=2)).then_inc(setup_dve, 1)
            dve.wait_ge(setup_in[3], 6)
            for n in range(16):
                b, k = n // KC, n % KC
                acc = ada_acc[:, b * HALF:b * HALF + HALF]
                dve.wait_ge(ada_full[n % 4], 16 * (n // 4 + 1))
                if n:
                    dve.wait_ge(ada_done, n)
                if k == 0:
                    ins = dve.tensor_scalar(out=acc, in0=ada_raw[:, n % 4, :], scalar1=c_act[:, k:k + 1], scalar2=None, op0=ALU.mult)
                else:
                    ins = dve.scalar_tensor_tensor(out=acc, in0=ada_raw[:, n % 4, :], scalar=c_act[:, k:k + 1],
                                                   in1=acc, op0=ALU.mult, op1=ALU.add)
                ins.then_inc(ada_done, 1)
            dve.wait_ge(setup_in[1], 64)
            dve.memset(w_raw[32:33, 0, 1024:1040], 1.0).then_inc(setup_dve, 1)
            dve.wait_ge(setup_pe, 8)
            dve.tensor_copy(w_raw[0:8, 1, 0:1024].rearrange("h (a n) -> h a n", n=512)[:, :, 0:384],
                            ps[0:8, 2:4, 0:384]).then_inc(setup_dve, 2)
            for i in range(4):
                dve.wait_ge(setup_pe, 9 + i)
                dve.tensor_copy(bias[:, 4 * i:4 * i + 4, :].rearrange("p a b -> p (a b)").rearrange("p (a b) -> p a b", b=512),
                                ps[:, 4 + 2 * (i % 2):6 + 2 * (i % 2), :]).then_inc(setup_dve, 1)

            modulate(0, 0, 1)
            own.end()
            with dve.Fori(0, DEPTH) as l:
                own.n, own.base = 0, l * OWN + OWN
                norm_h(l, 0)
                for k in range(RING):
                    lo_parts(l, k)
                ffn(l, 0)
                residual(l, 0)
                modulate(l, 1, l * 3 + 2)
                modulate(l, 2, l * 3 + 3)
                norm_h(l, 1)
                for v in range(MIX_UNITS):
                    if v in (2, 5, 6, 7):
                        dve.wait_ge(unit_used, used(l, FFN_UNITS + v))
                        bank = ps[:, QB + v % 2, :]
                        if v == 5:
                            for g in range(2):
                                ins = dve.tensor_copy(kvin[:, :, g, :],
                                                      bank[DH * g:DH * g + DH, :].rearrange("p (k s) -> p k s", s=S))
                            ins.then_inc(q_out_dve, 1)
                        else:
                            kdst = {2: ak, 6: bks, 7: bkw}[v]
                            vdst = {2: av, 6: bvs, 7: bvw}[v]
                            for g in range(2):
                                for half in range(2):
                                    dve.tensor_copy(kdst[DH * half:DH * half + DH, g, :], bank[DH * g:DH * g + DH, 0:S])
                            dve.tensor_copy(vdst[:, :, :], bank[:, S:2 * S].rearrange("p (t n) -> p t n", n=P)).then_inc(q_out_dve, 1)
                    if v == 5:
                        dve.wait_ge(q_out_dve, l * 4 + 2)
                        for e in range(2):
                            for half in range(2):
                                for g in range(2):
                                    a0 = kvin[:, e, g, :]
                                    src = bass.AP(tensor=a0.tensor, offset=a0.offset + half,
                                                  ap=[list(a0.ap[0]), [2, 16], [CMP_STRIDE, NCMP]])
                                    pp = pos_t[:, bass.ds(l, 1), e * CMP_BLOCK:(e + 1) * CMP_BLOCK]\
                                        .rearrange("p a (c r) -> p (a c) r", r=2)[:, :, half:half + 1].to_broadcast([DH, 16, NCMP])
                                    ins = dve.tensor_tensor(zc[DH * half:DH * half + DH, e, :, g * NCMP:(g + 1) * NCMP],
                                                            src, pp, ALU.add)
                        ins.then_inc(z_ready, 1)
                        dve.wait_ge(bg_hi, l + 1)
                        dve.tensor_tensor(g_lo[:, :, :], g_raw[:, :, :], g_hi[:, :, :].bitcast(F32), ALU.subtract).then_inc(bg_lo, 1)
                    if v == 6:
                        dve.wait_ge(hid_ready, l * 2 + 2)
                        for g in range(2):
                            ins = dve.tensor_copy(hid_v[:, g, :, 0:NCMP], hid[:, 1, g, :].unsqueeze(1).to_broadcast([P, 4, NCMP]))
                        ins.then_inc(hid_ready, 1) if False else ins.then_inc(kc_ready, 1)
                    if v == 7:
                        dve.wait_ge(kc_ps, l + 1)
                        dve.tensor_copy(kc_t[:, :, :], ps[:, MB, 128:128 + 2 * NCMP].rearrange("p (g n) -> p g n", g=2))
                        dve.tensor_copy(vc[:, :, :], ps[:, MB, 256:256 + 2 * DH].rearrange("p (g n) -> p g n", g=2)).then_inc(kc_ready, 1)
                        dve.wait_ge(bg_exp, l + 1)
                        own.done(dve.tensor_scalar(out=egate[:, :, :], in0=egate[:, :, :], scalar1=1.0, scalar2=None, op0=ALU.add))
                        dve.reciprocal(bgate[:, :, :], egate[:, :, :]).then_inc(bg_ready, 1)
                    if v == 8:
                        dve.wait_ge(cs_ps, l + 1)
                        dve.wait_ge(bg_ready, l + 1)
                        cp = cmp_p[:, :, 0:NCMP]
                        for odd in range(2):
                            logits = ps[:, MB + 1 - odd, 0:256].rearrange("p (g t h n) -> p g t h n", g=2, t=TOK, n=32)
                            for g in range(2):
                                for t in range(TOK):
                                    r = (g * TOK + t) * 4 + odd
                                    ins = dve.tensor_tensor(cp[:, r:r + 3:2], logits[:, g, t, :, 0:NCMP],
                                                            cmp_neg[:, t:t + 1, :].to_broadcast([P, 2, NCMP]), ALU.add)
                        own.done(ins)
                        own.done(dve.tensor_reduce(cst[:, 0, :], cp, axis=AX.X, op=ALU.max))
                        dve.tensor_tensor(cp, cp, cst[:, 0, :].unsqueeze(2).to_broadcast([P, 16, NCMP]), ALU.subtract).then_inc(cs_ready, 1)
                        dve.wait_ge(cexp_done, l + 1)
                        for g in range(2):
                            for t in range(TOK):
                                r = (g * TOK + t) * 4
                                ins = dve.tensor_tensor(cp[:, r:r + 4], cp[:, r:r + 4],
                                                        cmp_01[:, t:t + 1, :].to_broadcast([P, 4, NCMP]), ALU.mult)
                        own.done(ins)
                        own.done(dve.tensor_reduce(cst[:, 1, :], cp, axis=AX.X, op=ALU.add))
                        own.done(dve.tensor_scalar(out=cst[:, 1, :], in0=cst[:, 1, :], scalar1=1e-30, scalar2=None, op0=ALU.max))
                        own.done(dve.reciprocal(cst[:, 2, :], cst[:, 1, :]))
                        for g in range(2):
                            ins = dve.tensor_tensor(cst[:, 2, 8 * g:8 * g + 8].rearrange("p (t h) -> p t h", h=4),
                                                    cst[:, 2, 8 * g:8 * g + 8].rearrange("p (t h) -> p t h", h=4),
                                                    bgate[:, :, 4 * g:4 * g + 4], ALU.mult)
                        own.done(ins)
                        dve.tensor_tensor(cp, cp, cst[:, 2, :].unsqueeze(2).to_broadcast([P, 16, NCMP]), ALU.mult).then_inc(cp_ready, 1)
                    if 14 <= v < 32 and (v - 14) % 3 == 2:
                        it = (v - 14) // 3
                        i, half = it // 2, it % 2
                        for t in range(TOK):
                            if t == 0:
                                dve.wait_ge(br_ps, l * 6 + it + 1)
                            else:
                                dve.wait_ge(unit_used, used(l, FFN_UNITS + v))
                            dve.wait_ge(mg_ready, (l * 6 + it) * 2 + t + 1)
                            m = merged[:, t, half * 512:half * 512 + 512]
                            if i == 0:
                                dve.tensor_tensor(m, mg[:, t, :], ps[:, QB + t, :], ALU.mult).then_inc(br_read, 1)
                            else:
                                dve.tensor_tensor(mg[:, t, :], mg[:, t, :], ps[:, QB + t, :], ALU.mult).then_inc(dve_own, 1)
                                own.n += 1
                                dve.wait_ge(dve_own, own.base + own.n)
                                dve.tensor_tensor(m, m, mg[:, t, :], ALU.add).then_inc(br_read, 1)
                    if v >= 3 and v <= 26:
                        jobs(l, v)
                    if v == 31:
                        for q in range(4):
                            dve.wait_ge(mhi_ready, l * 4 + q + 1)
                            dve.tensor_tensor(h_lo[:, 2 * q:2 * q + 2, :], ps[:, SB + q, :].rearrange("p (a b) -> p a b", b=S),
                                              h_hi[:, 2 * q:2 * q + 2, :].bitcast(F32), ALU.subtract).then_inc(mlo_ready, 1)
                    lo_parts(l, FFN_UNITS + v + 3)
                residual(l, 1)
                norm_h(l, 2)
                ffn(l, 1)
                residual(l, 2)
                with dve.If(l < DEPTH - 1):
                    modulate(l, 0, l * 3 + 4, lw=(l + 1) % DEPTH)
                own.end()

        @block.tensor
        def _(pe):
            def three(out_, lhs, rhs, first, last):
                (lh, ll), (rh, rl) = lhs, rhs
                pe.matmul(out_, lh, rh, start=first, stop=False, skip_group_check=True)
                pe.matmul(out_, lh, rl, start=False, stop=False, skip_group_check=True)
                return pe.matmul(out_, ll, rh, start=False, stop=last, skip_group_check=True)

            def w_part(k, width):
                s = k % RING
                return (w_hi[:, s, :].rearrange("p (c n) -> p c n", n=width),
                        w_lo[:, s, :].rearrange("p (c n) -> p c n", n=width))

            def columns(s, n0, src):
                for c in range(24):
                    ins = pe.matmul(ps[:, MODB, s * 32 + c:s * 32 + c + 1], src[:, n0 + c * P:n0 + c * P + P], ones[:, 0:1],
                                    start=True, stop=True)
                return ins

            def gate_row(s, n):
                pe.wait_ge(mod_ready, n)
                pe.transpose(ps[0:KC, MODB, 128:256], mod_g[:, s, :], ident[:, :]).then_inc(gt_ps, 1)

            def h_columns(l, s):
                for t in range(TOK):
                    pe.wait_ge(xs_ready, (l * NSUB + s) * 2 + t + 1)
                for q in range(4):
                    for c in (2 * q, 2 * q + 1):
                        for t in range(TOK):
                            ins = pe.transpose(ps[:, 4 + q, (c % 2) * S + t * P:(c % 2) * S + t * P + P],
                                               xs[:, t, c * P:c * P + P], ident[:, :])
                    ins.then_inc(h_ps, 1)
                pe.wait_ge(hlo_ready, (l * NSUB + s) * 4 + 4)

            def gate_rows_out(l, s):
                pe.wait_ge(gt_ready, l * NSUB + s + 1)
                for c in range(KC):
                    ins = pe.matmul(ps[:, GU + c // 4, (c % 4) * P:(c % 4) * P + P],
                                    ident[0:KC, c:c + 1].to_broadcast([KC, P]), gt[:, s, :], start=True, stop=True)
                ins.then_inc(g_ps, 1)

            def ffn(l, f):
                k0 = f * (FFN_UNITS + MIX_UNITS)
                n = (l * 2 + f) * FSTEPS

                def wait_unit(k, j):
                    pe.wait_ge(lo_ready, unit_of(l, k) + 3 * j + RING + 1)

                def gate_up(k, part, j, jr, first=False):
                    wait_unit(k, jr)
                    wh, wl = w_part(k, 2 * FB)
                    if part == 0 and not first:
                        pe.wait_ge(act_done, 2 * (n + j))
                    for t in range(TOK):
                        for c in range(4):
                            kc = 4 * part + c
                            ts = slice(t * P, t * P + P)
                            ins = three(ps[:, GU + t, :], (h_hi[:, kc, ts], h_lo[:, kc, ts]), (wh[:, c], wl[:, c]),
                                        kc == 0, kc == KC - 1)
                        if t == 1:
                            ins.then_inc(unit_used, 1)
                        elif part == 1:
                            ins.then_inc(gu_done, 1)

                def turn(j):
                    pe.wait_ge(act_done, 2 * (n + j) + 2)
                    for c in range(2):
                        for t in range(TOK):
                            ins = pe.transpose(ps[:, TB, c * S + t * P:c * S + t * P + P], ffn_a[:, t, c * P:c * P + P], ident[:, :])
                    ins.then_inc(at_ps, 1)

                def down(k, j, jr, first, last):
                    wait_unit(k, jr)
                    pe.wait_ge(alo_ready, n + j + 1)
                    wh, wl = w_part(k, D)
                    for t in range(TOK):
                        for half in range(2):
                            for c in range(2):
                                ts = slice(t * P, t * P + P)
                                hs = slice(half * 512, half * 512 + 512)
                                ins = three(ps[:, 2 * t + half, :], (act_hi[:, 0, c, ts], act_lo[:, 0, c, ts]),
                                            (wh[:, c, hs], wl[:, c, hs]), first and c == 0, last and c == 1)
                    ins.then_inc(unit_used, 1)

                gate_up(k0, 0, 0, 0, first=True)
                gate_up(k0 + 1, 1, 0, 0)
                gate_up(k0 + 2, 0, 1, 0)
                turn(0)
                gate_up(k0 + 3, 1, 1, 0)
                down(k0 + 4, 0, 0, True, False)
                with pe.Fori(2, FSTEPS) as j:
                    gate_up(k0 - 1, 0, j, j)
                    turn(j - 1)
                    gate_up(k0, 1, j, j)
                    down(k0 + 1, j - 1, j, False, False)
                turn(FSTEPS - 1)
                down(k0 + FFN_UNITS - 1, FSTEPS - 1, 0, False, True)

            def front(l, n):
                kind, h = JOBS[n]
                b = n % 2
                po = DH * (h % 2)
                g = h // HPG
                hs = slice(po, po + DH)
                if n == 0 or n == 8 or n == 24:
                    pe.wait_ge(q_out_act, l * 10 + {0: 2, 8: 4, 24: 10}[n])
                    pe.wait_ge(q_out_dve, l * 4 + {0: 1, 8: 4, 24: 4}[n])
                if n >= 2:
                    pe.wait_ge(s_read, l * NJ + n - 1)
                S_ = ps[:, SB + b, :]
                if kind == "c":
                    q, k = cq[hs, h // 2, :], ck[hs, h // 2, :]
                    pe.matmul(S_[:, 0:S], k[:, 0:P], q, start=True, stop=True)
                    pe.matmul(S_[:, S:S + P], k[:, P:2 * P], q[:, P:2 * P], start=True, stop=True).then_inc(sc_done, 1)
                    return
                q = (aq if kind == "a" else bq)[hs, h // 2, :]
                k = {"a": ak, "slc": bks, "win": bkw}[kind][hs, g, :]
                pe.matmul(S_[:, 0:P], q[:, 0:P], k[:, 0:P], start=True, stop=True)
                pe.matmul(S_[:, P:3 * P], q[:, P:2 * P], k, start=True, stop=True).then_inc(sc_done, 1)

            def middle(l, n):
                kind, h = JOBS[n]
                b = n % 2
                po = DH * (h % 2)
                hs = slice(po, po + DH)
                pe.wait_ge(p_ready, l * NJ + n + 1)
                if n >= 1:
                    if JOBS[n - 1][0] == "c":
                        pe.wait_ge(mask_done, l * HEADS + n - 24)
                    else:
                        pe.wait_ge(pt_ready, l * NJ + n)
                M_ = ps[:, MID, :]
                if kind == "c":
                    q, k = cq[hs, h // 2, :], ck[hs, h // 2, :]
                    L = job_p[:, b, :]
                    pe.matmul(M_[:, 0:S], neg_tri[:, :], L[:, 0:S], start=True, stop=False, skip_group_check=True)
                    pe.matmul(M_[:, P:S], neg_ones[:, :], L[:, S:S + P], start=False, stop=False, skip_group_check=True)
                    pe.matmul(M_[:, S:S + P], neg_tri[:, :], L[:, S:S + P], start=False, stop=False, skip_group_check=True)
                    pe.matmul(M_[:, 0:S], k[:, 0:P], q, start=False, stop=False, skip_group_check=True)
                    pe.matmul(M_[:, S:S + P], k[:, P:2 * P], q[:, P:2 * P], start=False, stop=True,
                              skip_group_check=True).then_inc(mid_done, 1)
                    return
                for i in range(3):
                    ins = pe.transpose(M_[:, i * P:i * P + P], job_p[:, b, i * P:i * P + P], ident[:, :])
                ins.then_inc(mid_done, 1)

            def values(l, n):
                kind, h = JOBS[n]
                b = n % 2
                po = DH * (h % 2)
                g = h // HPG
                pe.wait_ge(pt_ready, l * NJ + n + 1)
                done = {"a": 0, "slc": 4, "win": 4, "c": 8}[kind] + h // 2
                if h % 2 == 0 and kind != "win" and n:
                    pe.wait_ge(y_lo, l * 12 + done)
                O = ps[po:po + DH, OB, :]
                v = {"a": av, "slc": bvs, "win": bvw, "c": cv}[kind]
                vs = slice(h * DH, h * DH + DH) if kind == "c" else slice(g * DH, g * DH + DH)
                pe.matmul(O[:, 0:S], v[:, 0, vs], job_t[:, b, 0:S], start=kind != "win", stop=False, skip_group_check=True)
                ins = pe.matmul(O[:, P:S], v[:, 1, vs], job_t[:, b, S:S + P], start=False, stop=kind in "ac",
                                skip_group_check=True)
                if kind == "win":
                    if h == 0:
                        pe.wait_ge(cpt_ready, l + 1)
                    r = 32 * (h % 4)
                    for t in range(TOK):
                        ins = pe.matmul(O[:, t * P:t * P + P], vc[r:r + NCMP, g, :], cmp_pt[r:r + NCMP, g, t, :],
                                        start=False, stop=t == 1, skip_group_check=True)
                ins.then_inc(pv_done, 1)

            def jobs(l, step):
                for n in job_slots(step):
                    if n < NJ:
                        front(l, n)
                    if 1 <= n <= NJ:
                        middle(l, n - 1)
                    if n >= 2:
                        values(l, n - 2)

            pe.sem_inc(unit_used, RING)
            pe.wait_ge(const_in, 96)
            pe.wait_ge(setup_in[0], 80)
            pe.wait_ge(setup_in[3], 5)
            pe.transpose(ps[:, 0, 0:KC], arena[0:KC, 12288:12288 + P], ident[0:KC, 0:KC]).then_inc(setup_pe, 1)
            for i in range(2):
                pe.transpose(ps[:, 1, 64 * i:64 * i + 48], arena[0:48, 12416 + P * i:12416 + P * i + P], ident[0:48, 0:48]).then_inc(setup_pe, 1)
            for i in range(2):
                pe.transpose(ps[:, 1, 128 + P * i:128 + P * i + 72], arena[0:72, 12672 + P * i:12672 + P * i + P], ident[0:72, 0:72]).then_inc(setup_pe, 1)
            for i in range(2):
                pe.transpose(ps[0:DH, 1, 384 + DH * i:384 + DH * i + DH], arena[0:DH, 12928 + DH * i:12928 + DH * i + DH],
                             ident[0:DH, 0:DH]).then_inc(setup_pe, 1)
            pe.wait_ge(setup_dve, 6)
            for i in range(2):
                ins = pe.matmul(ps[0:8, 2 + i, 0:384], w_raw[0:33, 0, 1024 + 8 * i:1032 + 8 * i], w_raw[0:33, 0, 512 * i:512 * i + 384],
                                start=True, stop=True)
            ins.then_inc(setup_pe, 1)
            pe.wait_ge(setup_in[2], 32)
            for i in range(4):
                if i >= 2:
                    pe.wait_ge(setup_dve, 8 + i - 1)
                for e in range(2):
                    ins = pe.matmul(ps[:, 4 + 2 * (i % 2) + e, :], w_raw[:, 0, 1536:1536 + P],
                                    w_raw[:, 1 + i // 2, (i % 2) * 1024 + e * 512:(i % 2) * 1024 + e * 512 + 512], start=True, stop=True)
                ins.then_inc(setup_pe, 1)
            pe.wait_ge(ada_done, 16)
            pe.wait_ge(setup_dve, 12)
            columns(0, 0, ada_acc).then_inc(modps_done, 1)
            gate_row(0, 1)
            with pe.Fori(0, DEPTH) as l:
                h_columns(l, 0)
                ffn(l, 0)
                gate_rows_out(l, 0)
                pe.wait_ge(ada_sums, ada_before(l, 1, 1) + SUMS_AHEAD)
                pe.wait_ge(gt_ready, l * NSUB + 1)
                columns(1, 0, ada_acc).then_inc(modps_done, 1)
                gate_row(1, l * 3 + 2)
                pe.wait_ge(gt_ready, l * NSUB + 2)
                columns(2, MOD, ada_acc).then_inc(modps_done, 1)
                gate_row(2, l * 3 + 3)
                h_columns(l, 1)
                for v in range(MIX_UNITS):
                    k = FFN_UNITS + v
                    pe.wait_ge(lo_ready, unit_of(l, k) + RING + 1)
                    if v < QKV_UNITS:
                        if v == 0:
                            pe.wait_ge(x_done, l * 6 + TOK + 2)
                        elif v >= 2:
                            a_ = sum(1 for w in range(v - 1) if w not in (2, 5, 6, 7))
                            d_ = sum(1 for w in range(v - 1) if w in (2, 5, 6, 7))
                            if v - 2 in (2, 5, 6, 7):
                                pe.wait_ge(q_out_dve, l * 4 + d_)
                            else:
                                pe.wait_ge(q_out_act, l * 10 + a_)
                        wh, wl = w_part(k, 256)
                        bank = ps[:, QB + v % 2, :]
                        for b in range(2):
                            bs = slice(b * P, b * P + P)
                            as_rows = v in (12, 13) or (b == 1 and v in (2, 6, 7))
                            if as_rows:
                                for t in range(TOK):
                                    ts = slice(t * P, t * P + P)
                                    for c in range(KC):
                                        ins = three(bank[:, b * S + t * P:b * S + t * P + P], (h_hi[:, c, ts], h_lo[:, c, ts]),
                                                    (wh[:, c, bs], wl[:, c, bs]), c == 0, c == KC - 1)
                            else:
                                for c in range(KC):
                                    ins = three(bank[:, b * S:b * S + S], (wh[:, c, bs], wl[:, c, bs]),
                                                (h_hi[:, c, :], h_lo[:, c, :]), c == 0, c == KC - 1)
                        ins.then_inc(unit_used, 1)
                    elif v < 32:
                        it, part = (v - 14) // 3, (v - 14) % 3
                        i = it // 2
                        wh, wl = w_part(k, 512)
                        if part == 0:
                            if it:
                                pe.wait_ge(mg_ready, (l * 6 + it) * 2)
                            else:
                                pe.wait_ge(cpt_ready, l + 1)
                        if part == 2:
                            if it:
                                pe.wait_ge(br_read, (l * 6 + it) * 2)
                            else:
                                pe.wait_ge(q_out_act, l * 10 + 10)
                            pe.wait_ge(y_lo, l * 12 + 4 * i + 4)
                        for t in range(TOK):
                            ts = slice(t * P, t * P + P)
                            for c in range(4):
                                if part < 2:
                                    kc = 4 * part + c
                                    ins = three(ps[:, MB + t, :], (h_hi[:, kc, ts], h_lo[:, kc, ts]), (wh[:, c], wl[:, c]),
                                                kc == 0, kc == KC - 1)
                                else:
                                    ins = three(ps[:, QB + t, :], (act_hi[:, i % 2, c, ts], act_lo[:, i % 2, c, ts]),
                                                (wh[:, c], wl[:, c]), c == 0, c == 3)
                            if t == 1:
                                ins.then_inc(unit_used, 1)
                            elif part == 1:
                                ins.then_inc(mg_ps, 1)
                            elif part == 2:
                                ins.then_inc(br_ps, 1)
                    else:
                        wh, wl = w_part(k, D)
                        if v == 32:
                            pe.wait_ge(mlo_ready, l * 4 + 4)
                        for t in range(TOK):
                            ts = slice(t * P, t * P + P)
                            for half in range(2):
                                hs = slice(half * 512, half * 512 + 512)
                                for c in range(2):
                                    kc = 2 * (v - 32) + c
                                    ins = three(ps[:, 2 * t + half, :], (h_hi[:, kc, ts], h_lo[:, kc, ts]),
                                                (wh[:, c, hs], wl[:, c, hs]), kc == 0, kc == KC - 1)
                        ins.then_inc(unit_used, 1)
                    if v == 5:
                        pe.wait_ge(w1_in, l * 112 + 112)
                        pe.wait_ge(z_ready, l + 1)
                        for e in range(2):
                            for c in range(16):
                                ins = pe.matmul(ps[:, MB, e * 2 * NCMP:(e + 1) * 2 * NCMP], w1[:, e, c, :], zc[:, e, c, :],
                                                start=c == 0, stop=c == 15)
                        ins.then_inc(hid_ps, 1)
                    if v == 6:
                        pe.wait_ge(kc_ready, l * 2 + 1)
                        pe.matmul(ps[:, MB, 128:128 + 2 * NCMP], w2k[:, :, :].rearrange("p a b -> p (a b)"),
                                  hid[:, 0, :, :].rearrange("p a b -> p (a b)"), start=True, stop=True)
                        for g in range(2):
                            ins = pe.matmul(ps[:, MB, 256 + g * DH:256 + g * DH + DH],
                                            hid_v[:, g, :, :].rearrange("p a b -> p (a b)"), w2v[:, :], start=True, stop=True)
                        ins.then_inc(kc_ps, 1)
                        pe.wait_ge(bg_lo, l + 1)
                        for t in range(TOK):
                            ts = slice(t * P, t * P + P)
                            for c in range(KC):
                                ins = three(ps[:, MB + 1, 24 * t:24 * t + 24], (h_hi[:, c, ts], h_lo[:, c, ts]),
                                            (g_hi[:, c, :], g_lo[:, c, :]), c == 0, c == KC - 1)
                        ins.then_inc(bg_ps, 1)
                    if v == 7:
                        pe.wait_ge(kc_ready, l * 2 + 2)
                        pe.wait_ge(bg_exp, l + 1)
                        pe.wait_ge(q_out_act, l * 10 + 4)
                        for h in range(HEADS):
                            g, po = h // HPG, DH * (h % 2)
                            for t in range(TOK):
                                r = (g * TOK + t) * 2 + h % 4 // 2
                                ins = pe.matmul(ps[:, MB + 1 - h % 2, r * 32:r * 32 + NCMP], bq[po:po + DH, h // 2, t * P:t * P + P],
                                                kc_t[po:po + DH, g, :], start=True, stop=True)
                        ins.then_inc(cs_ps, 1)
                    if v == 8:
                        pe.wait_ge(cp_ready, l + 1)
                        for i in range(4):
                            ins = pe.transpose(ps[:, MB + 1, i * P:i * P + P],
                                               cmp_p[:, 4 * i:4 * i + 4, :].rearrange("p a b -> p (a b)"), ident[:, :])
                        ins.then_inc(cpt_ps, 1)
                    if v >= 3 and v <= 26:
                        jobs(l, v)
                    if v == 31:
                        pe.wait_ge(br_read, l * 12 + 12)
                        for q in range(4):
                            for c in (2 * q, 2 * q + 1):
                                for t in range(TOK):
                                    ins = pe.transpose(ps[:, SB + q, (c % 2) * S + t * P:(c % 2) * S + t * P + P],
                                                       merged[:, t, c * P:c * P + P], ident[:, :])
                            ins.then_inc(m_ps, 1)
                gate_rows_out(l, 1)
                h_columns(l, 2)
                ffn(l, 1)
                gate_rows_out(l, 2)
                with pe.If(l < DEPTH - 1):
                    pe.wait_ge(ada_sums, ada_before(l, 2, 1) + SUMS_AHEAD)
                    columns(0, 0, ada_acc).then_inc(modps_done, 1)
                    gate_row(0, l * 3 + 4)


def constants():
    import numpy as np

    p = np.arange(P)
    out = {"k_ident": np.eye(P), "k_flip": np.eye(P)[::-1]}
    out["k_negtri"] = -(p[:, None] >= p[None, :]).astype(np.float32)
    before = (p[:, None] < p[None, :]).astype(np.float32)
    one = np.ones((P, P), np.float32)
    out["k_causal01"] = np.concatenate([before, one, before], 1)
    out["k_causalneg"] = np.where(out["k_causal01"] > 0, 0.0, NEG)
    t = p[:, None, None] + P * np.arange(TOK)[None, :, None]
    ok = np.arange(NCMP)[None, None, :] * CMP_STRIDE + CMP_BLOCK - 1 <= t
    out["k_cmp01"] = ok.astype(np.float32)
    out["k_cmpneg"] = np.where(ok, 0.0, NEG)
    dist = 255 - np.arange(384)
    d = np.maximum(dist, 0)
    ratio = np.log(np.maximum(d, 1).astype(np.float32) / np.float32(16)) / np.float32(np.log(128 / 16))
    big = np.minimum(16 + (ratio * np.float32(16)).astype(np.int32), 31)
    bucket = np.where(d < 16, d, big)
    k = np.zeros((33, 2, 512), np.float32)
    for i, ok in enumerate(((dist >= 0) & (dist < 128), dist >= 0)):
        k[bucket[ok], i, np.nonzero(ok)[0]] = 1.0
        k[32, i, 0:384] = np.where(ok, 0.0, NEG)
    out["k_buckets"] = k.reshape(33, 1024)
    return {n: np.ascontiguousarray(a.astype(np.float32)) for n, a in out.items()}


def kernel(x, c, rel_bias, ada_w, ada_b, ln_pre, ln_post, ffn_w_gate, ffn_w_up, ffn_w_down,
           w_in, attn_sinks, cmp_pos, cmp_w1, cmp_w2, w_branch, w_out):
    import numpy as np
    import concourse.bacc as bacc
    from concourse.bass_utils import run_bass_kernel_spmd

    given = dict(x=x, c=c, rel_bias=rel_bias, ada_w=ada_w, ada_b=ada_b, ln_pre=ln_pre, ln_post=ln_post,
                 ffn_w_gate=ffn_w_gate, ffn_w_up=ffn_w_up, ffn_w_down=ffn_w_down, w_in=w_in,
                 attn_sinks=attn_sinks, cmp_pos=cmp_pos, cmp_w1=cmp_w1, cmp_w2=cmp_w2,
                 w_branch=w_branch, w_out=w_out)
    nc = bacc.Bacc("TRN2", target_bir_lowering=False, num_devices=1)
    arrays, A = {}, {}
    for name, a in {**given, **constants()}.items():
        a = np.ascontiguousarray(a)
        arrays["in_" + name] = a
        A[name] = nc.dram_tensor("in_" + name, a.shape, mybir.dt.from_np(a.dtype), kind="ExternalInput").ap()
    A["scratch"] = nc.dram_tensor("bias_scratch", (2, 8, 384), F32, kind="Internal").ap()
    out = nc.dram_tensor("out", (1, S, D), F32, kind="ExternalOutput").ap()
    trunk_program(nc, A, out)
    return run_bass_kernel_spmd(nc, [arrays], core_ids=[0]).results[0]["out"]
```

```python
from contextlib import ExitStack

import concourse.bass as bass
from concourse import mybir

F32 = mybir.dt.float32
F32R = mybir.dt.float32r
ACT = mybir.ActivationFunctionType
ALU = mybir.AluOpType
AX = mybir.AxisListType

P = 128
D = 1024
S = 256
DEPTH = 2
DH = 64
HEADS = 8
HPG = 4
FF = 2816
NSUB = 3
CMP_BLOCK = 32
CMP_STRIDE = 16
NCMP = (S - CMP_BLOCK) // CMP_STRIDE + 1
IN_WIDTH = 6680
EPS = 1e-6
NEG = -1e30
KC = D // P
TOK = S // P

RING = 3
UNIT = 2048
LOADS = 2
FB = 256
FSTEPS = FF // FB
FFN_UNITS = 3 * FSTEPS
SUMS_AHEAD = 8
ADA_STEPS = 8
QKV_UNITS = 14
MIX_UNITS = QKV_UNITS + 3 * 6 + 4
LAYER_UNITS = 2 * FFN_UNITS + MIX_UNITS
GATE_COL = 2048
MERGE_COL = 3608
MOD = 3 * D
HALF = MOD // 2

JOBS = ([("a", h) for h in range(HEADS)]
        + [(k, h) for h in range(HEADS) for k in ("slc", "win")]
        + [("c", h) for h in range(HEADS)])
NJ = len(JOBS)


def job_slots(step):
    if 3 <= step <= 6:
        first = 2 * (step - 3)
    elif 9 <= step <= 16:
        first = HEADS + 2 * (step - 9)
    elif 19 <= step <= 23:
        first = 3 * HEADS + 2 * (step - 19)
    else:
        return range(0)
    return range(first, first + 2)


def pair_done(n):
    kind, h = JOBS[n]
    if h % 2 == 0 or kind == "slc":
        return None
    return {"a": 0, "win": 4, "c": 8}[kind] + h // 2


def trunk_program(nc, A, out):
    ctx = ExitStack()
    with ctx:
        def sb(name, shape, dt=F32):
            return ctx.enter_context(nc.sbuf_tensor(name, shape, dt))

        def sem(name):
            return ctx.enter_context(nc.semaphore(name))

        x = sb("x", [P, TOK, D])
        h_hi = sb("h_hi", [P, KC, S], F32R)
        h_lo = sb("h_lo", [P, KC, S], F32R)
        w_raw = sb("w_raw", [P, RING, UNIT])
        w_hi = sb("w_hi", [P, RING, UNIT], F32R)
        w_lo = sb("w_lo", [P, RING, UNIT], F32R)
        act_hi = sb("act_hi", [P, 2, 4, S], F32R)
        act_lo = sb("act_lo", [P, 2, 4, S], F32R)
        g_raw = sb("g_raw", [P, KC, 24])
        g_hi = sb("g_hi", [P, KC, 24], F32R)
        g_lo = sb("g_lo", [P, KC, 24], F32R)
        bias = sb("bias", [P, 2 * HEADS, 2 * P])
        ident = sb("ident", [P, P])
        neg_tri = sb("neg_tri", [P, P])
        neg_ones = sb("neg_ones", [P, P])
        ones = sb("ones", [P, 1])
        causal01 = sb("causal01", [P, 3 * P])
        causal_neg = sb("causal_neg", [P, 3 * P])
        cmp_neg = sb("cmp_neg", [P, TOK, NCMP])
        cmp_01 = sb("cmp_01", [P, TOK, NCMP])
        ln_t = sb("ln_t", [P, 2, DEPTH * NSUB * KC])
        adab_t = sb("adab_t", [P, DEPTH * NSUB * 24])
        pos_t = sb("pos_t", [DH, DEPTH, 2 * CMP_BLOCK])
        c_act = sb("c_act", [P, KC])
        sink = sb("sink", [P, DEPTH, HEADS])
        eps_t = sb("eps_t", [P, 1])
        modc = sb("modc", [P, NSUB, 24])
        mod_a = sb("mod_a", [P, NSUB, KC])
        mod_g = sb("mod_g", [P, NSUB, KC])
        gt = sb("gt", [KC, NSUB, P])
        stat = sb("stat", [P, 16])
        w2k = sb("w2k", [P, 2, DH])
        w2v = sb("w2v", [P, DH])
        hid = sb("hid", [P, 2, 2, NCMP])
        hid_v = sb("hid_v", [P, 2, 4, 32])
        kc_t = sb("kc_t", [P, 2, NCMP])
        vc = sb("vc", [P, 2, DH])
        egate = sb("egate", [P, TOK, 24])
        bgate = egate
        cmp_p = sb("cmp_p", [P, 2 * TOK * 4, 32])
        cmp_pt = sb("cmp_pt", [P, 2, TOK, P])
        cst = sb("cst", [P, 3, 16])
        jst = sb("jst", [P, 2, 12])

        AR = 15872
        arena = sb("arena", [P, AR])

        def region(at, *shape, parts=P):
            n = 1
            for d_ in shape:
                n *= d_
            v = arena[0:parts, at:at + n]
            if len(shape) == 2:
                return v.rearrange("p (a b) -> p a b", b=shape[1])
            if len(shape) == 3:
                return v.rearrange("p (a b c) -> p a b c", b=shape[1], c=shape[2])
            return v

        ada_acc = region(0, 2 * MOD)
        ada_raw = region(2 * MOD, 4, D)
        ffn_a = region(12288, TOK, FB)
        ffn_s = region(12800, TOK, FB)
        SCR = AR - 2048
        xs = region(SCR, TOK, D)
        gate_sb = region(12288, 2, 512)
        w1 = region(0, 2, 16, P)
        mg = region(0, TOK, 512)
        hbuf = region(10240, KC, S)
        junk = region(11264, D)
        o_ = 4096
        aq = region(o_, 4, S); o_ += 1024
        ak = region(o_, 2, S); o_ += 512
        bq = region(o_, 4, S); o_ += 1024
        bks = region(o_, 2, S); o_ += 512
        bkw = region(o_, 2, S); o_ += 512
        cq = region(o_, 4, S); o_ += 1024
        ck = region(o_, 4, S); o_ += 1024
        av = region(o_, TOK, P); o_ += 256
        bvs = region(o_, TOK, P); o_ += 256
        bvw = region(o_, TOK, P); o_ += 256
        cv = region(o_, TOK, 512); o_ += 1024
        job_s = region(o_, 2, 3 * P); o_ += 768
        job_p = region(o_, 2, 3 * P); o_ += 768
        job_t = region(o_, 2, 3 * P); o_ += 768
        assert o_ <= SCR
        kvin = region(SCR, 2, 2, S, parts=DH)
        zc = region(SCR + 1024, 2, 16, 2 * NCMP)
        merged = region(SCR, TOK, D)

        ps = ctx.enter_context(nc.psum_tensor("ps", [P, 8, 512], F32))
        GU, TB, MODB = 4, 6, 7
        HB = (4, 5, 6, 1)
        QB, MB, SB, MID, OB = 0, 2, 4, 6, 7

        const_in = sem("const_in")
        ident_in = sem("ident_in")
        c_in = sem("c_in")
        flip_in = sem("flip_in")
        setup_in = [sem(f"setup_in{i}") for i in range(4)]
        x_in = sem("x_in")
        raw_full = [sem(f"raw_full{i}") for i in range(RING)]
        hi_ready = sem("hi_ready")
        lo_ready = sem("lo_ready")
        unit_used = sem("unit_used")
        ada_full = [sem(f"ada_full{i}") for i in range(4)]
        ada_half = [sem(f"ada_half{i}") for i in range(2)]
        ada_sums = sem("ada_sums")
        ada_done = sem("ada_done")
        modps_done = sem("modps_done")
        modc_ready = sem("modc_ready")
        ada_gate = [sem(f"ada_gate{i}") for i in range(4)]
        setup_act = sem("setup_act")
        y_half = sem("y_half")
        mod_ready = sem("mod_ready")
        gt_ps = sem("gt_ps")
        gt_ready = sem("gt_ready")
        h_ps = sem("h_ps")
        h32_ready = sem("h32_ready")
        hhi_ready = sem("hhi_ready")
        hlo_ready = sem("hlo_ready")
        xsq_done = sem("xsq_done")
        xrms_done = sem("xrms_done")
        xs_ready = sem("xs_ready")
        x_done = sem("x_done")
        g_ps = sem("g_ps")
        ysq_done = sem("ysq_done")
        yrms_done = sem("yrms_done")
        gu_done = sem("gu_done")
        silu_done = sem("silu_done")
        act_done = sem("act_done")
        at_ps = sem("at_ps")
        ahi_ready = sem("ahi_ready")
        alo_ready = sem("alo_ready")
        q_out_act = sem("q_out_act")
        q_out_dve = sem("q_out_dve")
        bg_in = sem("bg_in")
        bg_hi = sem("bg_hi")
        bg_lo = sem("bg_lo")
        bg_ps = sem("bg_ps")
        bg_exp = sem("bg_exp")
        bg_ready = sem("bg_ready")
        w1_in = sem("w1_in")
        z_ready = sem("z_ready")
        hid_ps = sem("hid_ps")
        hid_ready = sem("hid_ready")
        kc_ps = sem("kc_ps")
        kc_ready = sem("kc_ready")
        cs_ps = sem("cs_ps")
        cs_ready = sem("cs_ready")
        cexp_done = sem("cexp_done")
        cp_ready = sem("cp_ready")
        cpt_ps = sem("cpt_ps")
        cpt_ready = sem("cpt_ready")
        sc_done = sem("sc_done")
        s_read = sem("s_read")
        s_ready = sem("s_ready")
        front_done = sem("front_done")
        p_ready = sem("p_ready")
        mid_done = sem("mid_done")
        mask_done = sem("mask_done")
        pt_ready = sem("pt_ready")
        pv_done = sem("pv_done")
        y_hi = sem("y_hi")
        y_lo = sem("y_lo")
        mg_ps = sem("mg_ps")
        mg_ready = sem("mg_ready")
        br_ps = sem("br_ps")
        br_read = sem("br_read")
        m_ready = sem("m_ready")
        m_ps = sem("m_ps")
        mhi_ready = sem("mhi_ready")
        mlo_ready = sem("mlo_ready")
        act_own = sem("act_own")
        dve_own = sem("dve_own")
        setup_pe = sem("setup_pe")
        setup_dve = sem("setup_dve")
        scratch_out = sem("scratch_out")
        out_sem = sem("out_sem")

        def branch_in(i, c, ts=slice(0, S)):
            return act_hi[:, i % 2, c, ts], act_lo[:, i % 2, c, ts]

        def branch_out(it, t):
            return ps[:, (SB if it == 5 else QB) + t, :]

        OWN = 512

        class Own:

            def __init__(self, eng, s):
                self.eng, self.s, self.n, self.base = eng, s, 0, 0

            def end(self):
                assert self.n < OWN
                self.eng.sem_inc(self.s, OWN - self.n)

            def done(self, ins):
                ins.then_inc(self.s, 1)
                self.n += 1
                self.eng.wait_ge(self.s, self.base + self.n)

        block = ctx.enter_context(nc.Block())

        def used(l, k):
            return l * LAYER_UNITS + k + RING + 1

        def unit_of(l, k):
            return l * LAYER_UNITS + k

        def ada_width(f):
            return (2 if f == 0 else 1) * MOD // ADA_STEPS

        def ada_view(f, half):
            w = ada_width(f)
            at = 2 * MOD + half * 4 * w
            return arena[:, at:at + 4 * w].rearrange("p (c n) -> p c n", n=w)

        def ada_before(l, f, j):
            return (l * 2 + f) * KC * ADA_STEPS + (j - 1) * KC

        def unit_parts(k, l, j):
            slot = k % RING
            r = w_raw[:, slot, :]
            f, q = (0, k) if k < FFN_UNITS else (1, k - FFN_UNITS - MIX_UNITS)
            if 0 <= q < FFN_UNITS:
                kind, j = j
                if kind == "D":
                    rows = A["ffn_w_down"][l, f, bass.ds(j * FB, FB), :].rearrange("(c p) n -> p c n", p=P)
                    v = r.rearrange("p (c n) -> p c n", n=D)
                    return [(v[:, c], rows[:, c]) for c in range(2)]
                v = r.rearrange("p (c n) -> p c n", n=2 * FB)
                k0 = 0 if kind == "GA" else 4 * P
                return [(v[:, :, i * FB:(i + 1) * FB],
                         A[w][l, f, k0:k0 + 4 * P, bass.ds(j * FB, FB)].rearrange("(c p) n -> p c n", p=P))
                        for i, w in enumerate(("ffn_w_gate", "ffn_w_up"))]
            v_ = k - FFN_UNITS
            if v_ < QKV_UNITS:
                col = 256 * v_ if v_ < 8 else GATE_COL + 24 + 256 * (v_ - 8)
                v = r.rearrange("p (c n) -> p c n", n=256)
                src = A["w_in"][l, :, col:col + 256].rearrange("(c p) n -> p c n", p=P)
                return [(v[:, 4 * i:4 * i + 4], src[:, 4 * i:4 * i + 4]) for i in range(2)]
            v_ -= QKV_UNITS
            if v_ < 18:
                i, half, part = v_ // 6, v_ // 3 % 2, v_ % 3
                v = r.rearrange("p (c n) -> p c n", n=512)
                if part < 2:
                    c0 = MERGE_COL + i * D + half * 512
                    src = A["w_in"][l, part * 512:part * 512 + 512, c0:c0 + 512]
                else:
                    src = A["w_branch"][l, i, :, half * 512:half * 512 + 512]
                src = src.rearrange("(c p) n -> p c n", p=P)
                return [(v[:, 2 * e:2 * e + 2], src[:, 2 * e:2 * e + 2]) for e in range(2)]
            v_ -= 18
            rows = A["w_out"][l, v_ * 256:v_ * 256 + 256, :].rearrange("(c p) n -> p c n", p=P)
            v = r.rearrange("p (c n) -> p c n", n=D)
            return [(v[:, c], rows[:, c]) for c in range(2)]

        @block.sync
        def _(sp):
            sp.dma_start(ident[:, :], A["k_ident"]).then_inc(ident_in, 16)
            sp.dma_start(arena[0:KC, 12288:12288 + P], A["c"].rearrange("b (c p) -> (b c) p", p=P)).then_inc(c_in, 16)
            sp.dma_start(w_raw[0:33, 0, 0:1024], A["k_buckets"]).then_inc(setup_in[1], 16)
            sp.dma_start(w_raw[0:32, 0, 1024:1040], A["rel_bias"]).then_inc(setup_in[1], 16)

            def first_modulation(n):
                if n >= 4:
                    sp.wait_ge(ada_done, n - 3)
                b, k = n // KC, n % KC
                sp.dma_start(ada_raw[:, n % 4, :],
                             A["ada_w"][0, k * P:k * P + P, b * D:b * D + D]).then_inc(ada_full[n % 4], 16)

            for n in range(4):
                first_modulation(n)
            sp.dma_start(arena[0:48, 12416:12416 + P],
                         A["ln_pre"].rearrange("l s (c p) -> (l s c) p", p=P)).then_inc(setup_in[0], 16)
            sp.dma_start(arena[0:48, 12544:12544 + P],
                         A["ln_post"].rearrange("l s (c p) -> (l s c) p", p=P)).then_inc(setup_in[0], 16)
            sp.dma_start(arena[0:72, 12672:12672 + 2 * P].rearrange("r (l p) -> r l p", p=P),
                         A["ada_b"].rearrange("l (r p) -> r l p", p=P)).then_inc(setup_in[0], 16)
            sp.dma_start(arena[0:DH, 12928:12928 + 2 * DH].rearrange("r (l d) -> r l d", d=DH),
                         A["cmp_pos"].rearrange("l k j d -> (k j) l d")).then_inc(setup_in[0], 16)
            sp.dma_start(w_raw[:, 0, 1536:1536 + P], A["k_flip"]).then_inc(flip_in, 16)
            sp.wait_ge(setup_dve, 3)
            sp.dma_start(A["scratch"][:, :, :].rearrange("a h n -> h a n"),
                         w_raw[0:8, 1, 0:1024].rearrange("h (a n) -> h a n", n=512)[:, :, 0:384]).then_inc(scratch_out, 16)
            for n in range(4, 8):
                first_modulation(n)
            sp.wait_ge(scratch_out, 16)
            sc = A["scratch"]
            for i in range(2):
                sp.dma_start(w_raw[:, 1 + i, :].rearrange("p (h n) -> p h n", n=256),
                             bass.AP(tensor=sc.tensor, offset=i * 8 * 384, ap=[[1, P], [384, 8], [1, 256]])).then_inc(setup_in[2], 16)
            sp.dma_start(x[:, :, :], A["x"][0].rearrange("(t p) d -> p t d", p=P)).then_inc(x_in, 16)
            for n in range(8, 16):
                first_modulation(n)
            for dst, src in ((neg_tri, "k_negtri"), (causal01, "k_causal01"), (causal_neg, "k_causalneg")):
                sp.dma_start(dst[:, :], A[src]).then_inc(const_in, 16)
            sp.dma_start(cmp_neg[:, :, :], A["k_cmpneg"]).then_inc(const_in, 16)
            sp.dma_start(cmp_01[:, :, :], A["k_cmp01"]).then_inc(const_in, 16)
            sp.dma_start(sink[:, :, :].rearrange("p l h -> p (l h)"),
                         A["attn_sinks"].rearrange("l h -> (l h)").unsqueeze(0).to_broadcast([P, DEPTH * HEADS])).then_inc(const_in, 16)
            sp.wait_ge(setup_pe, 12)

            def load(l, k, j=None):
                sp.wait_ge(lo_ready, unit_of(l, k) + 1)
                for dst, src in unit_parts(k, l, j):
                    sp.dma_start(dst, src).then_inc(raw_full[k % RING], 16)

            def ffn(l, f):
                k0 = f * (FFN_UNITS + MIX_UNITS)
                load(l, k0, ("GA", 0))
                load(l, k0 + 1, ("GB", 0))

                def step(j, ada):
                    for i, kind in enumerate(("GA", "GB", "D")):
                        sp.wait_ge(lo_ready, unit_of(l, k0 + i) + j * 3)
                        for dst, src in unit_parts(k0 + 2 + i, l, (kind, j - 1 if kind == "D" else j)):
                            sp.dma_start(dst, src).then_inc(raw_full[(k0 + 2 + i) % RING], 16)
                        if i < 2 and ada:
                            if f == 0:
                                ada_load(j - 1, i)
                            else:
                                with sp.If(l < DEPTH - 1):
                                    ada_load(j - 1, i)

                def ada_load(j, half):
                    w = ada_width(f)
                    lw, col = (l, MOD) if f == 0 else ((l + 1) % DEPTH, 0)
                    sp.wait_ge(ada_sums, ada_before(l, f, j) + 4 * half - 4 + SUMS_AHEAD)
                    sp.dma_start(ada_view(f, half),
                                 A["ada_w"][lw, 4 * P * half:4 * P * half + 4 * P, bass.ds(col + (j - 1) * w, w)]
                                 .rearrange("(c p) n -> p c n", p=P)).then_inc(ada_half[half], 16)

                step(1, False)
                sp.wait_ge(ada_done, 24)
                with sp.Fori(2, ADA_STEPS + 2) as j:
                    step(j, True)
                with sp.Fori(ADA_STEPS + 2, FSTEPS) as j:
                    step(j, False)
                load(l, k0 + FFN_UNITS - 1, ("D", FSTEPS - 1))

            with sp.Fori(0, DEPTH) as l:
                ffn(l, 0)
                for v in range(MIX_UNITS):
                    if v == 3:
                        sp.wait_ge(modps_done, l * 6 + 6)
                        for e in range(2):
                            rows = A["cmp_w1"][l, e].rearrange("(c p) h -> p c h", p=P)
                            for half in range(2):
                                cs = slice(8 * half, 8 * half + 8)
                                sp.dma_start(w1[:, e, cs], rows[:, cs]).then_inc(w1_in, 16)
                        for e in range(2):
                            sp.dma_start(w2k[:, e, :], A["cmp_w2"][l, 0]).then_inc(w1_in, 16)
                        sp.dma_start(w2v[:, :], A["cmp_w2"][l, 1]).then_inc(w1_in, 16)
                        sp.dma_start(g_raw[:, :, :], A["w_in"][l, :, GATE_COL:GATE_COL + 24].rearrange("(c p) n -> p c n", p=P)).then_inc(bg_in, 16)
                    load(l, FFN_UNITS + v)
                ffn(l, 1)
            sp.wait_ge(x_done, DEPTH * NSUB * TOK + TOK)
            sp.dma_start(out[0].rearrange("(t p) d -> p t d", p=P), x[:, :, :]).then_inc(out_sem, 16)
            sp.wait_ge(out_sem, 16)

        @block.gpsimd
        def _(pool):
            pool.memset(ones[:, :], 1.0).then_inc(setup_in[3], 1)
            pool.memset(neg_ones[:, :], -1.0).then_inc(setup_in[3], 1)
            pool.memset(eps_t[:, :], EPS).then_inc(setup_in[3], 1)
            pool.memset(hid_v[:, :, :, :], 0.0).then_inc(setup_in[3], 1)
            pool.memset(cmp_p[:, :, :], 0.0).then_inc(setup_in[3], 1)
            for n in range(16, 24):
                pool.wait_ge(ada_done, n - 3)
                k = n % KC
                pool.dma_start(ada_raw[:, n % 4, :], A["ada_w"][0, k * P:k * P + P, 2 * D:3 * D]).then_inc(ada_gate[n % 4], 16)

        @block.scalar
        def _(act):
            own = Own(act, act_own)

            def hi_parts(l, k):
                u = unit_of(l, k)
                act.wait_ge(raw_full[k % RING], l * (16 * LOADS * LAYER_UNITS // RING) + 16 * LOADS * (k // RING + 1) )
                act.wait_ge(unit_used, u + 1)
                act.activation(w_hi[:, k % RING, :], w_raw[:, k % RING, :], ACT.Copy).then_inc(hi_ready, 1)

            def rms_of_x(l, s):
                for t in range(TOK):
                    act.wait_ge(x_done, l * 6 + 2 * s + t + 1)
                    own.done(act.activation(junk, x[:, t, :], ACT.Square, accum_out=stat[:, t:t + 1]))
                    act.activation(stat[:, 2 + t:3 + t], stat[:, t:t + 1], ACT.Sqrt, scale=1.0 / D,
                                   bias=eps_t[:, 0:1]).then_inc(xrms_done, 1)

            def split_h(l, s):
                for q in range(4):
                    act.wait_ge(h32_ready, (l * NSUB + s) * 4 + q + 1)
                    act.activation(h_hi[:, 2 * q:2 * q + 2, :], hbuf[:, 2 * q:2 * q + 2, :], ACT.Copy).then_inc(hhi_ready, 1)

            def rms_of_y(l, s):
                own.done(act.activation(jst[:, 0, 11:12], eps_t[:, 0:1], ACT.Sqrt))
                for t in range(TOK):
                    if t == 0:
                        act.wait_ge(y_half, l * NSUB + s + 1)
                    else:
                        act.wait_ge(unit_used, used(l, (FFN_UNITS, FFN_UNITS + MIX_UNITS, LAYER_UNITS)[s] - 1))
                    own.done(act.activation(junk.rearrange("p (a b) -> p a b", b=512), ps[:, 2 * t:2 * t + 2, :],
                                            ACT.Square, accum_out=stat[:, 4 + t:5 + t]))
                    act.activation(stat[:, 6 + t:7 + t], stat[:, 4 + t:5 + t], ACT.Sqrt, scale=1.0 / D,
                                   bias=eps_t[:, 0:1]).then_inc(yrms_done, 1)

            def ffn(l, f):
                k0 = f * (FFN_UNITS + MIX_UNITS)

                def step(j, end, units):
                    n = (l * 2 + f) * FSTEPS
                    for t in range(TOK):
                        if t == 0:
                            act.wait_ge(gu_done, n + j + 1)
                        else:
                            act.wait_ge(unit_used, used(l, k0) + end)
                        act.activation(ffn_s[:, t, :], ps[:, GU + t, 0:FB], ACT.Silu).then_inc(silu_done, 1)
                    units(0)
                    units(1)
                    act.wait_ge(at_ps, n + j + 1)
                    act.activation(act_hi[:, 0, 0:2, :], ps[:, TB, :].rearrange("p (a b) -> p a b", b=S),
                                   ACT.Copy).then_inc(ahi_ready, 1)
                    units(2)

                step(0, 1, lambda i: hi_parts(l, k0 + 3 + i))
                with act.Fori(1, FSTEPS - 1) as j:
                    def units(i):
                        k = k0 + 3 + i
                        act.wait_ge(raw_full[k % RING], l * (16 * LOADS * LAYER_UNITS // RING) + j * (16 * LOADS) + 16 * LOADS * (k // RING + 1))
                        act.wait_ge(unit_used, unit_of(l, k) + j * 3 + 1)
                        act.activation(w_hi[:, k % RING, :], w_raw[:, k % RING, :], ACT.Copy).then_inc(hi_ready, 1)
                    step(j, 3 * j, units)
                def next_units(i):
                    if f == 0:
                        hi_parts(l, k0 + FFN_UNITS + i)
                    else:
                        with act.If(l < DEPTH - 1):
                            hi_parts(l, LAYER_UNITS + i)

                step(FSTEPS - 1, 3 * FSTEPS - 3, next_units)

            def front(l, n):
                kind, h = JOBS[n]
                b = n % 2
                if kind == "c":
                    act.wait_ge(sc_done, l * NJ + n + 1)
                    if n >= 26:
                        act.wait_ge(p_ready, l * NJ + n - 1)
                    own.done(act.activation(job_s[:, b, :], ps[:, SB + b, 0:3 * P], ACT.Abs))
                    own.done(act.activation(job_s[:, b, :], job_s[:, b, :], ACT.Exp, scale=-1.0))
                    act.activation(job_s[:, b, :], job_s[:, b, :], ACT.Ln, bias=1.0).then_inc(front_done, 1)
                    return
                act.wait_ge(s_ready, l * 24 + n + 1)
                if n >= 2:
                    act.wait_ge(mid_done, l * NJ + n - 1)
                st = jst[:, b, :]
                act.activation(job_p[:, b, 0:P], job_s[:, b, 0:P], ACT.Exp, bias=st[:, 2:3], accum_out=st[:, 4:5])
                if kind == "a":
                    act.activation(st[:, 6:8], st[:, 2:4], ACT.Exp, bias=sink[:, bass.ds(l, 1), h])
                act.activation(job_p[:, b, P:3 * P], job_s[:, b, P:3 * P], ACT.Exp, bias=st[:, 3:4],
                               accum_out=st[:, 5:6]).then_inc(front_done, 1)

            def back(l, n):
                b = n % 2
                if JOBS[n][0] == "c":
                    act.wait_ge(mask_done, l * HEADS + n - 24 + 1)
                    act.activation(job_t[:, b, :], job_t[:, b, :], ACT.Exp).then_inc(pt_ready, 1)
                    return
                act.wait_ge(mid_done, l * NJ + n + 1)
                act.activation(job_t[:, b, :], ps[:, MID, 0:3 * P], ACT.Copy).then_inc(pt_ready, 1)

            def pair_out(l, n):
                q = pair_done(n)
                if q is None:
                    return
                act.wait_ge(pv_done, l * NJ + n + 1)
                act.activation(branch_in(q // 4, q % 4)[0], ps[:, OB, 0:S], ACT.Copy).then_inc(y_hi, 1)

            def jobs(l, step):
                for n in job_slots(step):
                    if 2 <= n:
                        back(l, n - 2)
                    if n < NJ:
                        front(l, n)
                for n in job_slots(step):
                    if 2 <= n:
                        pair_out(l, n - 2)

            act.wait_ge(setup_in[3], 5)
            act.wait_ge(setup_dve, 1)
            act.activation(c_act[:, :], stat[:, 8:16], ACT.Silu).then_inc(setup_in[3], 1)
            for i in range(4):
                act.wait_ge(setup_pe, 9 + i)
                act.activation(bias[:, 4 * i:4 * i + 4, :].rearrange("p a b -> p (a b)").rearrange("p (a b) -> p a b", b=512),
                               ps[:, 4 + 2 * (i % 2):6 + 2 * (i % 2), :], ACT.Copy).then_inc(setup_act, 1)
            act.wait_ge(x_in, 16)
            act.wait_ge(const_in, 6 * 16)
            for k in range(RING):
                hi_parts(0, k)
            with act.Fori(0, DEPTH) as l:
                own.n, own.base = 0, l * OWN
                rms_of_x(l, 0)
                split_h(l, 0)
                ffn(l, 0)
                rms_of_y(l, 0)
                rms_of_x(l, 1)
                split_h(l, 1)
                for v in range(MIX_UNITS):
                    if v < QKV_UNITS:
                        if v not in (2, 5, 6, 7):
                            act.wait_ge(unit_used, used(l, FFN_UNITS + v))
                            bank = ps[:, QB + v % 2, :]
                            if v in (0, 1, 3, 4, 8, 9):
                                dst = {0: aq, 1: aq, 3: bq, 4: bq, 8: cq, 9: cq}[v]
                                b0 = {0: 0, 1: 2, 3: 0, 4: 2, 8: 0, 9: 2}[v]
                                act.activation(dst[:, b0:b0 + 2, :], bank.rearrange("p (a b) -> p a b", b=S),
                                               ACT.Copy, scale=DH ** -0.5).then_inc(q_out_act, 1)
                            elif v in (10, 11):
                                act.activation(ck[:, 2 * (v - 10):2 * (v - 10) + 2, :],
                                               bank.rearrange("p (a b) -> p a b", b=S), ACT.Copy).then_inc(q_out_act, 1)
                            else:
                                act.activation(cv[:, :, 256 * (v - 12):256 * (v - 12) + 256].rearrange("p t (a b) -> p t a b", b=P),
                                               bank.rearrange("p (a t b) -> p t a b", a=2, b=P), ACT.Copy).then_inc(q_out_act, 1)
                    if v == 5:
                        act.wait_ge(bg_in, l * 16 + 16)
                        act.activation(g_hi[:, :, :], g_raw[:, :, :], ACT.Copy).then_inc(bg_hi, 1)
                    if v == 6:
                        act.wait_ge(hid_ps, l + 1)
                        hp = ps[:, MB, 0:4 * NCMP].rearrange("p (k g n) -> p k g n", k=2, g=2)
                        act.activation(hid[:, 0, :, :], hp[:, 0], ACT.Gelu_apprx_tanh).then_inc(hid_ready, 1)
                        act.activation(hid[:, 1, :, :], hp[:, 1], ACT.Gelu_apprx_tanh).then_inc(hid_ready, 1)
                    if v == 7:
                        act.wait_ge(bg_ps, l + 1)
                        act.activation(egate[:, :, :], ps[:, MB + 1, 0:48].rearrange("p (t n) -> p t n", n=24),
                                       ACT.Exp, scale=-1.0).then_inc(bg_exp, 1)
                    if v == 8:
                        act.wait_ge(cs_ready, l + 1)
                        act.activation(cmp_p[:, :, 0:NCMP], cmp_p[:, :, 0:NCMP], ACT.Exp).then_inc(cexp_done, 1)
                    if v == 9:
                        act.wait_ge(cpt_ps, l + 1)
                        act.activation(cmp_pt[:, :, :, :], ps[:, MB + 1, :].rearrange("p (g t q) -> p g t q", g=2, t=2),
                                       ACT.Copy).then_inc(cpt_ready, 1)
                    if 14 <= v < 32 and (v - 14) % 3 == 1:
                        it = (v - 14) // 3
                        for t in range(TOK):
                            if t == 0:
                                act.wait_ge(mg_ps, l * 6 + it + 1)
                            else:
                                act.wait_ge(unit_used, used(l, FFN_UNITS + v))
                            if it:
                                act.wait_ge(br_read, (l * 6 + it) * 2)
                            act.activation(mg[:, t, :], ps[:, MB + t, :], ACT.Sigmoid).then_inc(mg_ready, 1)
                    jobs(l, v)
                    if v in (30, 32):
                        for q in range(2):
                            act.wait_ge(m_ps, l * 4 + (v - 30) + q + 1)
                            dst = act_hi[:, 1, 2 * q:2 * q + 2, :] if v == 30 else h_hi[:, 4 + 2 * q:6 + 2 * q, :]
                            act.activation(dst, ps[:, MID + q, :].rearrange("p (a b) -> p a b", b=S),
                                           ACT.Copy).then_inc(mhi_ready, 1)
                    hi_parts(l, FFN_UNITS + v + 3)
                rms_of_y(l, 1)
                rms_of_x(l, 2)
                split_h(l, 2)
                ffn(l, 1)
                rms_of_y(l, 2)
                own.end()

        @block.vector
        def _(dve):
            own = Own(dve, dve_own)

            def lo_parts(l, k):
                u = unit_of(l, k)
                dve.wait_ge(hi_ready, u + 1)
                dve.tensor_tensor(w_lo[:, k % RING, :], w_raw[:, k % RING, :], w_hi[:, k % RING, :].bitcast(F32),
                                  ALU.subtract).then_inc(lo_ready, 1)

            def modulate(l, s, n, lw=None):
                lw = l if lw is None else lw
                dve.wait_ge(modps_done, 2 * n - 1)
                c0 = (lw * NSUB + s) * 24
                ins = dve.tensor_tensor(modc[:, s, 0:16], ps[:, MODB, s * 32:s * 32 + 16], adab_t[:, bass.ds(c0, 16)], ALU.add)
                ins.then_inc(modc_ready, 1)
                dve.wait_ge(modc_ready, n)
                g0 = (lw * NSUB + s) * KC
                own.done(dve.scalar_tensor_tensor(out=mod_a[:, s, :], in0=modc[:, s, KC:2 * KC], scalar=1.0,
                                                  in1=ln_t[:, 0, bass.ds(g0, KC)], op0=ALU.add, op1=ALU.mult))

            def modulate_gate(l, s, n, lw=None):
                lw = l if lw is None else lw
                dve.wait_ge(modps_done, 2 * n)
                c0 = (lw * NSUB + s) * 24 + 16
                own.done(dve.tensor_tensor(modc[:, s, 16:24], ps[:, MODB, s * 32 + 16:s * 32 + 24], adab_t[:, bass.ds(c0, 8)], ALU.add))
                g0 = (lw * NSUB + s) * KC
                dve.scalar_tensor_tensor(out=mod_g[:, s, :], in0=modc[:, s, 16:24],
                                         scalar=1.0 if s == 1 else 0.5,
                                         in1=ln_t[:, 1, bass.ds(g0, KC)], op0=ALU.mult, op1=ALU.mult).then_inc(mod_ready, 1)

            def gate_turned(s, n):
                dve.wait_ge(gt_ps, n)
                dve.tensor_copy(gt[:, s, :], ps[0:KC, MODB, 128:256]).then_inc(gt_ready, 1)

            def scale_x(l, s):
                for t in range(TOK):
                    dve.wait_ge(xrms_done, (l * NSUB + s) * 2 + t + 1)
                    own.done(dve.reciprocal(stat[:, t:t + 1], stat[:, 2 + t:3 + t]))
                    dve.tensor_scalar(out=xs[:, t, :], in0=x[:, t, :], scalar1=stat[:, t:t + 1], scalar2=None,
                                      op0=ALU.mult).then_inc(xs_ready, 1)

            def norm_h(l, s):
                for q in range(4):
                    dve.wait_ge(h_ps, (l * NSUB + s) * 4 + q + 1)
                    for c in (2 * q, 2 * q + 1):
                        ins = dve.tensor_scalar(out=hbuf[:, c, :], in0=ps[:, HB[q], (c % 2) * S:(c % 2) * S + S],
                                                scalar1=mod_a[:, s, c:c + 1], scalar2=modc[:, s, c:c + 1],
                                                op0=ALU.mult, op1=ALU.add)
                    ins.then_inc(h32_ready, 1)
                    if q >= 1:
                        low_h(l, s, q - 1)
                low_h(l, s, 3)

            def low_h(l, s, q):
                dve.wait_ge(hhi_ready, (l * NSUB + s) * 4 + q + 1)
                dve.tensor_tensor(h_lo[:, 2 * q:2 * q + 2, :], hbuf[:, 2 * q:2 * q + 2, :],
                                  h_hi[:, 2 * q:2 * q + 2, :].bitcast(F32), ALU.subtract).then_inc(hlo_ready, 1)

            def gate_copy(l, s):
                dve.wait_ge(g_ps, l * NSUB + s + 1)
                own.done(dve.tensor_copy(gate_sb, ps[:, GU:GU + 2, :]))

            def residual(l, s):
                for t in range(TOK):
                    dve.wait_ge(yrms_done, (l * NSUB + s) * 2 + t + 1)
                    own.done(dve.reciprocal(stat[:, 4 + t:5 + t], stat[:, 6 + t:7 + t]))
                    own.done(dve.scalar_tensor_tensor(out=xs[:, t, :].rearrange("p (a b) -> p a b", b=512),
                                                      in0=ps[:, 2 * t:2 * t + 2, :], scalar=stat[:, 4 + t:5 + t],
                                                      in1=gate_sb, op0=ALU.mult, op1=ALU.mult))
                    dve.tensor_tensor(x[:, t, :], x[:, t, :], xs[:, t, :], ALU.add).then_inc(x_done, 1)

            def ffn(l, f):
                k0 = f * (FFN_UNITS + MIX_UNITS)

                def step(j, units, sums=lambda pair: None):
                    n = (l * 2 + f) * FSTEPS
                    for t in range(TOK):
                        dve.wait_ge(silu_done, n * 2 + j * 2 + t + 1)
                        dve.tensor_tensor(ffn_a[:, t, :], ffn_s[:, t, :], ps[:, GU + t, FB:2 * FB], ALU.mult).then_inc(act_done, 1)
                    sums(0)
                    units(0)
                    sums(1)
                    units(1)
                    dve.wait_ge(ahi_ready, n + j + 1)
                    dve.tensor_tensor(act_lo[:, 0, 0:2, :], ps[:, TB, :].rearrange("p (a b) -> p a b", b=S),
                                      act_hi[:, 0, 0:2, :].bitcast(F32), ALU.subtract).then_inc(alo_ready, 1)
                    sums(2)
                    units(2)
                    sums(3)

                step(0, lambda i: lo_parts(l, k0 + 3 + i))

                def loop_step(j, ada):
                    def units(i):
                        k = k0 + 3 + i
                        dve.wait_ge(hi_ready, unit_of(l, k) + j * 3 + 1)
                        dve.tensor_tensor(w_lo[:, k % RING, :], w_raw[:, k % RING, :], w_hi[:, k % RING, :].bitcast(F32),
                                          ALU.subtract).then_inc(lo_ready, 1)

                    def sums(pair):
                        if ada and f == 0:
                            ada_sum(j, pair)
                        elif ada:
                            with dve.If(l < DEPTH - 1):
                                ada_sum(j, pair)
                    step(j, units, sums)

                def ada_sum(j, pair):
                    w = ada_width(f)
                    acc = ada_acc[:, bass.ds((j - 1) * w, w)]
                    half = pair // 2
                    src = ada_view(f, half)
                    if pair % 2 == 0:
                        dve.wait_ge(ada_half[half], ((l * 2 + f) * ADA_STEPS + j) * 16)
                    for c in (2 * (pair % 2), 2 * (pair % 2) + 1):
                        k = 4 * half + c
                        if k == 0:
                            ins = dve.tensor_scalar(out=acc, in0=src[:, c], scalar1=c_act[:, k:k + 1], scalar2=None, op0=ALU.mult)
                        else:
                            dve.wait_ge(ada_sums, ada_before(l, f, j) + k + SUMS_AHEAD)
                            ins = dve.scalar_tensor_tensor(out=acc, in0=src[:, c], scalar=c_act[:, k:k + 1], in1=acc,
                                                           op0=ALU.mult, op1=ALU.add)
                        ins.then_inc(ada_sums, 1)

                with dve.Fori(1, ADA_STEPS + 1) as j:
                    loop_step(j, True)
                with dve.Fori(ADA_STEPS + 1, FSTEPS - 1) as j:
                    loop_step(j, False)
                def next_units(i):
                    if f == 0:
                        lo_parts(l, k0 + FFN_UNITS + i)
                    else:
                        with dve.If(l < DEPTH - 1):
                            lo_parts(l, LAYER_UNITS + i)

                step(FSTEPS - 1, next_units)

            def front(l, n):
                kind, h = JOBS[n]
                if kind == "c":
                    return
                b = n % 2
                st = jst[:, b, :]
                row = bias[:, h if kind == "a" else HEADS + h, :]
                dve.wait_ge(sc_done, l * NJ + n + 1)
                dve.tensor_tensor(job_s[:, b, 0:P], ps[:, SB + b, 0:P], row[:, P:2 * P], ALU.add)
                dve_read = dve.tensor_tensor(job_s[:, b, P:3 * P], ps[:, SB + b, P:3 * P], row, ALU.add)
                dve_read.then_inc(s_read, 1)
                dve.wait_ge(s_read, l * NJ + n + 1)
                dve.tensor_reduce(st[:, 0:1], job_s[:, b, 0:P], axis=AX.X, op=ALU.max)
                own.done(dve.tensor_reduce(st[:, 1:2], job_s[:, b, P:3 * P], axis=AX.X, op=ALU.max))
                if kind == "a":
                    dve.tensor_scalar(out=st[:, 2:4], in0=st[:, 0:2], scalar1=sink[:, bass.ds(l, 1), h], scalar2=-1.0,
                                      op0=ALU.max, op1=ALU.mult).then_inc(s_ready, 1)
                else:
                    dve.tensor_scalar(out=st[:, 2:4], in0=st[:, 0:2], scalar1=-1.0, scalar2=None,
                                      op0=ALU.mult).then_inc(s_ready, 1)

            def middle(l, n):
                kind, h = JOBS[n]
                b = n % 2
                st = jst[:, b, :]
                dve.wait_ge(front_done, l * NJ + n + 1)
                if kind == "c":
                    if n >= 26:
                        dve.wait_ge(mid_done, l * NJ + n - 1)
                    ins = dve.scalar_tensor_tensor(out=job_p[:, b, :], in0=ps[:, SB + b, 0:3 * P], scalar=0.0,
                                                   in1=job_s[:, b, :], op0=ALU.max, op1=ALU.add)
                    ins.then_inc(s_read, 1)
                    dve.wait_ge(s_read, l * NJ + n + 1)
                    dve.tensor_tensor(job_p[:, b, :], job_p[:, b, :], causal01[:, :], ALU.mult).then_inc(p_ready, 1)
                    return
                if kind == "a":
                    own.done(dve.tensor_tensor(st[:, 4:6], st[:, 4:6], st[:, 6:8], ALU.add))
                own.done(dve.reciprocal(st[:, 8:10], st[:, 4:6]))
                if kind != "a":
                    c0 = HEADS * (1 if kind == "slc" else 2) + h
                    own.done(dve.tensor_tensor(st[:, 8:10], st[:, 8:10], bgate[:, :, c0], ALU.mult))
                dve.tensor_scalar(out=job_p[:, b, 0:P], in0=job_p[:, b, 0:P], scalar1=st[:, 8:9], scalar2=None, op0=ALU.mult)
                dve.tensor_scalar(out=job_p[:, b, P:3 * P], in0=job_p[:, b, P:3 * P], scalar1=st[:, 9:10], scalar2=None,
                                  op0=ALU.mult).then_inc(p_ready, 1)

            def mask(l, n):
                dve.wait_ge(mid_done, l * NJ + n + 1)
                dve.wait_ge(pv_done, l * NJ + n - 1)
                dve.tensor_tensor(job_t[:, n % 2, :], ps[:, MID, 0:3 * P], causal_neg[:, :], ALU.add).then_inc(mask_done, 1)

            def pair_out(l, n):
                q = pair_done(n)
                if q is None:
                    return
                dve.wait_ge(y_hi, l * 12 + q + 1)
                hi, lo = branch_in(q // 4, q % 4)
                dve.tensor_tensor(lo, ps[:, OB, 0:S], hi.bitcast(F32), ALU.subtract).then_inc(y_lo, 1)

            def jobs(l, step):
                for n in job_slots(step):
                    if 2 <= n and JOBS[n - 2][0] == "c":
                        mask(l, n - 2)
                    if n < NJ:
                        front(l, n)
                for n in job_slots(step):
                    if n < NJ:
                        middle(l, n)
                for n in job_slots(step):
                    if 2 <= n:
                        pair_out(l, n - 2)

            dve.sem_inc(lo_ready, RING)
            dve.sem_inc(ada_sums, SUMS_AHEAD)
            dve.sem_inc(x_done, TOK)
            dve.wait_ge(setup_pe, 1)
            dve.tensor_copy(stat[:, 8:16], ps[:, 0, 0:KC]).then_inc(setup_dve, 1)
            dve.wait_ge(setup_in[1], 32)
            dve.memset(w_raw[32:33, 0, 1024:1040], 1.0).then_inc(setup_dve, 1)
            dve.wait_ge(setup_pe, 2)
            dve.tensor_copy(w_raw[0:8, 1, 0:1024].rearrange("h (a n) -> h a n", n=512)[:, :, 0:384],
                            ps[0:8, 2:4, 0:384]).then_inc(setup_dve, 1)
            dve.wait_ge(setup_in[3], 6)

            def first_sum(n):
                b, k = n // KC, n % KC
                acc = ada_acc[:, b * D:b * D + D]
                if b < 2:
                    dve.wait_ge(ada_full[n % 4], 16 * (n // 4 + 1))
                else:
                    dve.wait_ge(ada_gate[n % 4], 16 * (n // 4 - 3))
                if n:
                    dve.wait_ge(ada_done, n)
                if k == 0:
                    ins = dve.tensor_scalar(out=acc, in0=ada_raw[:, n % 4, :], scalar1=c_act[:, k:k + 1], scalar2=None, op0=ALU.mult)
                else:
                    ins = dve.scalar_tensor_tensor(out=acc, in0=ada_raw[:, n % 4, :], scalar=c_act[:, k:k + 1],
                                                   in1=acc, op0=ALU.mult, op1=ALU.add)
                ins.then_inc(ada_done, 1)

            for n in range(8):
                first_sum(n)
            dve.wait_ge(setup_pe, 8)
            dve.tensor_copy(ln_t[:, 0, :], ps[:, 1, 0:48])
            dve.tensor_copy(ln_t[:, 1, :], ps[:, 1, 64:112])
            dve.tensor_copy(adab_t[:, :].rearrange("p (l r) -> p l r", l=2),
                            ps[:, 1, 128:384].rearrange("p (l r) -> p l r", l=2)[:, :, 0:72])
            dve.tensor_copy(pos_t[:, :, :], ps[0:DH, 1, 384:512].rearrange("p (l r) -> p l r", l=2)).then_inc(setup_dve, 1)
            for n in range(8, 16):
                first_sum(n)
            dve.wait_ge(x_in, 16)
            dve.wait_ge(const_in, 6 * 16)
            for k in range(RING):
                lo_parts(0, k)
            with dve.Fori(0, DEPTH) as l:
                own.n, own.base = 0, l * OWN
                scale_x(l, 0)
                modulate(l, 0, l * 3 + 1)
                norm_h(l, 0)
                with dve.If(l < 1):
                    for n in range(16, 24):
                        first_sum(n)
                modulate_gate(l, 0, l * 3 + 1)
                gate_turned(0, l * 3 + 1)
                ffn(l, 0)
                modulate(l, 2, l * 3 + 2)
                modulate_gate(l, 2, l * 3 + 2)
                gate_copy(l, 0)
                gate_turned(2, l * 3 + 2)
                residual(l, 0)
                scale_x(l, 1)
                modulate(l, 1, l * 3 + 3)
                norm_h(l, 1)
                modulate_gate(l, 1, l * 3 + 3)
                gate_turned(1, l * 3 + 3)
                for v in range(MIX_UNITS):
                    if v in (2, 5, 6, 7):
                        dve.wait_ge(unit_used, used(l, FFN_UNITS + v))
                        bank = ps[:, QB + v % 2, :]
                        if v == 5:
                            for g in range(2):
                                ins = dve.tensor_copy(kvin[:, :, g, :],
                                                      bank[DH * g:DH * g + DH, :].rearrange("p (k s) -> p k s", s=S))
                            ins.then_inc(q_out_dve, 1)
                        else:
                            kdst = {2: ak, 6: bks, 7: bkw}[v]
                            vdst = {2: av, 6: bvs, 7: bvw}[v]
                            for g in range(2):
                                for half in range(2):
                                    dve.tensor_copy(kdst[DH * half:DH * half + DH, g, :], bank[DH * g:DH * g + DH, 0:S])
                            dve.tensor_copy(vdst[:, :, :], bank[:, S:2 * S].rearrange("p (t n) -> p t n", n=P)).then_inc(q_out_dve, 1)
                    if v == 5:
                        dve.wait_ge(q_out_dve, l * 4 + 2)
                        for e in range(2):
                            for half in range(2):
                                for g in range(2):
                                    a0 = kvin[:, e, g, :]
                                    src = bass.AP(tensor=a0.tensor, offset=a0.offset + half,
                                                  ap=[list(a0.ap[0]), [2, 16], [CMP_STRIDE, NCMP]])
                                    pp = pos_t[:, bass.ds(l, 1), e * CMP_BLOCK:(e + 1) * CMP_BLOCK]\
                                        .rearrange("p a (c r) -> p (a c) r", r=2)[:, :, half:half + 1].to_broadcast([DH, 16, NCMP])
                                    ins = dve.tensor_tensor(zc[DH * half:DH * half + DH, e, :, g * NCMP:(g + 1) * NCMP],
                                                            src, pp, ALU.add)
                        ins.then_inc(z_ready, 1)
                        dve.wait_ge(bg_hi, l + 1)
                        dve.tensor_tensor(g_lo[:, :, :], g_raw[:, :, :], g_hi[:, :, :].bitcast(F32), ALU.subtract).then_inc(bg_lo, 1)
                    if v == 6:
                        dve.wait_ge(hid_ready, l * 2 + 2)
                        for g in range(2):
                            ins = dve.tensor_copy(hid_v[:, g, :, 0:NCMP], hid[:, 1, g, :].unsqueeze(1).to_broadcast([P, 4, NCMP]))
                        ins.then_inc(kc_ready, 1)
                    if v == 7:
                        dve.wait_ge(kc_ps, l + 1)
                        dve.tensor_copy(kc_t[:, :, :], ps[:, MB, 128:128 + 2 * NCMP].rearrange("p (g n) -> p g n", g=2))
                        dve.tensor_copy(vc[:, :, :], ps[:, MB, 256:256 + 2 * DH].rearrange("p (g n) -> p g n", g=2)).then_inc(kc_ready, 1)
                        dve.wait_ge(bg_exp, l + 1)
                        own.done(dve.tensor_scalar(out=egate[:, :, :], in0=egate[:, :, :], scalar1=1.0, scalar2=None, op0=ALU.add))
                        dve.reciprocal(bgate[:, :, :], egate[:, :, :]).then_inc(bg_ready, 1)
                    if v == 8:
                        dve.wait_ge(cs_ps, l + 1)
                        dve.wait_ge(bg_ready, l + 1)
                        cp = cmp_p[:, :, 0:NCMP]
                        for odd in range(2):
                            logits = ps[:, MB + 1 - odd, 0:256].rearrange("p (g t h n) -> p g t h n", g=2, t=TOK, n=32)
                            for g in range(2):
                                for t in range(TOK):
                                    r = (g * TOK + t) * 4 + odd
                                    ins = dve.tensor_tensor(cp[:, r:r + 3:2], logits[:, g, t, :, 0:NCMP],
                                                            cmp_neg[:, t:t + 1, :].to_broadcast([P, 2, NCMP]), ALU.add)
                        own.done(ins)
                        own.done(dve.tensor_reduce(cst[:, 0, :], cp, axis=AX.X, op=ALU.max))
                        dve.tensor_tensor(cp, cp, cst[:, 0, :].unsqueeze(2).to_broadcast([P, 16, NCMP]), ALU.subtract).then_inc(cs_ready, 1)
                        dve.wait_ge(cexp_done, l + 1)
                        for g in range(2):
                            for t in range(TOK):
                                r = (g * TOK + t) * 4
                                ins = dve.tensor_tensor(cp[:, r:r + 4], cp[:, r:r + 4],
                                                        cmp_01[:, t:t + 1, :].to_broadcast([P, 4, NCMP]), ALU.mult)
                        own.done(ins)
                        own.done(dve.tensor_reduce(cst[:, 1, :], cp, axis=AX.X, op=ALU.add))
                        own.done(dve.tensor_scalar(out=cst[:, 1, :], in0=cst[:, 1, :], scalar1=1e-30, scalar2=None, op0=ALU.max))
                        own.done(dve.reciprocal(cst[:, 2, :], cst[:, 1, :]))
                        for g in range(2):
                            ins = dve.tensor_tensor(cst[:, 2, 8 * g:8 * g + 8].rearrange("p (t h) -> p t h", h=4),
                                                    cst[:, 2, 8 * g:8 * g + 8].rearrange("p (t h) -> p t h", h=4),
                                                    bgate[:, :, 4 * g:4 * g + 4], ALU.mult)
                        own.done(ins)
                        dve.tensor_tensor(cp, cp, cst[:, 2, :].unsqueeze(2).to_broadcast([P, 16, NCMP]), ALU.mult).then_inc(cp_ready, 1)
                    if 14 <= v < 32 and (v - 14) % 3 == 2:
                        it = (v - 14) // 3
                        i, half = it // 2, it % 2
                        for t in range(TOK):
                            if t == 0:
                                dve.wait_ge(br_ps, l * 6 + it + 1)
                            else:
                                dve.wait_ge(unit_used, used(l, FFN_UNITS + v))
                            dve.wait_ge(mg_ready, (l * 6 + it) * 2 + t + 1)
                            m = merged[:, t, half * 512:half * 512 + 512]
                            if i == 0:
                                dve.tensor_tensor(m, mg[:, t, :], branch_out(it, t), ALU.mult).then_inc(br_read, 1)
                            else:
                                dve.tensor_tensor(mg[:, t, :], mg[:, t, :], branch_out(it, t), ALU.mult).then_inc(dve_own, 1)
                                own.n += 1
                                dve.wait_ge(dve_own, own.base + own.n)
                                dve.tensor_tensor(m, m, mg[:, t, :], ALU.add).then_inc(br_read, 1)
                    jobs(l, v)
                    if v in (30, 32):
                        for q in range(2):
                            dve.wait_ge(mhi_ready, l * 4 + (v - 30) + q + 1)
                            lo, hi = ((act_lo[:, 1, 2 * q:2 * q + 2, :], act_hi[:, 1, 2 * q:2 * q + 2, :]) if v == 30 else
                                      (h_lo[:, 4 + 2 * q:6 + 2 * q, :], h_hi[:, 4 + 2 * q:6 + 2 * q, :]))
                            dve.tensor_tensor(lo, ps[:, MID + q, :].rearrange("p (a b) -> p a b", b=S),
                                              hi.bitcast(F32), ALU.subtract).then_inc(mlo_ready, 1)
                    lo_parts(l, FFN_UNITS + v + 3)
                    if v == 34:
                        gate_copy(l, 1)
                residual(l, 1)
                scale_x(l, 2)
                norm_h(l, 2)
                ffn(l, 1)
                gate_copy(l, 2)
                residual(l, 2)
                own.end()

        @block.tensor
        def _(pe):
            def three(out_, lhs, rhs, first, last):
                (lh, ll), (rh, rl) = lhs, rhs
                pe.matmul(out_, lh, rh, start=first, stop=False, skip_group_check=True)
                pe.matmul(out_, lh, rl, start=False, stop=False, skip_group_check=True)
                return pe.matmul(out_, ll, rh, start=False, stop=last, skip_group_check=True)

            def w_part(k, width):
                s = k % RING
                return (w_hi[:, s, :].rearrange("p (c n) -> p c n", n=width),
                        w_lo[:, s, :].rearrange("p (c n) -> p c n", n=width))

            def columns(s, n0, src, c0, c1):
                for c in range(c0, c1):
                    ins = pe.matmul(ps[:, MODB, s * 32 + c:s * 32 + c + 1], src[:, n0 + c * P:n0 + c * P + P], ones[:, 0:1],
                                    start=True, stop=True)
                ins.then_inc(modps_done, 1)

            def gate_row(s, n):
                pe.wait_ge(mod_ready, n)
                pe.transpose(ps[0:KC, MODB, 128:256], mod_g[:, s, :], ident[:, :]).then_inc(gt_ps, 1)

            def h_columns(l, s):
                for t in range(TOK):
                    pe.wait_ge(xs_ready, (l * NSUB + s) * 2 + t + 1)
                    for q in range(4):
                        for c in (2 * q, 2 * q + 1):
                            ins = pe.transpose(ps[:, HB[q], (c % 2) * S + t * P:(c % 2) * S + t * P + P],
                                               xs[:, t, c * P:c * P + P], ident[:, :])
                        if t == TOK - 1:
                            ins.then_inc(h_ps, 1)

            def wait_h(l, s, c):
                if c % 2 == 0:
                    pe.wait_ge(hlo_ready, (l * NSUB + s) * 4 + c // 2 + 1)

            def gate_rows_out(l, s):
                pe.wait_ge(gt_ready, l * NSUB + (1, 3, 2)[s])
                for c in range(KC):
                    ins = pe.matmul(ps[:, GU + c // 4, (c % 4) * P:(c % 4) * P + P],
                                    ident[0:KC, c:c + 1].to_broadcast([KC, P]), gt[:, s, :], start=True, stop=True)
                ins.then_inc(g_ps, 1)

            def ffn(l, f):
                k0 = f * (FFN_UNITS + MIX_UNITS)
                n = (l * 2 + f) * FSTEPS

                def wait_unit(k, j):
                    pe.wait_ge(lo_ready, unit_of(l, k) + 3 * j + RING + 1)

                def gate_up(k, part, j, jr, first=False):
                    wait_unit(k, jr)
                    wh, wl = w_part(k, 2 * FB)
                    if part == 0 and not first:
                        pe.wait_ge(act_done, 2 * (n + j))
                    for t in range(TOK):
                        for c in range(4):
                            kc = 4 * part + c
                            ts = slice(t * P, t * P + P)
                            if (first or part == 1) and t == 0:
                                wait_h(l, 2 * f, kc)
                            ins = three(ps[:, GU + t, :], (h_hi[:, kc, ts], h_lo[:, kc, ts]), (wh[:, c], wl[:, c]),
                                        kc == 0, kc == KC - 1)
                        if t == 1:
                            ins.then_inc(unit_used, 1)
                        elif part == 1:
                            ins.then_inc(gu_done, 1)

                def turn(j):
                    pe.wait_ge(act_done, 2 * (n + j) + 2)
                    for c in range(2):
                        for t in range(TOK):
                            ins = pe.transpose(ps[:, TB, c * S + t * P:c * S + t * P + P], ffn_a[:, t, c * P:c * P + P], ident[:, :])
                    ins.then_inc(at_ps, 1)

                def down(k, j, jr, first, last):
                    wait_unit(k, jr)
                    pe.wait_ge(alo_ready, n + j + 1)
                    wh, wl = w_part(k, D)
                    for t in range(TOK):
                        for half in range(2):
                            for c in range(2):
                                ts = slice(t * P, t * P + P)
                                hs = slice(half * 512, half * 512 + 512)
                                ins = three(ps[:, 2 * t + half, :], (act_hi[:, 0, c, ts], act_lo[:, 0, c, ts]),
                                            (wh[:, c, hs], wl[:, c, hs]), first and c == 0, last and c == 1)
                        if last and t == 0:
                            ins.then_inc(y_half, 1)
                    ins.then_inc(unit_used, 1)

                gate_up(k0, 0, 0, 0, first=True)
                gate_up(k0 + 1, 1, 0, 0)
                gate_up(k0 + 2, 0, 1, 0)
                turn(0)
                gate_up(k0 + 3, 1, 1, 0)
                down(k0 + 4, 0, 0, True, False)
                with pe.Fori(2, FSTEPS) as j:
                    gate_up(k0 - 1, 0, j, j)
                    turn(j - 1)
                    gate_up(k0, 1, j, j)
                    down(k0 + 1, j - 1, j, False, False)
                if f == 0:
                    pe.wait_ge(ada_sums, ada_before(l, 1, 1) + SUMS_AHEAD)
                    columns(2, MOD, ada_acc, 0, 16)
                    columns(2, MOD, ada_acc, 16, 24)
                turn(FSTEPS - 1)
                gate_rows_out(l, 2 * f)
                down(k0 + FFN_UNITS - 1, FSTEPS - 1, 0, False, True)
                if f == 0:
                    gate_row(2, l * 3 + 2)

            def front(l, n):
                kind, h = JOBS[n]
                b = n % 2
                po = DH * (h % 2)
                g = h // HPG
                hs = slice(po, po + DH)
                if n == 0 or n == 8 or n == 24:
                    pe.wait_ge(q_out_act, l * 10 + {0: 2, 8: 4, 24: 10}[n])
                    pe.wait_ge(q_out_dve, l * 4 + {0: 1, 8: 4, 24: 4}[n])
                if n >= 2:
                    pe.wait_ge(s_read, l * NJ + n - 1)
                S_ = ps[:, SB + b, :]
                if kind == "c":
                    q, k = cq[hs, h // 2, :], ck[hs, h // 2, :]
                    pe.matmul(S_[:, 0:S], k[:, 0:P], q, start=True, stop=True)
                    pe.matmul(S_[:, S:S + P], k[:, P:2 * P], q[:, P:2 * P], start=True, stop=True).then_inc(sc_done, 1)
                    return
                q = (aq if kind == "a" else bq)[hs, h // 2, :]
                k = {"a": ak, "slc": bks, "win": bkw}[kind][hs, g, :]
                pe.matmul(S_[:, 0:P], q[:, 0:P], k[:, 0:P], start=True, stop=True)
                pe.matmul(S_[:, P:3 * P], q[:, P:2 * P], k, start=True, stop=True).then_inc(sc_done, 1)

            def middle(l, n):
                kind, h = JOBS[n]
                b = n % 2
                po = DH * (h % 2)
                hs = slice(po, po + DH)
                pe.wait_ge(p_ready, l * NJ + n + 1)
                if n >= 1:
                    if JOBS[n - 1][0] == "c":
                        pe.wait_ge(mask_done, l * HEADS + n - 24)
                    else:
                        pe.wait_ge(pt_ready, l * NJ + n)
                M_ = ps[:, MID, :]
                if kind == "c":
                    q, k = cq[hs, h // 2, :], ck[hs, h // 2, :]
                    L = job_p[:, b, :]
                    pe.matmul(M_[:, 0:S], neg_tri[:, :], L[:, 0:S], start=True, stop=False, skip_group_check=True)
                    pe.matmul(M_[:, P:S], neg_ones[:, :], L[:, S:S + P], start=False, stop=False, skip_group_check=True)
                    pe.matmul(M_[:, S:S + P], neg_tri[:, :], L[:, S:S + P], start=False, stop=False, skip_group_check=True)
                    pe.matmul(M_[:, 0:S], k[:, 0:P], q, start=False, stop=False, skip_group_check=True)
                    pe.matmul(M_[:, S:S + P], k[:, P:2 * P], q[:, P:2 * P], start=False, stop=True,
                              skip_group_check=True).then_inc(mid_done, 1)
                    return
                for i in range(3):
                    ins = pe.transpose(M_[:, i * P:i * P + P], job_p[:, b, i * P:i * P + P], ident[:, :])
                ins.then_inc(mid_done, 1)

            def values(l, n):
                kind, h = JOBS[n]
                b = n % 2
                po = DH * (h % 2)
                g = h // HPG
                pe.wait_ge(pt_ready, l * NJ + n + 1)
                done = {"a": 0, "slc": 4, "win": 4, "c": 8}[kind] + h // 2
                if h % 2 == 0 and kind != "win" and n:
                    pe.wait_ge(y_lo, l * 12 + done)
                O = ps[po:po + DH, OB, :]
                v = {"a": av, "slc": bvs, "win": bvw, "c": cv}[kind]
                vs = slice(h * DH, h * DH + DH) if kind == "c" else slice(g * DH, g * DH + DH)
                pe.matmul(O[:, 0:S], v[:, 0, vs], job_t[:, b, 0:S], start=kind != "win", stop=False, skip_group_check=True)
                ins = pe.matmul(O[:, P:S], v[:, 1, vs], job_t[:, b, S:S + P], start=False, stop=kind in "ac",
                                skip_group_check=True)
                if kind == "win":
                    if h == 0:
                        pe.wait_ge(cpt_ready, l + 1)
                    r = 32 * (h % 4)
                    for t in range(TOK):
                        ins = pe.matmul(O[:, t * P:t * P + P], vc[r:r + NCMP, g, :], cmp_pt[r:r + NCMP, g, t, :],
                                        start=False, stop=t == 1, skip_group_check=True)
                ins.then_inc(pv_done, 1)

            def jobs(l, step):
                for n in job_slots(step):
                    if 2 <= n:
                        middle(l, n - 2)
                    if n < NJ:
                        front(l, n)
                for n in job_slots(step):
                    if 2 <= n:
                        values(l, n - 2)

            pe.sem_inc(unit_used, RING)
            pe.wait_ge(ident_in, 16)
            pe.wait_ge(c_in, 16)
            pe.wait_ge(setup_in[3], 5)
            pe.transpose(ps[:, 0, 0:KC], arena[0:KC, 12288:12288 + P], ident[0:KC, 0:KC]).then_inc(setup_pe, 1)
            pe.wait_ge(setup_dve, 2)
            for i in range(2):
                ins = pe.matmul(ps[0:8, 2 + i, 0:384], w_raw[0:33, 0, 1024 + 8 * i:1032 + 8 * i], w_raw[0:33, 0, 512 * i:512 * i + 384],
                                start=True, stop=True)
            ins.then_inc(setup_pe, 1)
            pe.wait_ge(setup_in[0], 64)
            for i in range(2):
                pe.transpose(ps[:, 1, 64 * i:64 * i + 48], arena[0:48, 12416 + P * i:12416 + P * i + P], ident[0:48, 0:48]).then_inc(setup_pe, 1)
            for i in range(2):
                pe.transpose(ps[:, 1, 128 + P * i:128 + P * i + 72], arena[0:72, 12672 + P * i:12672 + P * i + P], ident[0:72, 0:72]).then_inc(setup_pe, 1)
            for i in range(2):
                pe.transpose(ps[0:DH, 1, 384 + DH * i:384 + DH * i + DH], arena[0:DH, 12928 + DH * i:12928 + DH * i + DH],
                             ident[0:DH, 0:DH]).then_inc(setup_pe, 1)
            pe.wait_ge(flip_in, 16)
            pe.wait_ge(setup_in[2], 32)
            for i in range(4):
                if i >= 2:
                    pe.wait_ge(setup_act, i - 1)
                for e in range(2):
                    ins = pe.matmul(ps[:, 4 + 2 * (i % 2) + e, :], w_raw[:, 0, 1536:1536 + P],
                                    w_raw[:, 1 + i // 2, (i % 2) * 1024 + e * 512:(i % 2) * 1024 + e * 512 + 512], start=True, stop=True)
                ins.then_inc(setup_pe, 1)
            pe.wait_ge(setup_act, 4)
            pe.wait_ge(setup_dve, 4)
            pe.wait_ge(ada_done, 16)
            pe.wait_ge(const_in, 6 * 16)
            with pe.Fori(0, DEPTH) as l:
                pe.wait_ge(ada_sums, ada_before(l, 0, 1) + SUMS_AHEAD)
                columns(0, 0, ada_acc, 0, 16)
                h_columns(l, 0)
                pe.wait_ge(modc_ready, l * 3 + 1)
                with pe.If(l < 1):
                    pe.wait_ge(ada_done, 24)
                columns(0, 0, ada_acc, 16, 24)
                gate_row(0, l * 3 + 1)
                ffn(l, 0)
                pe.wait_ge(gt_ready, l * NSUB + 2)
                columns(1, 0, ada_acc, 0, 16)
                h_columns(l, 1)
                pe.wait_ge(modc_ready, l * 3 + 3)
                columns(1, 0, ada_acc, 16, 24)
                gate_row(1, l * 3 + 3)
                for v in range(MIX_UNITS):
                    k = FFN_UNITS + v
                    pe.wait_ge(lo_ready, unit_of(l, k) + RING + 1)
                    if v < QKV_UNITS:
                        if v >= 2:
                            a_ = sum(1 for w in range(v - 1) if w not in (2, 5, 6, 7))
                            d_ = sum(1 for w in range(v - 1) if w in (2, 5, 6, 7))
                            if v - 2 in (2, 5, 6, 7):
                                pe.wait_ge(q_out_dve, l * 4 + d_)
                            else:
                                pe.wait_ge(q_out_act, l * 10 + a_)
                        wh, wl = w_part(k, 256)
                        bank = ps[:, QB + v % 2, :]
                        for b in range(2):
                            bs = slice(b * P, b * P + P)
                            as_rows = v in (12, 13) or (b == 1 and v in (2, 6, 7))
                            if as_rows:
                                for t in range(TOK):
                                    ts = slice(t * P, t * P + P)
                                    for c in range(KC):
                                        ins = three(bank[:, b * S + t * P:b * S + t * P + P], (h_hi[:, c, ts], h_lo[:, c, ts]),
                                                    (wh[:, c, bs], wl[:, c, bs]), c == 0, c == KC - 1)
                            else:
                                for c in range(KC):
                                    if v == 0 and b == 0:
                                        wait_h(l, 1, c)
                                    ins = three(bank[:, b * S:b * S + S], (wh[:, c, bs], wl[:, c, bs]),
                                                (h_hi[:, c, :], h_lo[:, c, :]), c == 0, c == KC - 1)
                        ins.then_inc(unit_used, 1)
                    elif v < 32:
                        it, part = (v - 14) // 3, (v - 14) % 3
                        i = it // 2
                        wh, wl = w_part(k, 512)
                        if part == 0:
                            if it:
                                pe.wait_ge(mg_ready, (l * 6 + it) * 2)
                            else:
                                pe.wait_ge(cpt_ready, l + 1)
                        if part == 2:
                            if it:
                                pe.wait_ge(br_read, (l * 6 + it) * 2)
                            else:
                                pe.wait_ge(q_out_act, l * 10 + 10)
                            pe.wait_ge(y_lo, l * 12 + 4 * i + 4)
                        for t in range(TOK):
                            ts = slice(t * P, t * P + P)
                            for c in range(4):
                                if part < 2:
                                    kc = 4 * part + c
                                    ins = three(ps[:, MB + t, :], (h_hi[:, kc, ts], h_lo[:, kc, ts]), (wh[:, c], wl[:, c]),
                                                kc == 0, kc == KC - 1)
                                else:
                                    ins = three(branch_out(it, t), branch_in(i, c, ts),
                                                (wh[:, c], wl[:, c]), c == 0, c == 3)
                            if t == 1:
                                ins.then_inc(unit_used, 1)
                            elif part == 1:
                                ins.then_inc(mg_ps, 1)
                            elif part == 2:
                                ins.then_inc(br_ps, 1)
                    else:
                        wh, wl = w_part(k, D)
                        if v == 32:
                            pe.wait_ge(mg_ready, l * 12 + 12)
                        if v in (32, 34):
                            pe.wait_ge(mlo_ready, l * 4 + v - 30)
                        if v == 35:
                            gate_rows_out(l, 1)
                        mh, ml = (act_hi[:, 1], act_lo[:, 1]) if v < 34 else (h_hi[:, 4:8], h_lo[:, 4:8])
                        for t in range(TOK):
                            ts = slice(t * P, t * P + P)
                            for half in range(2):
                                hs = slice(half * 512, half * 512 + 512)
                                for c in range(2):
                                    kc = 2 * (v - 32) + c
                                    ins = three(ps[:, 2 * t + half, :], (mh[:, kc % 4, ts], ml[:, kc % 4, ts]),
                                                (wh[:, c, hs], wl[:, c, hs]), kc == 0, kc == KC - 1)
                            if v == 35 and t == 0:
                                ins.then_inc(y_half, 1)
                        ins.then_inc(unit_used, 1)
                    if v == 6:
                        pe.wait_ge(w1_in, l * 112 + 112)
                        pe.wait_ge(z_ready, l + 1)
                        for e in range(2):
                            for c in range(16):
                                ins = pe.matmul(ps[:, MB, e * 2 * NCMP:(e + 1) * 2 * NCMP], w1[:, e, c, :], zc[:, e, c, :],
                                                start=c == 0, stop=c == 15)
                        ins.then_inc(hid_ps, 1)
                    if v == 7:
                        pe.wait_ge(kc_ready, l * 2 + 1)
                        pe.matmul(ps[:, MB, 128:128 + 2 * NCMP], w2k[:, :, :].rearrange("p a b -> p (a b)"),
                                  hid[:, 0, :, :].rearrange("p a b -> p (a b)"), start=True, stop=True)
                        for g in range(2):
                            ins = pe.matmul(ps[:, MB, 256 + g * DH:256 + g * DH + DH],
                                            hid_v[:, g, :, :].rearrange("p a b -> p (a b)"), w2v[:, :], start=True, stop=True)
                        ins.then_inc(kc_ps, 1)
                        pe.wait_ge(bg_lo, l + 1)
                        for t in range(TOK):
                            ts = slice(t * P, t * P + P)
                            for c in range(KC):
                                ins = three(ps[:, MB + 1, 24 * t:24 * t + 24], (h_hi[:, c, ts], h_lo[:, c, ts]),
                                            (g_hi[:, c, :], g_lo[:, c, :]), c == 0, c == KC - 1)
                        ins.then_inc(bg_ps, 1)
                    if v == 8:
                        pe.wait_ge(kc_ready, l * 2 + 2)
                        pe.wait_ge(bg_exp, l + 1)
                        pe.wait_ge(q_out_act, l * 10 + 4)
                        for h in range(HEADS):
                            g, po = h // HPG, DH * (h % 2)
                            for t in range(TOK):
                                r = (g * TOK + t) * 2 + h % 4 // 2
                                ins = pe.matmul(ps[:, MB + 1 - h % 2, r * 32:r * 32 + NCMP], bq[po:po + DH, h // 2, t * P:t * P + P],
                                                kc_t[po:po + DH, g, :], start=True, stop=True)
                        ins.then_inc(cs_ps, 1)
                    if v == 9:
                        pe.wait_ge(cp_ready, l + 1)
                        for i in range(4):
                            ins = pe.transpose(ps[:, MB + 1, i * P:i * P + P],
                                               cmp_p[:, 4 * i:4 * i + 4, :].rearrange("p a b -> p (a b)"), ident[:, :])
                        ins.then_inc(cpt_ps, 1)
                    jobs(l, v)
                    if v in (30, 32):
                        pe.wait_ge(br_read, l * 12 + 10 + v - 30)
                        for q in range(2):
                            for c in (2 * q, 2 * q + 1):
                                for t in range(TOK):
                                    ch = c + (4 if v == 32 else 0)
                                    ins = pe.transpose(ps[:, MID + q, (c % 2) * S + t * P:(c % 2) * S + t * P + P],
                                                       merged[:, t, ch * P:ch * P + P], ident[:, :])
                            ins.then_inc(m_ps, 1)
                h_columns(l, 2)
                ffn(l, 1)


def constants():
    import numpy as np

    p = np.arange(P)
    out = {"k_ident": np.eye(P), "k_flip": np.eye(P)[::-1]}
    out["k_negtri"] = -(p[:, None] >= p[None, :]).astype(np.float32)
    before = (p[:, None] < p[None, :]).astype(np.float32)
    one = np.ones((P, P), np.float32)
    out["k_causal01"] = np.concatenate([before, one, before], 1)
    out["k_causalneg"] = np.where(out["k_causal01"] > 0, 0.0, NEG)
    t = p[:, None, None] + P * np.arange(TOK)[None, :, None]
    ok = np.arange(NCMP)[None, None, :] * CMP_STRIDE + CMP_BLOCK - 1 <= t
    out["k_cmp01"] = ok.astype(np.float32)
    out["k_cmpneg"] = np.where(ok, 0.0, NEG)
    dist = 255 - np.arange(384)
    d = np.maximum(dist, 0)
    ratio = np.log(np.maximum(d, 1).astype(np.float32) / np.float32(16)) / np.float32(np.log(128 / 16))
    big = np.minimum(16 + (ratio * np.float32(16)).astype(np.int32), 31)
    bucket = np.where(d < 16, d, big)
    k = np.zeros((33, 2, 512), np.float32)
    for i, ok in enumerate(((dist >= 0) & (dist < 128), dist >= 0)):
        k[bucket[ok], i, np.nonzero(ok)[0]] = 1.0
        k[32, i, 0:384] = np.where(ok, 0.0, NEG)
    out["k_buckets"] = k.reshape(33, 1024)
    return {n: np.ascontiguousarray(a.astype(np.float32)) for n, a in out.items()}


def kernel(x, c, rel_bias, ada_w, ada_b, ln_pre, ln_post, ffn_w_gate, ffn_w_up, ffn_w_down,
           w_in, attn_sinks, cmp_pos, cmp_w1, cmp_w2, w_branch, w_out):
    import numpy as np
    import concourse.bacc as bacc
    from concourse.bass_utils import run_bass_kernel_spmd

    given = dict(x=x, c=c, rel_bias=rel_bias, ada_w=ada_w, ada_b=ada_b, ln_pre=ln_pre, ln_post=ln_post,
                 ffn_w_gate=ffn_w_gate, ffn_w_up=ffn_w_up, ffn_w_down=ffn_w_down, w_in=w_in,
                 attn_sinks=attn_sinks, cmp_pos=cmp_pos, cmp_w1=cmp_w1, cmp_w2=cmp_w2,
                 w_branch=w_branch, w_out=w_out)
    nc = bacc.Bacc("TRN2", target_bir_lowering=False, num_devices=1)
    arrays, A = {}, {}
    for name, a in {**given, **constants()}.items():
        a = np.ascontiguousarray(a)
        arrays["in_" + name] = a
        A[name] = nc.dram_tensor("in_" + name, a.shape, mybir.dt.from_np(a.dtype), kind="ExternalInput").ap()
    A["scratch"] = nc.dram_tensor("bias_scratch", (2, 8, 384), F32, kind="Internal").ap()
    out = nc.dram_tensor("out", (1, S, D), F32, kind="ExternalOutput").ap()
    trunk_program(nc, A, out)
    return run_bass_kernel_spmd(nc, [arrays], core_ids=[0]).results[0]["out"]
```

```python
from contextlib import ExitStack

import concourse.bass as bass
from concourse import mybir

F32 = mybir.dt.float32
F32R = mybir.dt.float32r
ACT = mybir.ActivationFunctionType
ALU = mybir.AluOpType
AX = mybir.AxisListType

P = 128
D = 1024
S = 256
DEPTH = 2
DH = 64
HEADS = 8
HPG = 4
FF = 2816
NSUB = 3
CMP_BLOCK = 32
CMP_STRIDE = 16
NCMP = (S - CMP_BLOCK) // CMP_STRIDE + 1
EPS = 1e-6
NEG = -1e30
KC = D // P
TOK = S // P

RING = 3
UNIT = 2048
LOADS = 2
FB = 256
FSTEPS = FF // FB
FFN_UNITS = 3 * FSTEPS
SUMS_AHEAD = 8
ADA_STEPS = 8
ADA_COLS = (4 * D, 3 * D)
MIX_ADA_LOAD = {15: 0, 20: 1, 21: 2, 24: 3, 25: 4, 27: 5, 28: 6, 29: 7}
MIX_ADA_SUM = {17: 0, 18: 1, 20: 2, 22: 3, 23: 4, 24: 5, 25: 6, 26: 7}
QKV_UNITS = 14
MIX_UNITS = QKV_UNITS + 3 * 6 + 4
LAYER_UNITS = 2 * FFN_UNITS + MIX_UNITS
GATE_COL = 2048
MERGE_COL = 3608
MOD = 3 * D

JOBS = ([("a", h) for h in range(HEADS)]
        + [(k, h) for h in range(HEADS) for k in ("slc", "win")]
        + [("c", h) for h in range(HEADS)])
NJ = len(JOBS)
JOB_STEPS = (3, 4, 5, 6) + tuple(range(9, 17)) + (17, 18, 20, 22, 23, 24)


def job_slots(step):
    if step not in JOB_STEPS:
        return range(0)
    first = 2 * JOB_STEPS.index(step)
    return range(first, first + 2)


def pair_done(n):
    kind, h = JOBS[n]
    if h % 2 == 0 or kind == "slc":
        return None
    return {"a": 0, "win": 4, "c": 8}[kind] + h // 2


def trunk_program(nc, A, out):
    ctx = ExitStack()
    with ctx:
        def sb(name, shape, dt=F32):
            return ctx.enter_context(nc.sbuf_tensor(name, shape, dt))

        def sem(name):
            return ctx.enter_context(nc.semaphore(name))

        x = sb("x", [P, TOK, D])
        h_hi = sb("h_hi", [P, KC, S], F32R)
        h_lo = sb("h_lo", [P, KC, S], F32R)
        w_raw = sb("w_raw", [P, RING, UNIT])
        w_hi = sb("w_hi", [P, RING, UNIT], F32R)
        w_lo = sb("w_lo", [P, RING, UNIT], F32R)
        act_hi = sb("act_hi", [P, 2, 4, S], F32R)
        act_lo = sb("act_lo", [P, 2, 4, S], F32R)
        g_raw = sb("g_raw", [P, KC, 24])
        g_hi = sb("g_hi", [P, KC, 24], F32R)
        g_lo = sb("g_lo", [P, KC, 24], F32R)
        bias = sb("bias", [P, 2 * HEADS, 2 * P])
        ident = sb("ident", [P, P])
        neg_tri = sb("neg_tri", [P, P])
        neg_ones = sb("neg_ones", [P, P])
        causal01 = sb("causal01", [P, 3 * P])
        causal_neg = sb("causal_neg", [P, 3 * P])
        cmp_neg = sb("cmp_neg", [P, TOK, NCMP])
        cmp_01 = sb("cmp_01", [P, TOK, NCMP])
        ln_t = sb("ln_t", [P, 2, DEPTH * NSUB * KC])
        adab_t = sb("adab_t", [P, DEPTH * NSUB * 24])
        pos_t = sb("pos_t", [DH, DEPTH, 2 * CMP_BLOCK])
        c_act = sb("c_act", [P, KC])
        sink = sb("sink", [P, DEPTH, HEADS])
        eps_t = sb("eps_t", [P, 1])
        modc = sb("modc", [P, NSUB, 2 * KC])
        mod_a = sb("mod_a", [P, NSUB, KC])
        mod_g = sb("mod_g", [P, NSUB, KC])
        gt = sb("gt", [KC, 2, P])
        rows = sb("rows", [32, P])
        sel = sb("sel", [P, 63])
        stat = sb("stat", [P, 16])
        w2k = sb("w2k", [P, 2, DH])
        w2v = sb("w2v", [P, DH])
        hid = sb("hid", [P, 2, NCMP])
        hid_v = sb("hid_v", [P, 2, 4, 32])
        kc_t = sb("kc_t", [P, 2, NCMP])
        vc = sb("vc", [P, 2, DH])
        bgate = sb("bgate", [P, TOK, 24])
        cmp_p = sb("cmp_p", [P, 2 * TOK * 4, 32])
        cmp_pt = sb("cmp_pt", [P, 2, TOK, P])
        cst = sb("cst", [P, 3, 16])
        jst = sb("jst", [P, 2, 12])

        AR = 15872
        arena = sb("arena", [P, AR])

        def region(at, *shape, parts=P):
            n = 1
            for d_ in shape:
                n *= d_
            v = arena[0:parts, at:at + n]
            if len(shape) == 2:
                return v.rearrange("p (a b) -> p a b", b=shape[1])
            if len(shape) == 3:
                return v.rearrange("p (a b c) -> p a b c", b=shape[1], c=shape[2])
            return v

        ada_acc = region(0, 2 * MOD)
        ada_raw = region(2 * MOD, 4, D)
        buckets = region(3072, 2, 512)
        rel = region(4096, 2 * HEADS)
        vec = region(4112, 2, 512)
        flip = region(5136, P)
        ffn_a = region(12288, TOK, FB)
        ffn_s = region(12800, TOK, FB)
        SCR = AR - 2048
        xs = region(SCR, TOK, D)
        gate_sb = region(12288, 2, 512)
        job_z = [region(5120, 3 * P), cmp_p[:, 0:12, :].rearrange("p a b -> p (a b)")]
        mix_acc = region(1024, 2 * D)
        mix_raw = [region(3072, 2 * D), region(5632, 2 * D)]
        w1 = region(0, 2, 16, P)
        mg = region(0, TOK, 512)
        hbuf = region(10240, KC, S)
        junk = region(9216, D)
        o_ = 4096
        aq = region(o_, 4, S); o_ += 1024
        ak = region(o_, 2, S); o_ += 512
        bq = region(o_, 4, S); o_ += 1024
        bks = region(o_, 2, S); o_ += 512
        bkw = region(o_, 2, S); o_ += 512
        cq = region(o_, 4, S); o_ += 1024
        ck = region(o_, 4, S); o_ += 1024
        av = region(o_, TOK, P); o_ += 256
        bvs = region(o_, TOK, P); o_ += 256
        bvw = region(o_, TOK, P); o_ += 256
        cv = region(o_, TOK, 512); o_ += 1024
        job_s = region(o_, 2, 3 * P); o_ += 768
        job_p = region(o_, 2, 3 * P); o_ += 768
        job_t = region(o_, 2, 3 * P); o_ += 768
        assert o_ <= SCR
        kvin = region(SCR, 2, 2, S, parts=DH)
        hid_rows = region(SCR, 2, P, parts=2 * NCMP)
        gate_exp = region(SCR + 2 * P, S, parts=24)
        zc = region(SCR + 1024, 2, 16, 2 * NCMP)
        merged = region(SCR, TOK, D)

        ps = ctx.enter_context(nc.psum_tensor("ps", [P, 8, 512], F32))
        GU, TB, MODB = 4, 6, 7
        QB, MB, SB, MID, OB = 0, 2, 4, 6, 7

        const_in = sem("const_in")
        ident_in = sem("ident_in")
        c_in = sem("c_in")
        flip_in = sem("flip_in")
        setup_in = [sem(f"setup_in{i}") for i in range(4)]
        x_in = sem("x_in")
        raw_full = [sem(f"raw_full{i}") for i in range(RING)]
        hi_ready = sem("hi_ready")
        lo_ready = sem("lo_ready")
        unit_used = sem("unit_used")
        ada_full = [sem(f"ada_full{i}") for i in range(4)]
        ada_half = [sem(f"ada_half{i}") for i in range(2)]
        ada_sums = sem("ada_sums")
        ada_done = sem("ada_done")
        rows_ps = sem("rows_ps")
        rows_ready = sem("rows_ready")
        cols_ps = sem("cols_ps")
        mix_ada = [sem(f"mix_ada{i}") for i in range(2)]
        mix_sums = sem("mix_sums")
        ada_gate = [sem(f"ada_gate{i}") for i in range(4)]
        setup_act = sem("setup_act")
        y_half = sem("y_half")
        mod_ready = sem("mod_ready")
        gt_ps = sem("gt_ps")
        gt_ready = sem("gt_ready")
        h_ps = sem("h_ps")
        h32_ready = sem("h32_ready")
        hhi_ready = sem("hhi_ready")
        hlo_ready = sem("hlo_ready")
        xrms_done = sem("xrms_done")
        xinv_ready = sem("xinv_ready")
        xs_ready = sem("xs_ready")
        x_done = sem("x_done")
        g_ps = sem("g_ps")
        yrms_done = sem("yrms_done")
        gu_done = sem("gu_done")
        silu_done = sem("silu_done")
        act_done = sem("act_done")
        at_ps = sem("at_ps")
        ahi_ready = sem("ahi_ready")
        alo_ready = sem("alo_ready")
        q_out_act = sem("q_out_act")
        q_out_dve = sem("q_out_dve")
        bg_in = sem("bg_in")
        bg_hi = sem("bg_hi")
        bg_lo = sem("bg_lo")
        bg_ps = sem("bg_ps")
        bg_exp = sem("bg_exp")
        bg_turned = sem("bg_turned")
        bg_ready = sem("bg_ready")
        w1_in = sem("w1_in")
        z_ready = sem("z_ready")
        hid_ps = sem("hid_ps")
        hid_ready = sem("hid_ready")
        hid_turned = sem("hid_turned")
        kc_ps = sem("kc_ps")
        kc_ready = sem("kc_ready")
        cs_ps = sem("cs_ps")
        cs_ready = sem("cs_ready")
        cexp_done = sem("cexp_done")
        cp_ready = sem("cp_ready")
        cpt_ps = sem("cpt_ps")
        cpt_ready = sem("cpt_ready")
        sc_done = sem("sc_done")
        s_read = sem("s_read")
        s_ready = sem("s_ready")
        front_done = sem("front_done")
        p_ready = sem("p_ready")
        mid_done = sem("mid_done")
        mask_done = sem("mask_done")
        pt_ready = sem("pt_ready")
        pv_done = sem("pv_done")
        y_hi = sem("y_hi")
        y_lo = sem("y_lo")
        mg_ps = sem("mg_ps")
        mg_ready = sem("mg_ready")
        br_ps = sem("br_ps")
        br_read = sem("br_read")
        m_ps = sem("m_ps")
        mhi_ready = sem("mhi_ready")
        mlo_ready = sem("mlo_ready")
        act_own = sem("act_own")
        dve_own = sem("dve_own")
        mod_made = sem("mod_made")
        setup_pe = sem("setup_pe")
        setup_dve = sem("setup_dve")
        scratch_out = sem("scratch_out")
        out_sem = sem("out_sem")

        def branch_in(i, c, ts=slice(0, S)):
            return act_hi[:, i % 2, c, ts], act_lo[:, i % 2, c, ts]

        def mods_before(l, s):
            return l * 4 * NSUB + (3, 9, 12, 15)[s]

        def h_part(half, t):
            return slice(0, P), slice(4 * half, 4 * half + 4), slice(t * P, t * P + P)

        def branch_out(it, t):
            return ps[:, (SB if it == 5 else QB) + t, :]

        OWN = 512

        class Own:

            def __init__(self, eng, s):
                self.eng, self.s, self.n, self.base = eng, s, 0, 0

            def end(self):
                assert self.n < OWN
                self.eng.sem_inc(self.s, OWN - self.n)

            def counted(self, ins):
                ins.then_inc(self.s, 1)
                self.n += 1

            def done(self, ins):
                self.counted(ins)
                self.eng.wait_ge(self.s, self.base + self.n)

        block = ctx.enter_context(nc.Block())

        def used(l, k):
            return l * LAYER_UNITS + k + RING + 1

        def unit_of(l, k):
            return l * LAYER_UNITS + k

        def ada_width(f):
            return ADA_COLS[f] // ADA_STEPS

        def ada_view(f, half):
            w = ada_width(f)
            at = 2 * MOD + half * 4 * w
            return arena[:, at:at + 4 * w].rearrange("p (c n) -> p c n", n=w)

        def ada_before(l, f, j):
            return (l * 2 + f) * KC * ADA_STEPS + (j - 1) * KC

        def unit_parts(k, l, j):
            slot = k % RING
            r = w_raw[:, slot, :]
            f, q = (0, k) if k < FFN_UNITS else (1, k - FFN_UNITS - MIX_UNITS)
            if 0 <= q < FFN_UNITS:
                kind, j = j
                if kind == "D":
                    rows = A["ffn_w_down"][l, f, bass.ds(j * FB, FB), :].rearrange("(c p) n -> p c n", p=P)
                    v = r.rearrange("p (c n) -> p c n", n=D)
                    return [(v[:, c], rows[:, c]) for c in range(2)]
                v = r.rearrange("p (c n) -> p c n", n=2 * FB)
                k0 = 0 if kind == "GA" else 4 * P
                return [(v[:, :, i * FB:(i + 1) * FB],
                         A[w][l, f, k0:k0 + 4 * P, bass.ds(j * FB, FB)].rearrange("(c p) n -> p c n", p=P))
                        for i, w in enumerate(("ffn_w_gate", "ffn_w_up"))]
            v_ = k - FFN_UNITS
            if v_ < QKV_UNITS:
                v = r.rearrange("p (c n) -> p c n", n=256)
                if v_ in (6, 7):
                    return [(v[:, :, P * i:P * i + P],
                             A["w_in"][l, :, c0:c0 + P].rearrange("(c p) n -> p c n", p=P))
                            for i, c0 in enumerate((256 * 6 + P * (v_ - 6), 256 * 7 + P * (v_ - 6)))]
                col = 256 * v_ if v_ < 8 else GATE_COL + 24 + 256 * (v_ - 8)
                src = A["w_in"][l, :, col:col + 256].rearrange("(c p) n -> p c n", p=P)
                return [(v[:, 4 * i:4 * i + 4], src[:, 4 * i:4 * i + 4]) for i in range(2)]
            v_ -= QKV_UNITS
            if v_ < 18:
                i, half, part = v_ // 6, v_ // 3 % 2, v_ % 3
                v = r.rearrange("p (c n) -> p c n", n=512)
                if part < 2:
                    c0 = MERGE_COL + i * D + half * 512
                    src = A["w_in"][l, part * 512:part * 512 + 512, c0:c0 + 512]
                else:
                    src = A["w_branch"][l, i, :, half * 512:half * 512 + 512]
                src = src.rearrange("(c p) n -> p c n", p=P)
                return [(v[:, 2 * e:2 * e + 2], src[:, 2 * e:2 * e + 2]) for e in range(2)]
            v_ -= 18
            rows = A["w_out"][l, v_ * 256:v_ * 256 + 256, :].rearrange("(c p) n -> p c n", p=P)
            v = r.rearrange("p (c n) -> p c n", n=D)
            return [(v[:, c], rows[:, c]) for c in range(2)]

        @block.sync
        def _(sp):
            sp.dma_start(ident[:, :], A["k_ident"]).then_inc(ident_in, 16)
            sp.dma_start(arena[0:KC, 12288:12288 + P], A["c"].rearrange("b (c p) -> (b c) p", p=P)).then_inc(c_in, 16)
            sp.dma_start(buckets[0:33].rearrange("r a b -> r (a b)"), A["k_buckets"]).then_inc(setup_in[1], 16)
            sp.dma_start(rel[0:32], A["rel_bias"]).then_inc(setup_in[1], 16)

            def first_modulation(n):
                if n >= 4:
                    sp.wait_ge(ada_done, n - 3)
                b, k = n // KC, n % KC
                sp.dma_start(ada_raw[:, n % 4, :],
                             A["ada_w"][0, k * P:k * P + P, b * D:b * D + D]).then_inc(ada_full[n % 4], 16)

            for n in range(4):
                first_modulation(n)
            sp.dma_start(x[:, :, :], A["x"][0].rearrange("(t p) d -> p t d", p=P)).then_inc(x_in, 16)
            sp.dma_start(arena[0:48, 12416:12416 + P],
                         A["ln_pre"].rearrange("l s (c p) -> (l s c) p", p=P)).then_inc(setup_in[0], 16)
            sp.dma_start(arena[0:48, 12544:12544 + P],
                         A["ln_post"].rearrange("l s (c p) -> (l s c) p", p=P)).then_inc(setup_in[0], 16)
            sp.dma_start(arena[0:72, 12672:12672 + 2 * P].rearrange("r (l p) -> r l p", p=P),
                         A["ada_b"].rearrange("l (r p) -> r l p", p=P)).then_inc(setup_in[0], 16)
            sp.dma_start(arena[0:DH, 12928:12928 + 2 * DH].rearrange("r (l d) -> r l d", d=DH),
                         A["cmp_pos"].rearrange("l k j d -> (k j) l d")).then_inc(setup_in[0], 16)
            for n in range(4, 16):
                first_modulation(n)

            def load(l, k, j=None):
                sp.wait_ge(lo_ready, unit_of(l, k) + 1)
                for dst, src in unit_parts(k, l, j):
                    sp.dma_start(dst, src).then_inc(raw_full[k % RING], 16)

            def ffn(l, f):
                k0 = f * (FFN_UNITS + MIX_UNITS)
                load(l, k0, ("GA", 0))
                load(l, k0 + 1, ("GB", 0))

                def step(j, ada_1=None, ada_0=None):
                    for i, kind in enumerate(("GA", "GB", "D")):
                        sp.wait_ge(lo_ready, unit_of(l, k0 + i) + j * 3)
                        for dst, src in unit_parts(k0 + 2 + i, l, (kind, j - 1 if kind == "D" else j)):
                            sp.dma_start(dst, src).then_inc(raw_full[(k0 + 2 + i) % RING], 16)
                        if i == ada_1:
                            ada_load(j - 2, 1)
                        if i == ada_0:
                            ada_load(j - 1, 0)

                def ada_load(j, half):
                    if f == 0:
                        ada_half_load(j, half)
                    else:
                        with sp.If(l < DEPTH - 1):
                            ada_half_load(j, half)

                def ada_half_load(j, half):
                    w = ada_width(f)
                    lw, col = (l, MOD) if f == 0 else ((l + 1) % DEPTH, 0)
                    sp.wait_ge(ada_sums, ada_before(l, f, j) + 4 * half - 4 + SUMS_AHEAD)
                    sp.dma_start(ada_view(f, half),
                                 A["ada_w"][lw, 4 * P * half:4 * P * half + 4 * P, bass.ds(col + (j - 1) * w, w)]
                                 .rearrange("(c p) n -> p c n", p=P)).then_inc(ada_half[half], 16)

                step(1)
                sp.wait_ge(ada_done, 24)
                step(2, ada_0=2)
                with sp.Fori(3, ADA_STEPS + 2) as j:
                    step(j, ada_1=0, ada_0=2)
                step(ADA_STEPS + 2, ada_1=0)
                load(l, k0 + FFN_UNITS - 1, ("D", FSTEPS - 1))

            with sp.Fori(0, DEPTH) as l:
                ffn(l, 0)
                for v in range(MIX_UNITS):
                    if v == 3:
                        sp.wait_ge(rows_ps, l * 4 + 3)
                        for e in range(2):
                            rows = A["cmp_w1"][l, e].rearrange("(c p) h -> p c h", p=P)
                            for half in range(2):
                                cs = slice(8 * half, 8 * half + 8)
                                sp.dma_start(w1[:, e, cs], rows[:, cs]).then_inc(w1_in, 16)
                        for e in range(2):
                            sp.dma_start(w2k[:, e, :], A["cmp_w2"][l, 0]).then_inc(w1_in, 16)
                        sp.dma_start(w2v[:, :], A["cmp_w2"][l, 1]).then_inc(w1_in, 16)
                        sp.dma_start(g_raw[:, :, :], A["w_in"][l, :, GATE_COL:GATE_COL + 24].rearrange("(c p) n -> p c n", p=P)).then_inc(bg_in, 16)
                    load(l, FFN_UNITS + v)
                    if v in MIX_ADA_LOAD:
                        k = MIX_ADA_LOAD[v]
                        if k >= 2:
                            sp.wait_ge(mix_sums, l * KC + k - 1)
                        else:
                            sp.wait_ge(sc_done, l * NJ + (8, 24)[k])
                        sp.dma_start(mix_raw[k % 2], A["ada_w"][l, k * P:k * P + P, 2 * MOD + D:3 * MOD]).then_inc(mix_ada[k % 2], 16)
                ffn(l, 1)
            for t in range(TOK):
                sp.wait_ge(x_done, DEPTH * NSUB * TOK + t + 1)
                sp.dma_start(out[0, t * P:t * P + P, :], x[:, t, :]).then_inc(out_sem, 16)
            sp.wait_ge(out_sem, 16 * TOK)

        @block.gpsimd
        def _(pool):
            pool.memset(sel[:, 0:31], 0.0)
            pool.memset(sel[:, 32:63], 0.0)
            pool.memset(sel[:, 31:32], 1.0).then_inc(setup_in[3], 1)
            pool.memset(neg_ones[:, :], -1.0).then_inc(setup_in[3], 1)
            pool.memset(eps_t[:, :], EPS).then_inc(setup_in[3], 1)
            pool.memset(hid_v[:, :, :, :], 0.0).then_inc(setup_in[3], 1)
            pool.memset(cmp_p[:, :, :], 0.0).then_inc(setup_in[3], 1)
            for n in range(16, 24):
                pool.wait_ge(ada_done, n - 3)
                k = n % KC
                pool.dma_start(ada_raw[:, n % 4, :], A["ada_w"][0, k * P:k * P + P, 2 * D:3 * D]).then_inc(ada_gate[n % 4], 16)
            for dst, src in ((neg_tri, "k_negtri"), (causal01, "k_causal01"), (causal_neg, "k_causalneg")):
                pool.dma_start(dst[:, :], A[src]).then_inc(const_in, 16)
            pool.dma_start(cmp_neg[:, :, :], A["k_cmpneg"]).then_inc(const_in, 16)
            pool.dma_start(cmp_01[:, :, :], A["k_cmp01"]).then_inc(const_in, 16)
            pool.dma_start(sink[:, :, :].rearrange("p l h -> p (l h)"),
                          A["attn_sinks"].rearrange("l h -> (l h)").unsqueeze(0).to_broadcast([P, DEPTH * HEADS])).then_inc(const_in, 16)

        @block.scalar
        def _(act):
            own = Own(act, act_own)

            def hi_parts(l, k):
                u = unit_of(l, k)
                act.wait_ge(raw_full[k % RING], l * (16 * LOADS * LAYER_UNITS // RING) + 16 * LOADS * (k // RING + 1) )
                act.wait_ge(unit_used, u + 1)
                act.activation(w_hi[:, k % RING, :], w_raw[:, k % RING, :], ACT.Copy).then_inc(hi_ready, 1)

            def rms_of_x(l, s, t):
                act.wait_ge(x_done, l * 6 + 2 * s + t + 1)
                own.done(act.activation(xs[:, t, :], x[:, t, :], ACT.Square, accum_out=stat[:, t:t + 1]))
                act.activation(stat[:, 2 + t:3 + t], stat[:, t:t + 1], ACT.Sqrt, scale=1.0 / D,
                               bias=eps_t[:, 0:1]).then_inc(xrms_done, 1)

            def rms_of_y(l, s, t):
                if t == 0:
                    act.wait_ge(y_half, l * NSUB + s + 1)
                else:
                    act.wait_ge(unit_used, used(l, (FFN_UNITS, FFN_UNITS + MIX_UNITS, LAYER_UNITS)[s] - 1))
                own.done(act.activation(junk.rearrange("p (a b) -> p a b", b=512), ps[:, 2 * t:2 * t + 2, :],
                                        ACT.Square, accum_out=stat[:, 4 + t:5 + t]))
                act.activation(stat[:, 6 + t:7 + t], stat[:, 4 + t:5 + t], ACT.Sqrt, scale=1.0 / D,
                               bias=eps_t[:, 0:1]).then_inc(yrms_done, 1)

            def scale_x(l, s, t):
                act.wait_ge(xinv_ready, (l * NSUB + s) * 2 + t + 1)
                act.activation(xs[:, t, :], x[:, t, :], ACT.Copy, scale=stat[:, t:t + 1]).then_inc(xs_ready, 1)

            def split_h(l, s):
                for half in range(2):
                    part = h_part(half, 0)
                    act.wait_ge(h32_ready, (l * NSUB + s) * 2 + half + 1)
                    act.activation(h_hi[part], hbuf[part], ACT.Copy).then_inc(hhi_ready, 1)
                    act.wait_ge(h_ps, (l * NSUB + s) * 4 + 2 + half + 1)
                    for c in range(4):
                        kc = 4 * half + c
                        ins = act.activation(hbuf[:, kc, P:S], ps[:, 2 + half, c * P:c * P + P], ACT.Identity,
                                             scale=mod_a[:, s % 3, kc:kc + 1], bias=modc[:, s % 3, kc:kc + 1])
                    own.done(ins)
                    part = h_part(half, 1)
                    act.activation(h_hi[part], hbuf[part], ACT.Copy).then_inc(hhi_ready, 1)

            def sqrt_table():
                own.done(act.activation(jst[:, 0, 11:12], eps_t[:, 0:1], ACT.Sqrt))

            def boundary(l, s):
                sqrt_table()
                for t in range(TOK):
                    rms_of_y(l, s, t)
                for t in range(TOK):
                    rms_of_x(l, s + 1, t)
                    scale_x(l, s + 1, t)
                act.wait_ge(mod_made, mods_before(l, s + 1))
                split_h(l, s + 1)

            def ffn(l, f):
                k0 = f * (FFN_UNITS + MIX_UNITS)

                def step(j, end, units):
                    n = (l * 2 + f) * FSTEPS
                    for t in range(TOK):
                        if t == 0:
                            act.wait_ge(gu_done, n + j + 1)
                        else:
                            act.wait_ge(unit_used, used(l, k0) + end)
                        act.activation(ffn_s[:, t, :], ps[:, GU + t, 0:FB], ACT.Silu).then_inc(silu_done, 1)
                    units(0)
                    units(1)
                    act.wait_ge(at_ps, n + j + 1)
                    act.activation(act_hi[:, 0, 0:2, :], ps[:, TB, :].rearrange("p (a b) -> p a b", b=S),
                                   ACT.Copy).then_inc(ahi_ready, 1)
                    units(2)

                step(0, 1, lambda i: hi_parts(l, k0 + 3 + i))
                with act.Fori(1, FSTEPS - 1) as j:
                    def units(i):
                        k = k0 + 3 + i
                        act.wait_ge(raw_full[k % RING], l * (16 * LOADS * LAYER_UNITS // RING) + j * (16 * LOADS) + 16 * LOADS * (k // RING + 1))
                        act.wait_ge(unit_used, unit_of(l, k) + j * 3 + 1)
                        act.activation(w_hi[:, k % RING, :], w_raw[:, k % RING, :], ACT.Copy).then_inc(hi_ready, 1)
                    step(j, 3 * j, units)
                def next_units(i):
                    if i == 2:
                        return
                    if f == 0:
                        hi_parts(l, k0 + FFN_UNITS + i)
                    else:
                        with act.If(l < DEPTH - 1):
                            hi_parts(l, LAYER_UNITS + i)

                step(FSTEPS - 1, 3 * FSTEPS - 3, next_units)

            def front(l, n):
                kind, h = JOBS[n]
                b = n % 2
                if kind == "c":
                    act.wait_ge(sc_done, l * NJ + n + 1)
                    if n >= 26:
                        act.wait_ge(p_ready, l * NJ + n - 1)
                    own.done(act.activation(job_s[:, b, :], ps[:, SB + b, 0:3 * P], ACT.Abs))
                    own.counted(act.activation(job_s[:, b, :], job_s[:, b, :], ACT.Exp, scale=-1.0))
                    return
                act.wait_ge(s_ready, l * 24 + n + 1)
                if n >= 2:
                    act.wait_ge(mid_done, l * NJ + n - 1)
                st = jst[:, b, :]
                act.activation(job_p[:, b, 0:P], job_s[:, b, 0:P], ACT.Exp, bias=st[:, 2:3], accum_out=st[:, 4:5])
                if kind == "a":
                    act.activation(st[:, 6:8], st[:, 2:4], ACT.Exp, bias=sink[:, bass.ds(l, 1), h])
                act.activation(job_p[:, b, P:3 * P], job_s[:, b, P:3 * P], ACT.Exp, bias=st[:, 3:4],
                               accum_out=st[:, 5:6]).then_inc(front_done, 1)

            def back(l, n):
                b = n % 2
                if JOBS[n][0] == "c":
                    act.wait_ge(mask_done, l * HEADS + n - 24 + 1)
                    act.activation(job_t[:, b, :], job_t[:, b, :], ACT.Exp).then_inc(pt_ready, 1)
                    return
                act.wait_ge(mid_done, l * NJ + n + 1)
                if n >= 2:
                    act.wait_ge(pv_done, l * NJ + n - 1)
                act.activation(job_t[:, b, :], ps[:, MID, 0:3 * P], ACT.Copy).then_inc(pt_ready, 1)

            def pair_out(l, n):
                q = pair_done(n)
                if q is None:
                    return
                act.wait_ge(pv_done, l * NJ + n + 1)
                act.activation(branch_in(q // 4, q % 4)[0], ps[:, OB, 0:S], ACT.Copy).then_inc(y_hi, 1)

            def jobs(l, step):
                for n in job_slots(step):
                    if 4 <= n:
                        pair_out(l, n - 4)
                for n in job_slots(step):
                    if 2 <= n < NJ + 2:
                        back(l, n - 2)
                    if n < NJ:
                        front(l, n)
                    if n % 2 == 0 and n >= 3 * HEADS:
                        hi_parts(l, FFN_UNITS + step + 3)
                for n in job_slots(step):
                    if n < NJ and JOBS[n][0] == "c":
                        if n % 2 == 0:
                            act.wait_ge(act_own, own.base + own.n)
                        b = n % 2
                        act.activation(job_s[:, b, :], job_s[:, b, :], ACT.Ln, bias=1.0).then_inc(front_done, 1)

            act.wait_ge(setup_in[3], 5)
            act.wait_ge(setup_dve, 1)
            act.activation(c_act[:, :], stat[:, 8:16], ACT.Silu).then_inc(setup_in[3], 1)
            act.wait_ge(setup_dve, 3)
            act.dma_start(A["scratch"][:, :, :].rearrange("a h n -> h a n"), vec[0:8, :, 0:384]).then_inc(scratch_out, 16)
            act.dma_start(flip, A["k_flip"]).then_inc(flip_in, 16)
            act.wait_ge(scratch_out, 16)
            sc = A["scratch"]
            for i in range(2):
                act.dma_start(bias[:, HEADS * i:HEADS * i + HEADS, :],
                              bass.AP(tensor=sc.tensor, offset=i * 8 * 384, ap=[[1, P], [384, 8], [1, 256]])).then_inc(setup_in[2], 16)
            act.wait_ge(x_in, 16)
            sqrt_table()
            for t in range(TOK):
                rms_of_x(0, 0, t)
            for i in range(4):
                act.wait_ge(setup_pe, 9 + i)
                act.activation(bias[:, 4 * i:4 * i + 4, :].rearrange("p a b -> p (a b)").rearrange("p (a b) -> p a b", b=512),
                               ps[:, 4 + 2 * (i % 2):6 + 2 * (i % 2), :], ACT.Copy).then_inc(setup_act, 1)
            for t in range(TOK):
                scale_x(0, 0, t)
            hi_parts(0, 0)
            hi_parts(0, 1)
            act.wait_ge(mod_made, mods_before(0, 0))
            split_h(0, 0)
            hi_parts(0, 2)
            own.end()
            with act.Fori(0, DEPTH) as l:
                own.n, own.base = 0, l * OWN + OWN
                ffn(l, 0)
                boundary(l, 0)
                hi_parts(l, FFN_UNITS + 2)
                act.wait_ge(const_in, 6 * 16)
                for v in range(MIX_UNITS):
                    if v < QKV_UNITS:
                        if v not in (2, 5, 6, 7):
                            act.wait_ge(unit_used, used(l, FFN_UNITS + v))
                            bank = ps[:, QB + v % 2, :]
                            if v in (0, 1, 3, 4, 8, 9):
                                dst = {0: aq, 1: aq, 3: bq, 4: bq, 8: cq, 9: cq}[v]
                                b0 = {0: 0, 1: 2, 3: 0, 4: 2, 8: 0, 9: 2}[v]
                                act.activation(dst[:, b0:b0 + 2, :], bank.rearrange("p (a b) -> p a b", b=S),
                                               ACT.Copy, scale=DH ** -0.5).then_inc(q_out_act, 1)
                            elif v in (10, 11):
                                act.activation(ck[:, 2 * (v - 10):2 * (v - 10) + 2, :],
                                               bank.rearrange("p (a b) -> p a b", b=S), ACT.Copy).then_inc(q_out_act, 1)
                            else:
                                act.activation(cv[:, :, 256 * (v - 12):256 * (v - 12) + 256],
                                               bank.rearrange("p (t n) -> p t n", t=TOK), ACT.Copy).then_inc(q_out_act, 1)
                    if v == 5:
                        act.wait_ge(bg_in, l * 16 + 16)
                        act.activation(g_hi[:, :, :], g_raw[:, :, :], ACT.Copy).then_inc(bg_hi, 1)
                    if v == 6:
                        act.wait_ge(hid_ps, l + 1)
                        act.activation(hid_rows, ps[0:2 * NCMP, MB, 0:2 * P].rearrange("n (k h) -> n k h", k=2),
                                       ACT.Gelu_apprx_tanh).then_inc(hid_ready, 1)
                    if v == 7:
                        act.wait_ge(bg_ps, l + 1)
                        act.activation(gate_exp, ps[0:24, MB + 1, 0:S], ACT.Exp, scale=-1.0).then_inc(bg_exp, 1)
                    if v == 9:
                        act.wait_ge(cs_ready, l + 1)
                        act.activation(cmp_p[:, :, 0:NCMP], cmp_p[:, :, 0:NCMP], ACT.Exp).then_inc(cexp_done, 1)
                    if v == 10:
                        act.wait_ge(cpt_ps, l + 1)
                        act.activation(cmp_pt[:, :, :, :], ps[:, MB + 1, :].rearrange("p (g t q) -> p g t q", g=2, t=2),
                                       ACT.Copy).then_inc(cpt_ready, 1)
                    if 14 <= v < 32 and (v - 14) % 3 == 1:
                        it = (v - 14) // 3
                        for t in range(TOK):
                            if t == 0:
                                act.wait_ge(mg_ps, l * 6 + it + 1)
                            else:
                                act.wait_ge(unit_used, used(l, FFN_UNITS + v))
                            if it:
                                act.wait_ge(br_read, (l * 6 + it) * 2)
                            act.activation(mg[:, t, :], ps[:, MB + t, :], ACT.Sigmoid).then_inc(mg_ready, 1)
                    jobs(l, v)
                    if v in (30, 32):
                        for q in range(2):
                            act.wait_ge(m_ps, l * 4 + (v - 30) + q + 1)
                            dst = act_hi[:, 1, 2 * q:2 * q + 2, :] if v == 30 else h_hi[:, 4 + 2 * q:6 + 2 * q, :]
                            act.activation(dst, ps[:, MID + q, :].rearrange("p (a b) -> p a b", b=S),
                                           ACT.Copy).then_inc(mhi_ready, 1)
                    if v < MIX_UNITS - 1 and not any(n >= 3 * HEADS for n in job_slots(v)):
                        hi_parts(l, FFN_UNITS + v + 3)
                boundary(l, 1)
                hi_parts(l, FFN_UNITS + MIX_UNITS + 2)
                ffn(l, 1)
                before = own.n
                with act.If(l < DEPTH - 1):
                    boundary(l, 2)
                    own.end()
                    hi_parts(l, LAYER_UNITS + 2)
            own.n, own.base = before, DEPTH * OWN
            sqrt_table()
            for t in range(TOK):
                rms_of_y(DEPTH - 1, 2, t)

        @block.vector
        def _(dve):
            own = Own(dve, dve_own)
            mods = Own(dve, mod_made)

            def lo_parts(l, k):
                u = unit_of(l, k)
                dve.wait_ge(hi_ready, u + 1)
                dve.tensor_tensor(w_lo[:, k % RING, :], w_raw[:, k % RING, :], w_hi[:, k % RING, :].bitcast(F32),
                                  ALU.subtract).then_inc(lo_ready, 1)

            def rows_out(n, r):
                dve.wait_ge(rows_ps, n)
                dve.tensor_copy(rows[0:r, :], ps[0:r, MODB, 0:P]).then_inc(rows_ready, 1)

            def shift(l, s, at):
                c0 = (l * NSUB + s) * 24
                mods.counted(dve.tensor_tensor(modc[:, s, 0:KC], ps[:, MODB, 256 + at:256 + at + KC], adab_t[:, bass.ds(c0, KC)], ALU.add))

            def gain(l, s, at):
                c0 = (l * NSUB + s) * 24 + KC
                g0 = (l * NSUB + s) * KC
                mods.done(dve.tensor_tensor(modc[:, s, KC:2 * KC], ps[:, MODB, 256 + at:256 + at + KC], adab_t[:, bass.ds(c0, KC)], ALU.add))
                mods.counted(dve.scalar_tensor_tensor(out=mod_a[:, s, :], in0=modc[:, s, KC:2 * KC], scalar=1.0,
                                                  in1=ln_t[:, 0, bass.ds(g0, KC)], op0=ALU.add, op1=ALU.mult))

            def gate(l, s, at):
                c0 = (l * NSUB + s) * 24 + 2 * KC
                g0 = (l * NSUB + s) * KC
                mods.done(dve.tensor_tensor(mod_g[:, s, :], ps[:, MODB, 256 + at:256 + at + KC], adab_t[:, bass.ds(c0, KC)], ALU.add))
                dve.scalar_tensor_tensor(out=mod_g[:, s, :], in0=mod_g[:, s, :],
                                         scalar=1.0 if s == 1 else 0.5,
                                         in1=ln_t[:, 1, bass.ds(g0, KC)], op0=ALU.mult, op1=ALU.mult).then_inc(mod_ready, 1)

            def gate_turned(s, n):
                dve.wait_ge(gt_ps, n)
                dve.tensor_copy(gt[:, s % 2, :], ps[0:KC, MODB, 384:512]).then_inc(gt_ready, 1)

            def invert_x(l, s, t):
                dve.wait_ge(xrms_done, (l * NSUB + s) * 2 + t + 1)
                dve.reciprocal(stat[:, t:t + 1], stat[:, 2 + t:3 + t]).then_inc(xinv_ready, 1)

            def split_h(l, s):

                def shift_h(half):
                    dve.wait_ge(h_ps, (l * NSUB + s) * 4 + half + 1)
                    for c in range(4):
                        kc = 4 * half + c
                        ins = dve.tensor_scalar(out=hbuf[:, kc, 0:P], in0=ps[:, half, c * P:c * P + P],
                                                scalar1=mod_a[:, s % 3, kc:kc + 1], scalar2=modc[:, s % 3, kc:kc + 1],
                                                op0=ALU.mult, op1=ALU.add)
                    ins.then_inc(h32_ready, 1)

                def low_h(half, t):
                    dve.wait_ge(hhi_ready, (l * NSUB + s) * 4 + 2 * half + t + 1)
                    part = h_part(half, t)
                    dve.tensor_tensor(h_lo[part], hbuf[part], h_hi[part].bitcast(F32), ALU.subtract).then_inc(hlo_ready, 1)

                shift_h(0)
                low_h(0, 0)
                shift_h(1)
                low_h(0, 1)
                low_h(1, 0)
                low_h(1, 1)

            def gate_copy(l, s):
                dve.wait_ge(g_ps, l * NSUB + s + 1)
                own.counted(dve.tensor_copy(gate_sb, ps[:, GU:GU + 2, :]))

            def residual(l, s, t, between=None):
                dve.wait_ge(yrms_done, (l * NSUB + s) * 2 + t + 1)
                own.done(dve.reciprocal(stat[:, 4 + t:5 + t], stat[:, 6 + t:7 + t]))
                own.counted(dve.scalar_tensor_tensor(out=xs[:, t, :].rearrange("p (a b) -> p a b", b=512),
                                                     in0=ps[:, 2 * t:2 * t + 2, :], scalar=stat[:, 4 + t:5 + t],
                                                     in1=gate_sb, op0=ALU.mult, op1=ALU.mult))
                if between:
                    between()
                dve.wait_ge(dve_own, own.base + own.n)
                dve.tensor_tensor(x[:, t, :], x[:, t, :], xs[:, t, :], ALU.add).then_inc(x_done, 1)

            def boundary(l, s):
                residual(l, s, 0)
                residual(l, s, 1, lambda: invert_x(l, s + 1, 0))
                invert_x(l, s + 1, 1)
                dve.wait_ge(mod_made, mods_before(l, s + 1))
                split_h(l, s + 1)

            def ffn(l, f):
                k0 = f * (FFN_UNITS + MIX_UNITS)

                def step(j, units, sums=lambda pair: None):
                    n = (l * 2 + f) * FSTEPS
                    for t in range(TOK):
                        dve.wait_ge(silu_done, n * 2 + j * 2 + t + 1)
                        dve.tensor_tensor(ffn_a[:, t, :], ffn_s[:, t, :], ps[:, GU + t, FB:2 * FB], ALU.mult).then_inc(act_done, 1)
                    sums(0)
                    units(0)
                    sums(1)
                    units(1)
                    dve.wait_ge(ahi_ready, n + j + 1)
                    dve.tensor_tensor(act_lo[:, 0, 0:2, :], ps[:, TB, :].rearrange("p (a b) -> p a b", b=S),
                                      act_hi[:, 0, 0:2, :].bitcast(F32), ALU.subtract).then_inc(alo_ready, 1)
                    sums(2)
                    units(2)
                    sums(3)

                def first_gate(i):
                    if f == 0 and i < 2:
                        with dve.If(l < 1):
                            for n in range(16 + 4 * i, 20 + 4 * i):
                                first_sum(n)
                    if f == 0 and i == 1:
                        rows_out(l * 4 + 2, KC)
                    if f == 0 and i == 2:
                        dve.wait_ge(cols_ps, l * 4 + 2)
                        gate(l, 0, 0)
                    if f == 0 and i == 3:
                        gate_turned(0, l * 3 + 1)

                first_gate(0)
                step(0, lambda i: lo_parts(l, k0 + 3 + i), lambda i: first_gate(i) if i else None)

                def loop_step(j, ada):
                    def units(i):
                        k = k0 + 3 + i
                        dve.wait_ge(hi_ready, unit_of(l, k) + j * 3 + 1)
                        dve.tensor_tensor(w_lo[:, k % RING, :], w_raw[:, k % RING, :], w_hi[:, k % RING, :].bitcast(F32),
                                          ALU.subtract).then_inc(lo_ready, 1)

                    def sums(pair):
                        if ada and f == 0:
                            ada_sum(j, pair)
                        elif ada:
                            with dve.If(l < DEPTH - 1):
                                ada_sum(j, pair)
                    step(j, units, sums)

                def ada_sum(j, pair):
                    w = ada_width(f)
                    acc = ada_acc[:, bass.ds((j - 1) * w, w)]
                    half = pair // 2
                    src = ada_view(f, half)
                    if pair % 2 == 0:
                        dve.wait_ge(ada_half[half], ((l * 2 + f) * ADA_STEPS + j) * 16)
                    for c in (2 * (pair % 2), 2 * (pair % 2) + 1):
                        k = 4 * half + c
                        if k == 0:
                            ins = dve.tensor_scalar(out=acc, in0=src[:, c], scalar1=c_act[:, k:k + 1], scalar2=None, op0=ALU.mult)
                        else:
                            dve.wait_ge(ada_sums, ada_before(l, f, j) + k + SUMS_AHEAD)
                            ins = dve.scalar_tensor_tensor(out=acc, in0=src[:, c], scalar=c_act[:, k:k + 1], in1=acc,
                                                           op0=ALU.mult, op1=ALU.add)
                        ins.then_inc(ada_sums, 1)

                with dve.Fori(1, ADA_STEPS + 1) as j:
                    loop_step(j, True)
                with dve.Fori(ADA_STEPS + 1, FSTEPS - 1) as j:
                    loop_step(j, False)
                def next_units(i):
                    if i == 2:
                        return
                    if f == 0:
                        lo_parts(l, k0 + FFN_UNITS + i)
                    else:
                        with dve.If(l < DEPTH - 1):
                            lo_parts(l, LAYER_UNITS + i)

                def modulation(i):
                    if f == 0:
                        if i == 2:
                            rows_out(l * 4 + 3, 32)
                        if i == 3:
                            gate_copy(l, 0)
                            dve.wait_ge(cols_ps, l * 4 + 3)
                            shift(l, 1, 0)
                            shift(l, 2, 3 * KC)
                            gain(l, 1, KC)
                            gate(l, 1, 2 * KC)
                        return
                    if i == 3:
                        gate_copy(l, 2)
                    if i in (2, 3):
                        with dve.If(l < DEPTH - 1):
                            if i == 2:
                                rows_out(l * 4 + 5, 16)
                            else:
                                dve.wait_ge(cols_ps, l * 4 + 5)
                                shift((l + 1) % DEPTH, 0, 0)
                                gain((l + 1) % DEPTH, 0, KC)

                step(FSTEPS - 1, next_units, modulation)

            def front(l, n):
                kind, h = JOBS[n]
                if kind == "c":
                    return
                b = n % 2
                st = jst[:, b, :]
                row = bias[:, h if kind == "a" else HEADS + h, :]
                dve.wait_ge(sc_done, l * NJ + n + 1)
                dve.tensor_tensor(job_s[:, b, 0:P], ps[:, SB + b, 0:P], row[:, P:2 * P], ALU.add)
                dve.tensor_tensor(job_s[:, b, P:3 * P], ps[:, SB + b, P:3 * P], row, ALU.add).then_inc(s_read, 1)
                dve.wait_ge(s_read, l * NJ + n + 1)
                dve.tensor_reduce(st[:, 0:1], job_s[:, b, 0:P], axis=AX.X, op=ALU.max)
                own.done(dve.tensor_reduce(st[:, 1:2], job_s[:, b, P:3 * P], axis=AX.X, op=ALU.max))
                if kind == "a":
                    dve.tensor_scalar(out=st[:, 2:4], in0=st[:, 0:2], scalar1=sink[:, bass.ds(l, 1), h], scalar2=-1.0,
                                      op0=ALU.max, op1=ALU.mult).then_inc(s_ready, 1)
                else:
                    dve.tensor_scalar(out=st[:, 2:4], in0=st[:, 0:2], scalar1=-1.0, scalar2=None,
                                      op0=ALU.mult).then_inc(s_ready, 1)

            def middle(l, n):
                kind, h = JOBS[n]
                b = n % 2
                st = jst[:, b, :]
                dve.wait_ge(front_done, l * NJ + n + 1)
                if kind == "c":
                    if n >= 26:
                        dve.wait_ge(mid_done, l * NJ + n - 1)
                    dve.scalar_tensor_tensor(out=job_p[:, b, :], in0=ps[:, SB + b, 0:3 * P], scalar=0.0,
                                             in1=job_s[:, b, :], op0=ALU.max, op1=ALU.add)
                    dve.tensor_tensor(job_z[b], ps[:, SB + b, 0:3 * P], causal_neg[:, :], ALU.add).then_inc(s_read, 1)
                    dve.wait_ge(s_read, l * NJ + n + 1)
                    dve.tensor_tensor(job_p[:, b, :], job_p[:, b, :], causal01[:, :], ALU.mult).then_inc(p_ready, 1)
                    return
                if kind == "a":
                    own.done(dve.tensor_tensor(st[:, 4:6], st[:, 4:6], st[:, 6:8], ALU.add))
                own.done(dve.reciprocal(st[:, 8:10], st[:, 4:6]))
                if kind != "a":
                    c0 = HEADS * (1 if kind == "slc" else 2) + h
                    own.done(dve.tensor_tensor(st[:, 8:10], st[:, 8:10], bgate[:, :, c0], ALU.mult))
                dve.tensor_scalar(out=job_p[:, b, 0:P], in0=job_p[:, b, 0:P], scalar1=st[:, 8:9], scalar2=None, op0=ALU.mult)
                dve.tensor_scalar(out=job_p[:, b, P:3 * P], in0=job_p[:, b, P:3 * P], scalar1=st[:, 9:10], scalar2=None,
                                  op0=ALU.mult).then_inc(p_ready, 1)

            def mask(l, n):
                dve.wait_ge(mid_done, l * NJ + n + 1)
                dve.wait_ge(pv_done, l * NJ + n - 1)
                dve.tensor_tensor(job_t[:, n % 2, :], ps[:, MID, 0:3 * P], job_z[n % 2], ALU.add).then_inc(mask_done, 1)

            def pair_out(l, n):
                q = pair_done(n)
                if q is None:
                    return
                dve.wait_ge(y_hi, l * 12 + q + 1)
                hi, lo = branch_in(q // 4, q % 4)
                dve.tensor_tensor(lo, ps[:, OB, 0:S], hi.bitcast(F32), ALU.subtract).then_inc(y_lo, 1)

            def jobs(l, step):
                for n in job_slots(step):
                    if 4 <= n:
                        pair_out(l, n - 4)
                for n in job_slots(step):
                    if 2 <= n < NJ + 2 and JOBS[n - 2][0] == "c":
                        mask(l, n - 2)
                    if n < NJ:
                        front(l, n)
                if any(n >= 3 * HEADS for n in job_slots(step)):
                    lo_parts(l, FFN_UNITS + step + 3)
                for n in job_slots(step):
                    if n < NJ:
                        middle(l, n)

            dve.sem_inc(lo_ready, RING)
            dve.sem_inc(ada_sums, SUMS_AHEAD)
            dve.sem_inc(x_done, TOK)
            dve.wait_ge(setup_pe, 1)
            dve.tensor_copy(stat[:, 8:16], ps[:, 0, 0:KC]).then_inc(setup_dve, 1)
            dve.wait_ge(setup_in[1], 32)
            dve.memset(rel[32:33], 1.0).then_inc(setup_dve, 1)
            dve.wait_ge(setup_pe, 2)
            dve.tensor_copy(vec[0:8, :, 0:384], ps[0:8, 2:4, 0:384]).then_inc(setup_dve, 1)
            dve.wait_ge(setup_in[3], 6)

            def first_sum(n):
                b, k = n // KC, n % KC
                acc = ada_acc[:, b * D:b * D + D]
                if b < 2:
                    dve.wait_ge(ada_full[n % 4], 16 * (n // 4 + 1))
                else:
                    dve.wait_ge(ada_gate[n % 4], 16 * (n // 4 - 3))
                if n:
                    dve.wait_ge(ada_done, n)
                if k == 0:
                    ins = dve.tensor_scalar(out=acc, in0=ada_raw[:, n % 4, :], scalar1=c_act[:, k:k + 1], scalar2=None, op0=ALU.mult)
                else:
                    ins = dve.scalar_tensor_tensor(out=acc, in0=ada_raw[:, n % 4, :], scalar=c_act[:, k:k + 1],
                                                   in1=acc, op0=ALU.mult, op1=ALU.add)
                ins.then_inc(ada_done, 1)

            for n in range(8):
                first_sum(n)
            dve.wait_ge(setup_pe, 8)
            dve.tensor_copy(ln_t[:, 0, :], ps[:, 1, 0:48])
            dve.tensor_copy(ln_t[:, 1, :], ps[:, 1, 64:112])
            dve.tensor_copy(adab_t[:, :].rearrange("p (l r) -> p l r", l=2),
                            ps[:, 1, 128:384].rearrange("p (l r) -> p l r", l=2)[:, :, 0:72])
            dve.tensor_copy(pos_t[:, :, :], ps[0:DH, 1, 384:512].rearrange("p (l r) -> p l r", l=2)).then_inc(setup_dve, 1)
            for n in range(8, 12):
                first_sum(n)
            for t in range(TOK):
                invert_x(0, 0, t)
            for n in range(12, 16):
                first_sum(n)
            lo_parts(0, 0)
            rows_out(1, 16)
            dve.wait_ge(cols_ps, 1)
            shift(0, 0, 0)
            gain(0, 0, KC)
            dve.wait_ge(mod_made, mods_before(0, 0))
            split_h(0, 0)
            for k in range(1, RING):
                lo_parts(0, k)
            own.end()
            with dve.Fori(0, DEPTH) as l:
                own.n, own.base = 0, l * OWN + OWN
                mods.n, mods.base = 0, l * 4 * NSUB + 3
                ffn(l, 0)
                boundary(l, 0)
                gate_turned(1, l * 3 + 2)
                lo_parts(l, FFN_UNITS + 2)
                dve.wait_ge(const_in, 6 * 16)
                for v in range(MIX_UNITS):
                    if v in (2, 5, 6, 7):
                        dve.wait_ge(unit_used, used(l, FFN_UNITS + v))
                        bank = ps[:, QB + v % 2, :]
                        if v == 5:
                            for g in range(2):
                                ins = dve.tensor_copy(kvin[:, :, g, :],
                                                      bank[DH * g:DH * g + DH, :].rearrange("p (k s) -> p k s", s=S))
                            ins.then_inc(q_out_dve, 1)
                        else:
                            for b, dst in enumerate({2: (ak,), 6: (bks, bkw), 7: ()}[v]):
                                for g in range(2):
                                    for half in range(2):
                                        ins = dve.tensor_copy(dst[DH * half:DH * half + DH, g, :],
                                                              bank[DH * g:DH * g + DH, b * S:b * S + S])
                            if v == 2:
                                ins = dve.tensor_copy(av[:, :, :], bank[:, S:2 * S].rearrange("p (t n) -> p t n", n=P))
                            if v == 7:
                                for b, dst in enumerate((bvs, bvw)):
                                    ins = dve.tensor_copy(dst[:, :, :],
                                                          bank.rearrange("p (t b n) -> p b t n", t=TOK, n=P)[:, b])
                            ins.then_inc(q_out_dve, 1)
                    if v == 5:
                        dve.wait_ge(q_out_dve, l * 4 + 2)
                        for e in range(2):
                            for half in range(2):
                                for g in range(2):
                                    a0 = kvin[:, e, g, :]
                                    src = bass.AP(tensor=a0.tensor, offset=a0.offset + half,
                                                  ap=[list(a0.ap[0]), [2, 16], [CMP_STRIDE, NCMP]])
                                    pp = pos_t[:, bass.ds(l, 1), e * CMP_BLOCK:(e + 1) * CMP_BLOCK]\
                                        .rearrange("p a (c r) -> p (a c) r", r=2)[:, :, half:half + 1].to_broadcast([DH, 16, NCMP])
                                    ins = dve.tensor_tensor(zc[DH * half:DH * half + DH, e, :, g * NCMP:(g + 1) * NCMP],
                                                            src, pp, ALU.add)
                        ins.then_inc(z_ready, 1)
                        dve.wait_ge(bg_hi, l + 1)
                        dve.tensor_tensor(g_lo[:, :, :], g_raw[:, :, :], g_hi[:, :, :].bitcast(F32), ALU.subtract).then_inc(bg_lo, 1)
                    if v == 7:
                        dve.wait_ge(hid_turned, l + 1)
                        ht = ps[:, MB, 256:320].rearrange("p (k m) -> p k m", k=2)[:, :, 0:2 * NCMP]
                        dve.tensor_copy(hid[:, :, :], ht[:, 0].rearrange("p (g n) -> p g n", g=2))
                        for g in range(2):
                            ins = dve.tensor_copy(hid_v[:, g, :, 0:NCMP],
                                                  ht[:, 1, g * NCMP:g * NCMP + NCMP].unsqueeze(1).to_broadcast([P, 4, NCMP]))
                        ins.then_inc(kc_ready, 1)
                        dve.wait_ge(bg_turned, l + 1)
                        own.done(dve.tensor_scalar(out=bgate[:, :, :], in0=ps[:, MB + 1, 256:304].rearrange("p (t n) -> p t n", n=24),
                                                   scalar1=1.0, scalar2=None, op0=ALU.add))
                        dve.reciprocal(bgate[:, :, :], bgate[:, :, :]).then_inc(bg_ready, 1)
                    if v == 8:
                        dve.wait_ge(kc_ps, l + 1)
                        dve.tensor_copy(kc_t[:, :, :], ps[:, MB, 128:128 + 2 * NCMP].rearrange("p (g n) -> p g n", g=2))
                        dve.tensor_copy(vc[:, :, :], ps[:, MB, 256:256 + 2 * DH].rearrange("p (g n) -> p g n", g=2)).then_inc(kc_ready, 1)
                    if v == 9:
                        dve.wait_ge(cs_ps, l + 1)
                        dve.wait_ge(bg_ready, l + 1)
                        cp = cmp_p[:, :, 0:NCMP]
                        for odd in range(2):
                            logits = ps[:, MB + 1 - odd, 0:256].rearrange("p (g t h n) -> p g t h n", g=2, t=TOK, n=32)
                            for g in range(2):
                                for t in range(TOK):
                                    r = (g * TOK + t) * 4 + odd
                                    ins = dve.tensor_tensor(cp[:, r:r + 3:2], logits[:, g, t, :, 0:NCMP],
                                                            cmp_neg[:, t:t + 1, :].to_broadcast([P, 2, NCMP]), ALU.add)
                        own.done(ins)
                        own.done(dve.tensor_reduce(cst[:, 0, :], cp, axis=AX.X, op=ALU.max))
                        dve.tensor_tensor(cp, cp, cst[:, 0, :].unsqueeze(2).to_broadcast([P, 16, NCMP]), ALU.subtract).then_inc(cs_ready, 1)
                        dve.wait_ge(cexp_done, l + 1)
                        for g in range(2):
                            for t in range(TOK):
                                r = (g * TOK + t) * 4
                                ins = dve.tensor_tensor(cp[:, r:r + 4], cp[:, r:r + 4],
                                                        cmp_01[:, t:t + 1, :].to_broadcast([P, 4, NCMP]), ALU.mult)
                        own.done(ins)
                        own.done(dve.tensor_reduce(cst[:, 1, :], cp, axis=AX.X, op=ALU.add))
                        own.done(dve.tensor_scalar(out=cst[:, 1, :], in0=cst[:, 1, :], scalar1=1e-30, scalar2=None, op0=ALU.max))
                        own.done(dve.reciprocal(cst[:, 2, :], cst[:, 1, :]))
                        for g in range(2):
                            ins = dve.tensor_tensor(cst[:, 2, 8 * g:8 * g + 8].rearrange("p (t h) -> p t h", h=4),
                                                    cst[:, 2, 8 * g:8 * g + 8].rearrange("p (t h) -> p t h", h=4),
                                                    bgate[:, :, 4 * g:4 * g + 4], ALU.mult)
                        own.done(ins)
                        dve.tensor_tensor(cp, cp, cst[:, 2, :].unsqueeze(2).to_broadcast([P, 16, NCMP]), ALU.mult).then_inc(cp_ready, 1)
                    if 14 <= v < 32 and (v - 14) % 3 == 2:
                        it = (v - 14) // 3
                        i, half = it // 2, it % 2
                        for t in range(TOK):
                            if t == 0:
                                dve.wait_ge(br_ps, l * 6 + it + 1)
                            else:
                                dve.wait_ge(unit_used, used(l, FFN_UNITS + v))
                            dve.wait_ge(mg_ready, (l * 6 + it) * 2 + t + 1)
                            m = merged[:, t, half * 512:half * 512 + 512]
                            if i == 0:
                                dve.tensor_tensor(m, mg[:, t, :], branch_out(it, t), ALU.mult).then_inc(br_read, 1)
                            else:
                                dve.tensor_tensor(mg[:, t, :], mg[:, t, :], branch_out(it, t), ALU.mult).then_inc(dve_own, 1)
                                own.n += 1
                                dve.wait_ge(dve_own, own.base + own.n)
                                dve.tensor_tensor(m, m, mg[:, t, :], ALU.add).then_inc(br_read, 1)
                    jobs(l, v)
                    if v == 30:
                        gate_turned(2, l * 3 + 3)
                    if v in (30, 32):
                        for q in range(2):
                            dve.wait_ge(mhi_ready, l * 4 + (v - 30) + q + 1)
                            lo, hi = ((act_lo[:, 1, 2 * q:2 * q + 2, :], act_hi[:, 1, 2 * q:2 * q + 2, :]) if v == 30 else
                                      (h_lo[:, 4 + 2 * q:6 + 2 * q, :], h_hi[:, 4 + 2 * q:6 + 2 * q, :]))
                            dve.tensor_tensor(lo, ps[:, MID + q, :].rearrange("p (a b) -> p a b", b=S),
                                              hi.bitcast(F32), ALU.subtract).then_inc(mlo_ready, 1)
                    if v == 29:
                        dve.wait_ge(cols_ps, l * 4 + 4)
                        gain(l, 2, 0)
                        gate(l, 2, KC)
                    if v < MIX_UNITS - 1 and not any(n >= 3 * HEADS for n in job_slots(v)):
                        lo_parts(l, FFN_UNITS + v + 3)
                    if v in MIX_ADA_SUM:
                        k = MIX_ADA_SUM[v]
                        dve.wait_ge(mix_ada[k % 2], l * 64 + 16 * (k // 2) + 16)
                        if k == 0:
                            ins = dve.tensor_scalar(out=mix_acc, in0=mix_raw[0], scalar1=c_act[:, 0:1], scalar2=None, op0=ALU.mult)
                        else:
                            dve.wait_ge(mix_sums, l * KC + k)
                            ins = dve.scalar_tensor_tensor(out=mix_acc, in0=mix_raw[k % 2], scalar=c_act[:, k:k + 1], in1=mix_acc,
                                                           op0=ALU.mult, op1=ALU.add)
                        ins.then_inc(mix_sums, 1)
                    if v == 28:
                        rows_out(l * 4 + 4, 16)
                    if v == 34:
                        gate_copy(l, 1)
                boundary(l, 1)
                lo_parts(l, FFN_UNITS + MIX_UNITS + 2)
                ffn(l, 1)
                before = own.n
                with dve.If(l < DEPTH - 1):
                    boundary(l, 2)
                    own.end()
                    lo_parts(l, LAYER_UNITS + 2)
            own.n, own.base = before, DEPTH * OWN
            for t in range(TOK):
                residual(DEPTH - 1, 2, t)

        @block.tensor
        def _(pe):
            def three(out_, lhs, rhs, first, last):
                (lh, ll), (rh, rl) = lhs, rhs
                pe.matmul(out_, lh, rh, start=first, stop=False, skip_group_check=True)
                pe.matmul(out_, lh, rl, start=False, stop=False, skip_group_check=True)
                return pe.matmul(out_, ll, rh, start=False, stop=last, skip_group_check=True)

            def w_part(k, width):
                s = k % RING
                return (w_hi[:, s, :].rearrange("p (c n) -> p c n", n=width),
                        w_lo[:, s, :].rearrange("p (c n) -> p c n", n=width))

            def sum_rows(src, n, halfway=None):
                for i in range(n):
                    if halfway and 2 * i == n:
                        halfway()
                    ins = pe.matmul(ps[0:n, MODB, 0:P], sel[:, 31 - i:31 - i + n], src[:, i * P:i * P + P],
                                    start=i == 0, stop=i == n - 1)
                ins.then_inc(rows_ps, 1)

            def turn_rows(n, r):
                pe.wait_ge(rows_ready, n)
                pe.matmul(ps[:, MODB, 256:256 + r], rows[0:r, :], ident[0:r, 0:r], start=True, stop=True).then_inc(cols_ps, 1)

            def gate_row(s, n):
                pe.wait_ge(mod_ready, n)
                pe.transpose(ps[0:KC, MODB, 384:512], mod_g[:, s, :], ident[:, :]).then_inc(gt_ps, 1)

            def h_columns(l, s):
                for t in range(TOK):
                    pe.wait_ge(xs_ready, (l * NSUB + s) * 2 + t + 1)
                    for half in range(2):
                        for c in range(4):
                            kc = 4 * half + c
                            ins = pe.transpose(ps[:, 2 * t + half, c * P:c * P + P], xs[:, t, kc * P:kc * P + P], ident[:, :])
                        ins.then_inc(h_ps, 1)

            def wait_h(l, s, c, t):
                if c % 4 == 0:
                    pe.wait_ge(hlo_ready, (l * NSUB + s) * 4 + 2 * (c // 4) + t + 1)

            def gate_rows_out(l, s):
                pe.wait_ge(gt_ready, l * NSUB + s + 1)
                for c in range(KC):
                    ins = pe.matmul(ps[:, GU + c // 4, (c % 4) * P:(c % 4) * P + P],
                                    ident[0:KC, c:c + 1].to_broadcast([KC, P]), gt[:, s % 2, :], start=True, stop=True)
                ins.then_inc(g_ps, 1)

            def ffn(l, f):
                k0 = f * (FFN_UNITS + MIX_UNITS)
                n = (l * 2 + f) * FSTEPS

                def wait_unit(k, j):
                    pe.wait_ge(lo_ready, unit_of(l, k) + 3 * j + RING + 1)

                def gate_up(k, part, j, jr, first=False):
                    wait_unit(k, jr)
                    wh, wl = w_part(k, 2 * FB)
                    if part == 0 and not first:
                        pe.wait_ge(act_done, 2 * (n + j))
                    for t in range(TOK):
                        for c in range(4):
                            kc = 4 * part + c
                            ts = slice(t * P, t * P + P)
                            if first:
                                wait_h(l, 2 * f, kc, t)
                            ins = three(ps[:, GU + t, :], (h_hi[:, kc, ts], h_lo[:, kc, ts]), (wh[:, c], wl[:, c]),
                                        kc == 0, kc == KC - 1)
                        if t == 1:
                            ins.then_inc(unit_used, 1)
                        elif part == 1:
                            ins.then_inc(gu_done, 1)

                def turn(j):
                    pe.wait_ge(act_done, 2 * (n + j) + 2)
                    for c in range(2):
                        for t in range(TOK):
                            ins = pe.transpose(ps[:, TB, c * S + t * P:c * S + t * P + P], ffn_a[:, t, c * P:c * P + P], ident[:, :])
                    ins.then_inc(at_ps, 1)

                def down(k, j, jr, first, last):
                    wait_unit(k, jr)
                    pe.wait_ge(alo_ready, n + j + 1)
                    wh, wl = w_part(k, D)
                    for t in range(TOK):
                        for half in range(2):
                            for c in range(2):
                                ts = slice(t * P, t * P + P)
                                hs = slice(half * 512, half * 512 + 512)
                                ins = three(ps[:, 2 * t + half, :], (act_hi[:, 0, c, ts], act_lo[:, 0, c, ts]),
                                            (wh[:, c, hs], wl[:, c, hs]), first and c == 0, last and c == 1)
                        if last and t == 0:
                            ins.then_inc(y_half, 1)
                    ins.then_inc(unit_used, 1)

                h_columns(l, 2 * f)
                gate_up(k0, 0, 0, 0, first=True)
                gate_up(k0 + 1, 1, 0, 0, first=True)
                gate_up(k0 + 2, 0, 1, 0)
                if f == 0:
                    pe.wait_ge(ada_done, 24)
                    sum_rows(ada_acc[:, 2 * D:3 * D], KC)
                turn(0)
                if f == 0:
                    turn_rows(l * 4 + 2, KC)
                gate_up(k0 + 3, 1, 1, 0)
                if f == 0:
                    gate_row(0, l * 3 + 1)
                down(k0 + 4, 0, 0, True, False)
                with pe.Fori(2, FSTEPS) as j:
                    gate_up(k0 - 1, 0, j, j)
                    turn(j - 1)
                    gate_up(k0, 1, j, j)
                    down(k0 + 1, j - 1, j, False, False)
                turn(FSTEPS - 1)
                if f == 0:
                    pe.wait_ge(ada_sums, ada_before(l, 1, 1) + SUMS_AHEAD)
                    sum_rows(ada_acc, 32)
                else:
                    with pe.If(l < DEPTH - 1):
                        pe.wait_ge(ada_sums, ada_before(l + 1, 0, 1) + SUMS_AHEAD)
                        sum_rows(ada_acc, 16)
                gate_rows_out(l, 2 * f)
                if f == 0:
                    turn_rows(l * 4 + 3, 32)
                else:
                    with pe.If(l < DEPTH - 1):
                        turn_rows(l * 4 + 5, 16)
                down(k0 + FFN_UNITS - 1, FSTEPS - 1, 0, False, True)
                if f == 0:
                    gate_row(1, l * 3 + 2)

            def front(l, n):
                kind, h = JOBS[n]
                b = n % 2
                po = DH * (h % 2)
                g = h // HPG
                hs = slice(po, po + DH)
                if n == 0 or n == 8 or n == 24:
                    pe.wait_ge(q_out_act, l * 10 + {0: 2, 8: 4, 24: 10}[n])
                    pe.wait_ge(q_out_dve, l * 4 + {0: 1, 8: 4, 24: 4}[n])
                if n >= 2:
                    pe.wait_ge(s_read, l * NJ + n - 1)
                S_ = ps[:, SB + b, :]
                if kind == "c":
                    q, k = cq[hs, h // 2, :], ck[hs, h // 2, :]
                    pe.matmul(S_[:, 0:S], k[:, 0:P], q, start=True, stop=True)
                    pe.matmul(S_[:, S:S + P], k[:, P:2 * P], q[:, P:2 * P], start=True, stop=True).then_inc(sc_done, 1)
                    return
                q = (aq if kind == "a" else bq)[hs, h // 2, :]
                k = {"a": ak, "slc": bks, "win": bkw}[kind][hs, g, :]
                pe.matmul(S_[:, 0:P], q[:, 0:P], k[:, 0:P], start=True, stop=True)
                pe.matmul(S_[:, P:3 * P], q[:, P:2 * P], k, start=True, stop=True).then_inc(sc_done, 1)

            def middle(l, n):
                kind, h = JOBS[n]
                b = n % 2
                po = DH * (h % 2)
                hs = slice(po, po + DH)
                pe.wait_ge(p_ready, l * NJ + n + 1)
                if n >= 1:
                    if JOBS[n - 1][0] == "c":
                        pe.wait_ge(mask_done, l * HEADS + n - 24)
                    else:
                        pe.wait_ge(pt_ready, l * NJ + n)
                M_ = ps[:, MID, :]
                if kind == "c":
                    L = job_p[:, b, :]
                    pe.matmul(M_[:, 0:S], neg_tri[:, :], L[:, 0:S], start=True, stop=False, skip_group_check=True)
                    pe.matmul(M_[:, P:S], neg_ones[:, :], L[:, S:S + P], start=False, stop=False, skip_group_check=True)
                    pe.matmul(M_[:, S:S + P], neg_tri[:, :], L[:, S:S + P], start=False, stop=True,
                              skip_group_check=True).then_inc(mid_done, 1)
                    return
                for i in range(3):
                    ins = pe.transpose(M_[:, i * P:i * P + P], job_p[:, b, i * P:i * P + P], ident[:, :])
                ins.then_inc(mid_done, 1)

            def values(l, n):
                kind, h = JOBS[n]
                b = n % 2
                po = DH * (h % 2)
                g = h // HPG
                pe.wait_ge(pt_ready, l * NJ + n + 1)
                done = {"a": 0, "slc": 4, "win": 4, "c": 8}[kind] + h // 2
                if h % 2 == 0 and kind != "win" and n:
                    pe.wait_ge(y_lo, l * 12 + done)
                O = ps[po:po + DH, OB, :]
                v = {"a": av, "slc": bvs, "win": bvw, "c": cv}[kind]
                vs = slice(h * DH, h * DH + DH) if kind == "c" else slice(g * DH, g * DH + DH)
                pe.matmul(O[:, 0:S], v[:, 0, vs], job_t[:, b, 0:S], start=kind != "win", stop=False, skip_group_check=True)
                ins = pe.matmul(O[:, P:S], v[:, 1, vs], job_t[:, b, S:S + P], start=False, stop=kind in "ac",
                                skip_group_check=True)
                if kind == "win":
                    if h == 0:
                        pe.wait_ge(cpt_ready, l + 1)
                    r = 32 * (h % 4)
                    for t in range(TOK):
                        ins = pe.matmul(O[:, t * P:t * P + P], vc[r:r + NCMP, g, :], cmp_pt[r:r + NCMP, g, t, :],
                                        start=False, stop=t == 1, skip_group_check=True)
                ins.then_inc(pv_done, 1)

            def jobs(l, step):
                for n in job_slots(step):
                    if 4 <= n:
                        values(l, n - 4)
                for n in job_slots(step):
                    if n % 2 and 3 * HEADS <= n < NJ:
                        front(l, n)
                    if 2 <= n < NJ + 2:
                        middle(l, n - 2)
                    if n < NJ and not (n % 2 and n >= 3 * HEADS):
                        front(l, n)

            pe.sem_inc(unit_used, RING)
            pe.wait_ge(ident_in, 16)
            pe.wait_ge(c_in, 16)
            pe.wait_ge(setup_in[3], 5)
            pe.transpose(ps[:, 0, 0:KC], arena[0:KC, 12288:12288 + P], ident[0:KC, 0:KC]).then_inc(setup_pe, 1)
            pe.wait_ge(setup_dve, 2)
            for i in range(2):
                ins = pe.matmul(ps[0:8, 2 + i, 0:384], rel[0:33, 8 * i:8 * i + 8], buckets[0:33, i, 0:384],
                                start=True, stop=True)
            ins.then_inc(setup_pe, 1)
            pe.wait_ge(setup_in[0], 64)
            for i in range(2):
                pe.transpose(ps[:, 1, 64 * i:64 * i + 48], arena[0:48, 12416 + P * i:12416 + P * i + P], ident[0:48, 0:48]).then_inc(setup_pe, 1)
            for i in range(2):
                pe.transpose(ps[:, 1, 128 + P * i:128 + P * i + 72], arena[0:72, 12672 + P * i:12672 + P * i + P], ident[0:72, 0:72]).then_inc(setup_pe, 1)
            for i in range(2):
                pe.transpose(ps[0:DH, 1, 384 + DH * i:384 + DH * i + DH], arena[0:DH, 12928 + DH * i:12928 + DH * i + DH],
                             ident[0:DH, 0:DH]).then_inc(setup_pe, 1)
            pe.wait_ge(flip_in, 16)
            pe.wait_ge(setup_in[2], 32)
            for i in range(4):
                if i >= 2:
                    pe.wait_ge(setup_act, i - 1)
                for e in range(2):
                    ins = pe.matmul(ps[:, 4 + 2 * (i % 2) + e, :], flip,
                                    bias[:, 4 * i + 2 * e:4 * i + 2 * e + 2, :].rearrange("p a b -> p (a b)"), start=True, stop=True)
                ins.then_inc(setup_pe, 1)
            pe.wait_ge(setup_act, 4)
            pe.wait_ge(setup_dve, 4)
            pe.wait_ge(ada_done, 8)
            sum_rows(ada_acc, 16, lambda: pe.wait_ge(ada_done, 16))
            turn_rows(1, 16)
            with pe.Fori(0, DEPTH) as l:
                ffn(l, 0)
                h_columns(l, 1)
                pe.wait_ge(const_in, 6 * 16)
                for v in range(MIX_UNITS):
                    k = FFN_UNITS + v
                    pe.wait_ge(lo_ready, unit_of(l, k) + RING + 1)
                    if v < QKV_UNITS:
                        if v >= 2:
                            a_ = sum(1 for w in range(v - 1) if w not in (2, 5, 6, 7))
                            d_ = sum(1 for w in range(v - 1) if w in (2, 5, 6, 7))
                            if v - 2 in (2, 5, 6, 7):
                                pe.wait_ge(q_out_dve, l * 4 + d_)
                            else:
                                pe.wait_ge(q_out_act, l * 10 + a_)
                        wh, wl = w_part(k, 256)
                        bank = ps[:, QB + v % 2, :]
                        if v in (7, 12, 13):
                            for t in range(TOK):
                                ts = slice(t * P, t * P + P)
                                for c in range(KC):
                                    ins = three(bank[:, t * S:t * S + S], (h_hi[:, c, ts], h_lo[:, c, ts]),
                                                (wh[:, c, :], wl[:, c, :]), c == 0, c == KC - 1)
                        for b in range(0 if v in (7, 12, 13) else 2):
                            bs = slice(b * P, b * P + P)
                            if b == 1 and v == 2:
                                for t in range(TOK):
                                    ts = slice(t * P, t * P + P)
                                    for c in range(KC):
                                        ins = three(bank[:, b * S + t * P:b * S + t * P + P], (h_hi[:, c, ts], h_lo[:, c, ts]),
                                                    (wh[:, c, bs], wl[:, c, bs]), c == 0, c == KC - 1)
                            else:
                                for c in range(KC):
                                    if v == 0 and b == 0:
                                        wait_h(l, 1, c, 1)
                                    ins = three(bank[:, b * S:b * S + S], (wh[:, c, bs], wl[:, c, bs]),
                                                (h_hi[:, c, :], h_lo[:, c, :]), c == 0, c == KC - 1)
                        ins.then_inc(unit_used, 1)
                    elif v < 32:
                        it, part = (v - 14) // 3, (v - 14) % 3
                        i = it // 2
                        wh, wl = w_part(k, 512)
                        if part == 0:
                            if it:
                                pe.wait_ge(mg_ready, (l * 6 + it) * 2)
                            else:
                                pe.wait_ge(cpt_ready, l + 1)
                        if part == 2:
                            if it:
                                pe.wait_ge(br_read, (l * 6 + it) * 2)
                            else:
                                pe.wait_ge(q_out_act, l * 10 + 10)
                            pe.wait_ge(y_lo, l * 12 + 4 * i + 4)
                        for t in range(TOK):
                            ts = slice(t * P, t * P + P)
                            for c in range(4):
                                if part < 2:
                                    kc = 4 * part + c
                                    ins = three(ps[:, MB + t, :], (h_hi[:, kc, ts], h_lo[:, kc, ts]), (wh[:, c], wl[:, c]),
                                                kc == 0, kc == KC - 1)
                                else:
                                    ins = three(branch_out(it, t), branch_in(i, c, ts),
                                                (wh[:, c], wl[:, c]), c == 0, c == 3)
                            if t == 1:
                                ins.then_inc(unit_used, 1)
                            elif part == 1:
                                ins.then_inc(mg_ps, 1)
                            elif part == 2:
                                ins.then_inc(br_ps, 1)
                    else:
                        wh, wl = w_part(k, D)
                        if v == 32:
                            pe.wait_ge(mg_ready, l * 12 + 12)
                        if v in (32, 34):
                            pe.wait_ge(mlo_ready, l * 4 + v - 30)
                        if v == 35:
                            gate_rows_out(l, 1)
                        mh, ml = (act_hi[:, 1], act_lo[:, 1]) if v < 34 else (h_hi[:, 4:8], h_lo[:, 4:8])
                        for t in range(TOK):
                            ts = slice(t * P, t * P + P)
                            for half in range(2):
                                hs = slice(half * 512, half * 512 + 512)
                                for c in range(2):
                                    kc = 2 * (v - 32) + c
                                    ins = three(ps[:, 2 * t + half, :], (mh[:, kc % 4, ts], ml[:, kc % 4, ts]),
                                                (wh[:, c, hs], wl[:, c, hs]), kc == 0, kc == KC - 1)
                            if v == 35 and t == 0:
                                ins.then_inc(y_half, 1)
                        ins.then_inc(unit_used, 1)
                    if v == 6:
                        pe.wait_ge(w1_in, l * 112 + 112)
                        pe.wait_ge(z_ready, l + 1)
                        for e in range(2):
                            for c in range(16):
                                ins = pe.matmul(ps[0:2 * NCMP, MB, e * P:e * P + P], zc[:, e, c, :], w1[:, e, c, :],
                                                start=c == 0, stop=c == 15)
                        ins.then_inc(hid_ps, 1)
                    if v == 7:
                        pe.wait_ge(bg_lo, l + 1)
                        for c in range(KC):
                            ins = three(ps[0:24, MB + 1, 0:S], (g_hi[:, c, :], g_lo[:, c, :]), (h_hi[:, c, :], h_lo[:, c, :]),
                                        c == 0, c == KC - 1)
                        ins.then_inc(bg_ps, 1)
                        pe.wait_ge(hid_ready, l + 1)
                        for e in range(2):
                            ins = pe.matmul(ps[:, MB, 256 + 32 * e:256 + 32 * e + 2 * NCMP], hid_rows[:, e, :],
                                            ident[0:2 * NCMP, 0:2 * NCMP], start=True, stop=True)
                        ins.then_inc(hid_turned, 1)
                        pe.wait_ge(bg_exp, l + 1)
                        for t in range(TOK):
                            ins = pe.matmul(ps[:, MB + 1, 256 + 24 * t:256 + 24 * t + 24], gate_exp[:, t * P:t * P + P],
                                            ident[0:24, 0:24], start=True, stop=True)
                        ins.then_inc(bg_turned, 1)
                    if v == 8:
                        pe.wait_ge(kc_ready, l * 2 + 1)
                        pe.matmul(ps[:, MB, 128:128 + 2 * NCMP], w2k[:, :, :].rearrange("p a b -> p (a b)"),
                                  hid[:, :, :].rearrange("p a b -> p (a b)"), start=True, stop=True)
                        for g in range(2):
                            ins = pe.matmul(ps[:, MB, 256 + g * DH:256 + g * DH + DH],
                                            hid_v[:, g, :, :].rearrange("p a b -> p (a b)"), w2v[:, :], start=True, stop=True)
                        ins.then_inc(kc_ps, 1)
                    if v == 9:
                        pe.wait_ge(kc_ready, l * 2 + 2)
                        pe.wait_ge(bg_ready, l + 1)
                        pe.wait_ge(q_out_act, l * 10 + 4)
                        for h in range(HEADS):
                            g, po = h // HPG, DH * (h % 2)
                            for t in range(TOK):
                                r = (g * TOK + t) * 2 + h % 4 // 2
                                ins = pe.matmul(ps[:, MB + 1 - h % 2, r * 32:r * 32 + NCMP], bq[po:po + DH, h // 2, t * P:t * P + P],
                                                kc_t[po:po + DH, g, :], start=True, stop=True)
                        ins.then_inc(cs_ps, 1)
                    if v == 10:
                        pe.wait_ge(cp_ready, l + 1)
                        for i in range(4):
                            ins = pe.transpose(ps[:, MB + 1, i * P:i * P + P],
                                               cmp_p[:, 4 * i:4 * i + 4, :].rearrange("p a b -> p (a b)"), ident[:, :])
                        ins.then_inc(cpt_ps, 1)
                    jobs(l, v)
                    if v == 28:
                        pe.wait_ge(mix_sums, l * KC + KC)
                        sum_rows(mix_acc, 16)
                    if v == 29:
                        turn_rows(l * 4 + 4, 16)
                    if v == 30:
                        gate_row(2, l * 3 + 3)
                        pe.wait_ge(gt_ready, l * 3 + 3)
                    if v in (30, 32):
                        pe.wait_ge(br_read, l * 12 + 10 + v - 30)
                        for q in range(2):
                            for c in (2 * q, 2 * q + 1):
                                for t in range(TOK):
                                    ch = c + (4 if v == 32 else 0)
                                    ins = pe.transpose(ps[:, MID + q, (c % 2) * S + t * P:(c % 2) * S + t * P + P],
                                                       merged[:, t, ch * P:ch * P + P], ident[:, :])
                            ins.then_inc(m_ps, 1)
                ffn(l, 1)


def constants():
    import numpy as np

    p = np.arange(P)
    out = {"k_ident": np.eye(P), "k_flip": np.eye(P)[::-1]}
    out["k_negtri"] = -(p[:, None] >= p[None, :]).astype(np.float32)
    before = (p[:, None] < p[None, :]).astype(np.float32)
    one = np.ones((P, P), np.float32)
    out["k_causal01"] = np.concatenate([before, one, before], 1)
    out["k_causalneg"] = np.where(out["k_causal01"] > 0, 0.0, NEG)
    t = p[:, None, None] + P * np.arange(TOK)[None, :, None]
    ok = np.arange(NCMP)[None, None, :] * CMP_STRIDE + CMP_BLOCK - 1 <= t
    out["k_cmp01"] = ok.astype(np.float32)
    out["k_cmpneg"] = np.where(ok, 0.0, NEG)
    dist = 255 - np.arange(384)
    d = np.maximum(dist, 0)
    ratio = np.log(np.maximum(d, 1).astype(np.float32) / np.float32(16)) / np.float32(np.log(128 / 16))
    big = np.minimum(16 + (ratio * np.float32(16)).astype(np.int32), 31)
    bucket = np.where(d < 16, d, big)
    k = np.zeros((33, 2, 512), np.float32)
    for i, ok in enumerate(((dist >= 0) & (dist < 128), dist >= 0)):
        k[bucket[ok], i, np.nonzero(ok)[0]] = 1.0
        k[32, i, 0:384] = np.where(ok, 0.0, NEG)
    out["k_buckets"] = k.reshape(33, 1024)
    return {n: np.ascontiguousarray(a.astype(np.float32)) for n, a in out.items()}


def kernel(x, c, rel_bias, ada_w, ada_b, ln_pre, ln_post, ffn_w_gate, ffn_w_up, ffn_w_down,
           w_in, attn_sinks, cmp_pos, cmp_w1, cmp_w2, w_branch, w_out):
    import numpy as np
    import concourse.bacc as bacc
    from concourse.bass_utils import run_bass_kernel_spmd

    given = dict(x=x, c=c, rel_bias=rel_bias, ada_w=ada_w, ada_b=ada_b, ln_pre=ln_pre, ln_post=ln_post,
                 ffn_w_gate=ffn_w_gate, ffn_w_up=ffn_w_up, ffn_w_down=ffn_w_down, w_in=w_in,
                 attn_sinks=attn_sinks, cmp_pos=cmp_pos, cmp_w1=cmp_w1, cmp_w2=cmp_w2,
                 w_branch=w_branch, w_out=w_out)
    nc = bacc.Bacc("TRN2", target_bir_lowering=False, num_devices=1)
    arrays, A = {}, {}
    for name, a in {**given, **constants()}.items():
        a = np.ascontiguousarray(a)
        arrays["in_" + name] = a
        A[name] = nc.dram_tensor("in_" + name, a.shape, mybir.dt.from_np(a.dtype), kind="ExternalInput").ap()
    A["scratch"] = nc.dram_tensor("bias_scratch", (2, 8, 384), F32, kind="Internal").ap()
    out = nc.dram_tensor("out", (1, S, D), F32, kind="ExternalOutput").ap()
    trunk_program(nc, A, out)
    return run_bass_kernel_spmd(nc, [arrays], core_ids=[0]).results[0]["out"]
```
